# Optimizing a Trainium2 kernel written in Bass

```python
import jax, jax.numpy as jnp
from jax import lax
import numpy as np

D_MODEL = 1024
BATCH = 1
SEQ = 128
DEPTH = 2
DEC_BATCH = 1
DEC_SEQ = 512
PAST_LEN = 256

GRID_W = 64
N_HEADS = 8
KV_HEADS = 2
HEAD_DIM = 64
Q_GROUP = N_HEADS // KV_HEADS
WINDOW = 128
BLOCK = 128
ROPE_THETA = 10000.0
R_HEADS = 8
R_HEAD = 64
RW = R_HEADS * R_HEAD
LORA_W = 64
LORA_A = 64
LORA_G = 128
ATT_Q = N_HEADS * HEAD_DIM
ATT_KV = KV_HEADS * HEAD_DIM
D_IN = ATT_Q + 2 * ATT_KV + 3 * RW
MIX_W = ATT_Q + RW
D_FF = 2816
N_EXPERTS = 8
TOP_K = 2
D_FF_EXPERT = 1408
N_DENSE = (DEPTH + 1) // 2
N_MOE = DEPTH // 2
NORM_EPS = 1e-6
GN_EPS = 64e-5
NEG_INF = -1e30

kernel_name = 'hybrid_dit_rwkv7_swa_prefix_step'

def rmsnorm(x, g):
    xf = x.astype(jnp.float32)
    y = xf * lax.rsqrt(jnp.mean(xf * xf, -1, keepdims=True) + NORM_EPS)
    return (y * g.astype(jnp.float32)).astype(x.dtype)

def modulation(cond, w_mod, b_mod):
    m = jax.nn.silu(cond) @ w_mod + b_mod
    return jnp.split(m, 6, axis=-1)

def centred_shift(u, mu):
    prev = jnp.pad(u[:, :-1], ((0, 0), (1, 0), (0, 0)))
    nxt = jnp.pad(u[:, 1:], ((0, 0), (0, 1), (0, 0)))
    return u + mu * (0.5 * (prev + nxt) - u)

def axial_rope(x, row, col):
    half = HEAD_DIM // 2
    nf = half // 2
    inv = ROPE_THETA ** (-jnp.arange(nf, dtype=jnp.float32) / nf)

    def rot(xa, pos):
        ang = pos.astype(jnp.float32)[:, None] * inv[None, :]
        cos = jnp.cos(ang)[:, None, :]
        sin = jnp.sin(ang)[:, None, :]
        x1 = xa[..., :nf].astype(jnp.float32)
        x2 = xa[..., nf:].astype(jnp.float32)
        return jnp.concatenate([x1 * cos - x2 * sin, x1 * sin + x2 * cos], -1)

    out = jnp.concatenate([rot(x[..., :half], row), rot(x[..., half:], col)], -1)
    return out.astype(x.dtype)

def sink_softmax(logits, sink):
    s = jnp.broadcast_to(sink[None, :, :, None, None], logits.shape[:-1] + (1,))
    p = jax.nn.softmax(jnp.concatenate([s, logits], -1), axis=-1)
    return p[..., 1:]

def attn_context(q, k, v, sink):
    B, S = q.shape[:2]
    nb = S // BLOCK
    qb = jnp.moveaxis(q.reshape(B, nb, BLOCK, KV_HEADS, Q_GROUP, HEAD_DIM), 1, 0)
    scale = HEAD_DIM ** -0.5

    def blk(qblk):
        s = jnp.einsum('bqkgd,bskd->bkgqs', qblk, k, preferred_element_type=jnp.float32) * scale
        p = sink_softmax(s, sink).astype(v.dtype)
        return jnp.einsum('bkgqs,bskd->bqkgd', p, v)

    o = lax.map(blk, qb)
    return jnp.moveaxis(o, 0, 1).reshape(B, S, ATT_Q)

def attn_latent(q, k, v, ck, cv, sink):
    B, T = q.shape[:2]
    nb = T // BLOCK
    span = BLOCK + 2 * WINDOW
    P = ck.shape[1]
    kp = jnp.pad(k, ((0, 0), (WINDOW, WINDOW), (0, 0), (0, 0)))
    vp = jnp.pad(v, ((0, 0), (WINDOW, WINDOW), (0, 0), (0, 0)))
    scale = HEAD_DIM ** -0.5

    def blk(i):
        start = i * BLOCK
        qblk = lax.dynamic_slice_in_dim(q, start, BLOCK, 1).reshape(B, BLOCK, KV_HEADS, Q_GROUP, HEAD_DIM)
        kw = lax.dynamic_slice_in_dim(kp, start, span, 1)
        vw = lax.dynamic_slice_in_dim(vp, start, span, 1)
        qpos = start + jnp.arange(BLOCK)
        kpos = start - WINDOW + jnp.arange(span)
        ok = (kpos >= 0)[None, :] & (kpos < T)[None, :] & (jnp.abs(qpos[:, None] - kpos[None, :]) <= WINDOW)
        s_c = jnp.einsum('bqkgd,bskd->bkgqs', qblk, ck, preferred_element_type=jnp.float32) * scale
        s_w = jnp.einsum('bqkgd,bskd->bkgqs', qblk, kw, preferred_element_type=jnp.float32) * scale
        s_w = jnp.where(ok, s_w, NEG_INF)
        p = sink_softmax(jnp.concatenate([s_c, s_w], -1), sink).astype(v.dtype)
        return (jnp.einsum('bkgqs,bskd->bqkgd', p[..., :P], cv)
                + jnp.einsum('bkgqs,bskd->bqkgd', p[..., P:], vw))

    o = lax.map(blk, jnp.arange(nb))
    return jnp.moveaxis(o, 0, 1).reshape(B, T, ATT_Q)

def wkv_scan(r, w, k, v, kk, a, s0, reverse):
    xs = tuple(jnp.moveaxis(t, 1, 0) for t in (r, w, k, v, kk, a))

    def step(S, inp):
        r_t, w_t, k_t, v_t, kk_t, a_t = inp
        sa = jnp.einsum('bhvk,bhk->bhv', S, -kk_t)
        S = (S * w_t[:, :, None, :] + sa[..., None] * (kk_t * a_t)[:, :, None, :]
             + v_t[..., None] * k_t[:, :, None, :])
        return S, jnp.einsum('bhvk,bhk->bhv', S, r_t)

    sT, ys = lax.scan(step, s0, xs, reverse=reverse)
    return jnp.moveaxis(ys, 0, 1), sT

def rwkv_mix(h, r, k, v, lp, s0):
    f32 = jnp.float32
    B, T = h.shape[:2]
    hf = h.astype(f32)

    def heads(t):
        return t.astype(f32).reshape(B, T, R_HEADS, R_HEAD)

    r_h, k_h, v_h = heads(r), heads(k), heads(v)
    kk = k_h * lp['k_k'].astype(f32).reshape(R_HEADS, R_HEAD)
    kk = kk * lax.rsqrt(jnp.sum(kk * kk, -1, keepdims=True) + 1e-12)
    k_a = lp['k_a'].astype(f32).reshape(R_HEADS, R_HEAD)
    r_k = lp['r_k'].astype(f32)
    ys, bonuses, states = [], [], []
    for d in range(2):
        w_pre = lp['w0'][d] + jnp.tanh(hf @ lp['w1'][d]) @ lp['w2'][d]
        decay = jnp.exp(-jnp.exp(-jax.nn.softplus(-w_pre) - 0.5))
        a = jax.nn.sigmoid(lp['a0'][d] + (hf @ lp['a1'][d]) @ lp['a2'][d])
        decay_h, a_h = heads(decay), heads(a)
        k_d = k_h * (1.0 + (a_h - 1.0) * k_a)
        y_d, s_d = wkv_scan(r_h, decay_h, k_d, v_h, kk, a_h, s0[:, d].astype(f32), reverse=(d == 1))
        ys.append(y_d)
        bonuses.append(jnp.sum(r_h * k_d * r_k, -1, keepdims=True) * v_h)
        states.append(s_d)
    y = ys[0] + ys[1]
    mu = jnp.mean(y, -1, keepdims=True)
    var = jnp.mean(jnp.square(y - mu), -1, keepdims=True)
    y = ((y - mu) * lax.rsqrt(var + GN_EPS)).reshape(B, T, RW)
    y = y * lp['ln_g'] + lp['ln_b'] + (bonuses[0] + bonuses[1]).reshape(B, T, RW)
    g = jax.nn.sigmoid(hf @ lp['g1']) @ lp['g2']
    return (y * g).astype(h.dtype), jnp.stack(states, 1)

def project(h, lp):
    B, T = h.shape[:2]
    u = h @ lp['w_in']
    q, k_att, v_att, rkv = jnp.split(u, [ATT_Q, ATT_Q + ATT_KV, ATT_Q + 2 * ATT_KV], axis=-1)
    rkv = centred_shift(rkv, lp['mu'])
    r, k_rw, v_rw = jnp.split(rkv, 3, axis=-1)
    return (q.reshape(B, T, N_HEADS, HEAD_DIM), k_att.reshape(B, T, KV_HEADS, HEAD_DIM),
            v_att.reshape(B, T, KV_HEADS, HEAD_DIM), r, k_rw, v_rw)

def mix_context(h, lp):
    B = h.shape[0]
    q, k_att, v_att, r, k_rw, v_rw = project(h, lp)
    sink = lp['sink'].astype(jnp.float32).reshape(KV_HEADS, Q_GROUP)
    o_att = attn_context(q, k_att, v_att, sink)
    s0 = jnp.zeros((B, 2, R_HEADS, R_HEAD, R_HEAD), jnp.float32)
    o_rw, s_ctx = rwkv_mix(h, r, k_rw, v_rw, lp, s0)
    out = jnp.concatenate([o_att, o_rw], -1) @ lp['w_o']
    return out, k_att, v_att, s_ctx

def mix_latent(h, lp, ck, cv, s_ctx, row, col):
    q, k_att, v_att, r, k_rw, v_rw = project(h, lp)
    q = axial_rope(q, row, col)
    k_att = axial_rope(k_att, row, col)
    sink = lp['sink'].astype(jnp.float32).reshape(KV_HEADS, Q_GROUP)
    o_att = attn_latent(q, k_att, v_att, ck, cv, sink)
    o_rw, _ = rwkv_mix(h, r, k_rw, v_rw, lp, s_ctx)
    return jnp.concatenate([o_att, o_rw], -1) @ lp['w_o']

def swiglu(h, w1, w3, w2):
    return (jax.nn.silu(h @ w1) * (h @ w3)) @ w2

def moe_swiglu(h, router, w1, w3, w2):
    probs = jax.nn.softmax((h @ router).astype(jnp.float32), axis=-1)
    top_p, top_i = lax.top_k(probs, TOP_K)
    top_p = top_p / jnp.sum(top_p, -1, keepdims=True)
    gates = jnp.sum(jax.nn.one_hot(top_i, N_EXPERTS, dtype=jnp.float32) * top_p[..., None], axis=-2)
    y = jnp.zeros(h.shape, jnp.float32)
    for e in range(N_EXPERTS):
        y = y + gates[..., e:e + 1] * swiglu(h, w1[e], w3[e], w2[e]).astype(jnp.float32)
    return y.astype(h.dtype)

def channel_mix(h, l, ffn_w1, ffn_w3, ffn_w2, moe_router, moe_w1, moe_w3, moe_w2):
    if l % 2 == 0:
        i = l // 2
        return swiglu(h, ffn_w1[i], ffn_w3[i], ffn_w2[i])
    i = l // 2
    return moe_swiglu(h, moe_router[i], moe_w1[i], moe_w3[i], moe_w2[i])

def setup_inputs(seed: int = 0) -> dict:
    key = jax.random.key(seed)
    ks = iter(jax.random.split(key, 48))

    def nrm(shape, scale):
        return jax.random.normal(next(ks), shape, jnp.float32) * scale

    D = D_MODEL
    return {
        'x_prompt': nrm((BATCH, SEQ, D), 1.0),
        'x_sample': nrm((DEC_BATCH, DEC_SEQ, D), 1.0),
        'cache_k': nrm((DEC_BATCH, DEPTH, PAST_LEN, KV_HEADS, HEAD_DIM), 1.0),
        'cache_v': nrm((DEC_BATCH, DEPTH, PAST_LEN, KV_HEADS, HEAD_DIM), 1.0),
        'state_rwkv': nrm((DEC_BATCH, DEPTH, 2, R_HEADS, R_HEAD, R_HEAD), 0.5),
        'c': nrm((DEC_BATCH, D), 1.0),
        'c_ctx': nrm((D,), 1.0),
        'w_mod': nrm((DEPTH, D, 6 * D), 0.5 * D ** -0.5),
        'b_mod': nrm((DEPTH, 6 * D), 0.02),
        'g_pre_mix': 1.0 + nrm((DEPTH, D), 0.1),
        'g_post_mix': 1.0 + nrm((DEPTH, D), 0.1),
        'g_pre_ffn': 1.0 + nrm((DEPTH, D), 0.1),
        'g_post_ffn': 1.0 + nrm((DEPTH, D), 0.1),
        'w_in': nrm((DEPTH, D, D_IN), D ** -0.5),
        'mu_shift': 0.5 + nrm((DEPTH, 3 * RW), 0.1),
        'w_o': nrm((DEPTH, MIX_W, D), MIX_W ** -0.5),
        'attn_sink': nrm((DEPTH, N_HEADS), 0.5),
        'rw_w0': -0.5 + nrm((DEPTH, 2, RW), 0.5),
        'rw_w1': nrm((DEPTH, 2, D, LORA_W), D ** -0.5),
        'rw_w2': nrm((DEPTH, 2, LORA_W, RW), 0.1 * LORA_W ** -0.5),
        'rw_a0': nrm((DEPTH, 2, RW), 0.5),
        'rw_a1': nrm((DEPTH, 2, D, LORA_A), D ** -0.5),
        'rw_a2': nrm((DEPTH, 2, LORA_A, RW), 0.5 * LORA_A ** -0.5),
        'rw_g1': nrm((DEPTH, D, LORA_G), D ** -0.5),
        'rw_g2': nrm((DEPTH, LORA_G, RW), LORA_G ** -0.5),
        'rw_k_k': 0.85 + nrm((DEPTH, RW), 0.05),
        'rw_k_a': 1.0 + nrm((DEPTH, RW), 0.05),
        'rw_r_k': nrm((DEPTH, R_HEADS, R_HEAD), 0.1),
        'rw_ln_g': 1.0 + nrm((DEPTH, RW), 0.1),
        'rw_ln_b': nrm((DEPTH, RW), 0.02),
        'ffn_w1': nrm((N_DENSE, D, D_FF), D ** -0.5),
        'ffn_w3': nrm((N_DENSE, D, D_FF), D ** -0.5),
        'ffn_w2': nrm((N_DENSE, D_FF, D), D_FF ** -0.5),
        'moe_router': nrm((N_MOE, D, N_EXPERTS), D ** -0.5),
        'moe_w1': nrm((N_MOE, N_EXPERTS, D, D_FF_EXPERT), D ** -0.5),
        'moe_w3': nrm((N_MOE, N_EXPERTS, D, D_FF_EXPERT), D ** -0.5),
        'moe_w2': nrm((N_MOE, N_EXPERTS, D_FF_EXPERT, D), D_FF_EXPERT ** -0.5),
    }

def reference(x_prompt, x_sample, cache_k, cache_v, state_rwkv, c, c_ctx,
              w_mod, b_mod, g_pre_mix, g_post_mix, g_pre_ffn, g_post_ffn,
              w_in, mu_shift, w_o, attn_sink,
              rw_w0, rw_w1, rw_w2, rw_a0, rw_a1, rw_a2, rw_g1, rw_g2,
              rw_k_k, rw_k_a, rw_r_k, rw_ln_g, rw_ln_b,
              ffn_w1, ffn_w3, ffn_w2, moe_router, moe_w1, moe_w3, moe_w2):
    T = x_sample.shape[1]
    n_rows = T // GRID_W
    row = jnp.repeat(jnp.arange(n_rows), GRID_W)
    col = jnp.tile(jnp.arange(GRID_W), n_rows)
    cond_ctx = c_ctx[None, None, :]
    cond_lat = c[:, None, :]
    xp, xs = x_prompt, x_sample
    new_k, new_v, new_s = [], [], []
    for l in range(DEPTH):
        lp = {'w_in': w_in[l], 'mu': mu_shift[l], 'w_o': w_o[l], 'sink': attn_sink[l],
              'w0': rw_w0[l], 'w1': rw_w1[l], 'w2': rw_w2[l],
              'a0': rw_a0[l], 'a1': rw_a1[l], 'a2': rw_a2[l],
              'g1': rw_g1[l], 'g2': rw_g2[l], 'k_k': rw_k_k[l], 'k_a': rw_k_a[l],
              'r_k': rw_r_k[l], 'ln_g': rw_ln_g[l], 'ln_b': rw_ln_b[l]}
        sh1, sc1, gt1, sh2, sc2, gt2 = modulation(cond_ctx, w_mod[l], b_mod[l])
        h = rmsnorm(xp, g_pre_mix[l]) * (1.0 + sc1) + sh1
        o, k_ctx, v_ctx, s_ctx = mix_context(h, lp)
        xp = xp + gt1 * rmsnorm(o, g_post_mix[l])
        h = rmsnorm(xp, g_pre_ffn[l]) * (1.0 + sc2) + sh2
        f = channel_mix(h, l, ffn_w1, ffn_w3, ffn_w2, moe_router, moe_w1, moe_w3, moe_w2)
        xp = xp + gt2 * rmsnorm(f, g_post_ffn[l])
        new_k.append(k_ctx)
        new_v.append(v_ctx)
        new_s.append(s_ctx.astype(state_rwkv.dtype))
        sh1, sc1, gt1, sh2, sc2, gt2 = modulation(cond_lat, w_mod[l], b_mod[l])
        h = rmsnorm(xs, g_pre_mix[l]) * (1.0 + sc1) + sh1
        o = mix_latent(h, lp, cache_k[:, l], cache_v[:, l], state_rwkv[:, l], row, col)
        xs = xs + gt1 * rmsnorm(o, g_post_mix[l])
        h = rmsnorm(xs, g_pre_ffn[l]) * (1.0 + sc2) + sh2
        f = channel_mix(h, l, ffn_w1, ffn_w3, ffn_w2, moe_router, moe_w1, moe_w3, moe_w2)
        xs = xs + gt2 * rmsnorm(f, g_post_ffn[l])
    new_cache_k = jnp.stack(new_k, axis=1)
    new_cache_v = jnp.stack(new_v, axis=1)
    new_state_rwkv = jnp.stack(new_s, axis=1)
    return (xp, xs, new_cache_k, new_cache_v, new_state_rwkv)


_drawn_inputs = setup_inputs


def setup_inputs(seed=0):
    import zlib

    import numpy as np

    out = dict(_drawn_inputs(seed))
    spreads = {}
    factors = {'attn_sink': 28.2, 'rw_w1': 2.679, 'rw_w2': 3.21, 'rw_ln_b': 3.372}
    for name, (base, spread) in spreads.items():
        noise = np.random.default_rng([zlib.crc32(name.encode()), seed]).standard_normal(out[name].shape)
        drawn = base * np.exp(spread * noise) if base else spread * noise
        out[name] = __import__('jax').numpy.asarray(drawn.astype(out[name].dtype))
    for name, factor in factors.items():
        out[name] = (out[name] * factor).astype(out[name].dtype)
    return out
```

```python
from contextlib import ExitStack

import numpy as np

import concourse.bass as bass
from concourse import mybir

ALU = mybir.AluOpType
ACT = mybir.ActivationFunctionType
AX = mybir.AxisListType
F32 = mybir.dt.float32
I32 = mybir.dt.int32
BF16 = mybir.dt.bfloat16

P = 128
D = 1024
KC = D // P
CTX = 128
LAT = 512
T = CTX + LAT
NT = T // P
DEPTH = 2
PAST = 256
NH, KVH, HD = 8, 2, 64
RH = 8
NPAIR = RH // 2
GRID_W = 64
WINDOW = 128
THETA = 10000.0
DFF = 2816
NE = 8
DFE = 1408
FT = DFF // P
FE = DFE // P
CAP = 256
NORM_EPS = 1e-6
GN_EPS = 64e-5
ARENA = 30208
HALF_DECAY = 0.5 * float(np.exp(-0.5))

RING = 9
MOD_B = 48
PROJ_B = 21
WO_B = 8
DENSE_B = 3 * FT
EXP_B = 3 * FE
LAYER_B = [MOD_B + PROJ_B + WO_B + DENSE_B, MOD_B + PROJ_B + WO_B + NE * EXP_B]
N_BLOCKS = sum(LAYER_B)
MOE_FIRST = N_BLOCKS - NE * EXP_B

PAR = {}
_n = 0
for _name, _w in [("b_mod", 48), ("g_pre_mix", 8), ("g_post_mix", 8), ("g_pre_ffn", 8), ("g_post_ffn", 8),
                  ("mu", 12), ("w0", 8), ("a0", 8), ("k_k", 4), ("k_a", 4), ("r_k", 4), ("ln_g", 4), ("ln_b", 4)]:
    PAR[_name] = (_n, _w)
    _n += _w
NPAR = _n

CON = {}
_n = 0
for _name, _w in [("ident", 128), ("rot", 128), ("mask_f", 256), ("mask_b", 256), ("cos", 512), ("sin", 512),
                  ("m_prev", 128), ("m_next", 128), ("head_ones", 128), ("head_mean", 128), ("ones", 128),
                  ("before", 128), ("iota", 256), ("head_sel", 2), ("head_exp", 128), ("power", 40)]:
    CON[_name] = (_n, _w)
    _n += _w
NCON = _n


def constants():
    c = np.zeros((P, NCON), np.float32)

    def put(name, a):
        at, w = CON[name]
        c[:a.shape[0], at:at + a.shape[1]] = a

    i = np.arange(P)
    put("ident", np.eye(P, dtype=np.float32))
    rot = np.zeros((P, P), np.float32)
    for ch in range(P):
        if ch % 32 < 16:
            rot[ch + 16, ch] = -1.0
        else:
            rot[ch - 16, ch] = 1.0
    put("rot", rot)
    s, t = i[:, None], i[None, :]
    put("mask_f", np.concatenate([s < t, s <= t], 1).astype(np.float32))
    put("mask_b", np.concatenate([s > t, s >= t], 1).astype(np.float32))
    nf = HD // 4
    inv = (np.float32(THETA) ** (-np.arange(nf, dtype=np.float32) / np.float32(nf))).astype(np.float32)
    tok = np.arange(LAT)
    ch = i % HD
    pos = np.where((ch < 32)[:, None], (tok // GRID_W)[None, :], (tok % GRID_W)[None, :]).astype(np.float32)
    ang = pos * inv[ch % nf][:, None]
    put("cos", np.cos(ang).astype(np.float32))
    put("sin", np.sin(ang).astype(np.float32))
    q, k = i[:, None], i[None, :]
    put("m_prev", np.where(k >= q, 0.0, -1e30).astype(np.float32))
    put("m_next", np.where(k <= q, 0.0, -1e30).astype(np.float32))
    same = (s // HD == t // HD).astype(np.float32)
    put("head_ones", same)
    put("head_mean", same / HD)
    put("ones", np.ones((P, P), np.float32))
    put("before", (s < t).astype(np.float32))
    put("iota", np.broadcast_to(np.arange(CAP, dtype=np.float32), (P, CAP)))
    put("head_sel", (s // HD == np.arange(2)[None, :]).astype(np.float32))
    put("head_exp", (np.arange(2)[:, None] == t // HD).astype(np.float32))
    put("power", np.full((P, NT * RH), -0.5, np.float32))
    return c


SEMS = """consts_in cond_in x_in misc_in block_used silu_c mod_done rowvec_diag rowvec_mm norm_sq norm_ms norm_pow
norm_x norm_tr norm_ev_act norm_ev_dve proj_ev_act proj_ev_dve rope_mm rope_ev kc_tr kc_ev att_s att_max
att_exp att_p att_tr att_trev att_o att_oev kk_prod kk_sum kk_ss kk_pow kk_mm spread_ev kk_done vt_tr vt_ev
low_mm low_w low_ev dec_cum dec_cumx dec_exp dec_ph rw_ops ar_done hat_tr hat_ev gram_mm gram_ev lt_tr lt_ev
n_ev x0_ev lt_sub mv_mm mv_ev sq_mm sq_ev inv_mm inv_ev xb_ev nw_p nw_e nw_t nw_c nw_x st_tr st_ev st_scaled
x_mm x_ev u_mm u_ev s_mm s_ev so_tr so_ev y_mm y_ev gn_mean_mm gn_cent gn_sq gn_sum gn_ms gn_pow bon_prod
bon_mm bon_ev gn_mm gn_used wo_mm wo_ev post_sq post_ms post_pow post_tmp post_x ff_th ff_g ff_yev rt_mm
rt_max rt_exp rt_gate rt_cum rt_rank htok_tr htok_ev sel_dve selt_tr selt_ev gat_mm gat_ev eh_th eh_g ey_ev
comb_mm comb_ev o_sel_dve o_selt_tr o_selt_ev o_gat_mm o_gat_ev o_eh_th o_eh_g o_ey_ev o_comb_mm o_comb_ev
o_block_used act_step dve_step pe_phase act_phase dve_phase pool_phase results_out""".split()


class Signals:

    def __init__(self, name, sem):
        self.name, self.sem, self.count, self.last = name, sem, {}, None

    def sig(self, what):
        self.count[what] = self.count.get(what, 0) + 1
        self.last = (self.sem[what], self.count[what])
        return self.sem[what], 1

    def own_last(self):
        return self.last


def build(nc, blocks, x_all, small, cond, sinkrows, router, low2, cache_k, cache_v, state, consts, flag,
          y_all, new_k, new_v, new_state, debug=None):
    ctx = ExitStack()
    with ctx:
        def sb(name, shape, dt=F32):
            return ctx.enter_context(nc.sbuf_tensor(name, shape, dt))

        con = sb("con", [P, NCON])
        par = sb("par", [P, DEPTH * NPAR])
        condT = sb("condT", [P, KC, 2])
        sink = sb("sink", [P, DEPTH * NH])
        rout = sb("rout", [P, KC, NE])
        w2 = sb("w2", [P, 3, 512])
        ring = sb("ring", [P, RING, D])
        x = sb("x", [P, NT, D])
        mod = sb("mod", [P, 48, 2])
        gpre = sb("gpre", [P, 2, 8, 2])
        gpost = sb("gpost", [P, 2, 8, 2])
        hpar = sb("hpar", [P, 64])
        st_in = sb("st_in", [64, 2, RH, HD])
        st_out = sb("st_out", [P, 2, NPAIR, HD])
        identb = sb("identb", [P, P], BF16)
        rw_s = sb("rw_s", [P, 4, NT, RH])
        ck = sb("ck", [P, 2, P])
        cv = sb("cv", [P, 2, P])
        tiny = sb("tiny", [P, 128])
        arena = sb("arena", [P, ARENA])
        ps = ctx.enter_context(nc.psum_tensor("ps", [P, 8, 512], F32))
        sem = {n: ctx.enter_context(nc.semaphore(n)) for n in SEMS}
        ring_sem = [ctx.enter_context(nc.semaphore(f"block_in{i}")) for i in range(RING)]
        o_ring_sem = [ctx.enter_context(nc.semaphore(f"o_block_in{i}")) for i in range(RING)]

        def C(name, rows=P):
            at, w = CON[name]
            return con[0:rows, at:at + w]

        def PR(l, name, j=None, n=1):
            at, w = PAR[name]
            at += l * NPAR
            return par[:, at:at + w] if j is None else par[:, at + j:at + j + n]

        ident = C("ident")

        cursor = [0]

        def take(n, **dims):
            a = arena[:, cursor[0]:cursor[0] + n]
            cursor[0] += n
            assert cursor[0] <= ARENA, cursor[0]
            if not dims:
                return a
            names = list(dims)
            return a.rearrange(f"p ({' '.join(names)}) -> p {' '.join(names)}", **{k: dims[k] for k in names[:-1]})

        rkv = take(12 * T, c=12, t=T)
        zlow = take(3 * T, c=3, t=T)
        oT = take(8 * T, c=8, t=T)
        MIX_END = cursor[0]
        hT = take(KC * T, c=KC, t=T)
        ATT_AT = cursor[0]
        qT = take(4 * T, c=4, t=T)
        kT = take(T)
        vtok = take(NT * P, i=NT, c=P)
        kctok = take(P)
        kcT = take(PAST)
        SCR_AT = cursor[0]
        xn = take(NT * D, i=NT, d=D)
        cursor[0] = SCR_AT
        praw = take(2 * 643, b=2, t=643)
        pshift = take(2 * T, b=2, t=T)
        cursor[0] = SCR_AT
        prob = take(2 * 640, b=2, k=640)
        probT = take(2 * 640, b=2, k=640)
        ropetmp = take(2 * 512, b=2, k=512)
        cursor[0] = MIX_END
        kk = take(T)
        kds = take(T)
        vt_rw = take(NT * P, i=NT, c=P)
        ar = take(NT * 2 * P, i=NT, a=2, t=P)
        bkbar = take(2 * T, a=2, t=T)
        bktok = take(NT * 2 * P, i=NT, a=2, c=P)
        mv = take(NT * P, i=NT, v=P)
        xb = take(2 * P, b=2, v=P)
        st = take(2 * P, b=2, v=P)
        stpc = take(P)
        LG_AT = cursor[0]
        gm = take(10 * 4 * P, u=10, a=4, t=P)
        lfi = take(10 * P, u=10, t=P)
        nb = take(10 * P, u=10, t=P).bitcast(BF16).rearrange("p u (a t) -> p u a t", a=2)
        xq = take(5 * P).bitcast(BF16).rearrange("p (u t) -> p u t", u=10)
        gmb = gm.bitcast(BF16)
        over = bkbar.rearrange("p a t -> p (a t)")
        ub = over[:, 0:T].rearrange("p (i v) -> p i v", i=NT)
        s0s = over[:, T:2 * T].rearrange("p (i v) -> p i v", i=NT)
        cursor[0] = LG_AT
        tw = take(T)
        ta = take(T)
        lw = take(T)
        cumc = take(T)
        cumx = take(T)
        e_in = take(T)
        e_inv = take(T)
        e_ex = take(T)
        avec = take(T)
        kdt = take(T)
        spr = take(2 * T, b=2, t=T)
        cursor[0] = LG_AT
        sq4 = take(4 * T, c=4, t=T)
        bon = take(2 * T, c=2, t=T)
        assert cursor[0] <= LG_AT + 10 * T
        cursor[0] = 0
        gT = take(FT * T, f=FT, t=T)
        cursor[0] = ATT_AT
        fo = take(NT * D, i=NT, d=D)
        ftmp = take(2 * T, b=2, t=T)
        cursor[0] = 0
        htok = take(NT * D, i=NT, d=D)
        hgT = take(KC * CAP, c=KC, s=CAP)
        geT = take(FE * CAP, f=FE, s=CAP)
        ye = take(2 * D, s=2, d=D)
        sel = take(NT * CAP, i=NT, s=CAP)
        assert cursor[0] <= MIX_END, cursor[0]
        cursor[0] = ATT_AT + NT * D + 2 * T
        selg = take(NT * CAP, i=NT, s=CAP)
        selT = take(2 * T, s=2, t=T)
        lg = tiny[:, 0:40].rearrange("p (i e) -> p i e", i=NT)
        rk = tiny[:, 40:80].rearrange("p (i e) -> p i e", i=NT)
        gate = tiny[:, 80:120].rearrange("p (i e) -> p i e", i=NT)
        small2 = sb("small2", [P, 256])
        flag_i = sb("flag_i", [1, 8], I32)
        m8 = small2[:, 0:40].rearrange("p (i e) -> p i e", i=NT)
        msk = small2[:, 40:80].rearrange("p (i e) -> p i e", i=NT)
        nstat = small2[:, 80:100]
        phs = small2[:, 100:110].rearrange("p (a i) -> p a i", a=2)
        attst = small2[:, 110:150].rearrange("p (b a) -> p b a", b=4)
        rstat = small2[:, 150:200]

        def pair(n):
            return ps[:, 2 * n:2 * n + 2, :].rearrange("p b c -> p (b c)")

        def pair640(n):
            return pair(n)[:, 384:1024]

        def mm640(nc, n, lhsT, rhs, start, stop, rows=P):
            nc.tensor.matmul(pair(n)[0:rows, 384:512], lhsT, rhs[:, 0:CTX], start=start, stop=stop)
            return nc.tensor.matmul(pair(n)[0:rows, 512:1024], lhsT, rhs[:, CTX:T], start=start, stop=stop)

        def MOE_SP(sp):
            sp.wait_ge(sem["rt_rank"], 2)

            def body():
                n = 0
                for base in (CAP, 2 * CAP):
                    for m in range(NE * EXP_B):
                        if n >= RING:
                            sp.wait_ge(sem["o_block_used"], n - RING + 1)
                        elif n < RING:
                            sp.wait_ge(sem["block_used"], N_BLOCKS)
                        sp.dma_start(ring[:, n % RING, :], blocks[MOE_FIRST + m]).then_inc(o_ring_sem[n % RING], 16)
                        n += 1
            with_flag(sp, body)

        def with_flag(eng, body):
            r = eng.value_load(flag_i[0:1, 0:1], min_val=0, max_val=T)
            with eng.If(r > CAP):
                body()

        def unit(u):
            return (u // 2) % 4, u % 2, u // 8 - 1

        N_UNITS = NH * NT

        def order(d):
            return [0] + (list(range(1, NT)) if d == 0 else list(range(NT - 1, 0, -1)))

        def diag(n):
            return diags[:, n % 4, :]

        diags = arena[:, ARENA - 512:ARENA].rearrange("p (n t) -> p n t", n=4)

        def up_done(f):
            return 2 * (f + 1) + max(0, f - 1)

        def BL(l):
            return sum(LAYER_B[:l])

        def n_keys(blkq):
            return P if blkq < 0 else PAST + P * (3 if 0 < blkq < 3 else 2)

        def sq_scratch(i):
            return arena[:, MIX_END + i * D:MIX_END + (i + 1) * D]

        block = ctx.enter_context(nc.Block())

        @block.sync
        def _(sp):
            sp.dma_start(con[:, :], consts).then_inc(sem["consts_in"], 16)
            sp.dma_start(par[:, :], small).then_inc(sem["cond_in"], 16)
            sp.dma_start(condT[:, :, :], cond).then_inc(sem["cond_in"], 16)
            sp.dma_start(sink[:, :], sinkrows).then_inc(sem["cond_in"], 16)
            sp.dma_start(rout[:, :, :], router).then_inc(sem["cond_in"], 16)
            for n in range(N_BLOCKS):
                if n >= RING:
                    sp.wait_ge(sem["block_used"], n - RING + 1)
                sp.dma_start(ring[:, n % RING, :], blocks[n]).then_inc(ring_sem[n % RING], 16)
                if n == 3:
                    sp.dma_start(x[:, :, :], x_all.rearrange("(i p) d -> p i d", p=P)).then_inc(sem["x_in"], 16)
            MOE_SP(sp)

        @block.tensor
        def _(pe):
            E = Signals("pe", sem)
            phase = [0]

            def next_phase():
                phase[0] += 1
                pe.drain().then_inc(sem["pe_phase"], 1)
                pe.wait_ge(sem["pe_phase"], phase[0])
                pe.wait_ge(sem["act_phase"], phase[0])
                pe.wait_ge(sem["dve_phase"], phase[0])
                pe.wait_ge(sem["pool_phase"], phase[0])

            used = [0]

            def blk():
                n = used[0]
                pe.wait_ge(ring_sem[n % RING], 16 * (n // RING + 1))
                return ring[:, n % RING, :]

            def mod_phase(l):
                if l == 0:
                    pe.wait_ge(sem["consts_in"], 16)
                    pe.wait_ge(sem["silu_c"], 1)
                for j in range(MOD_B):
                    b = blk()
                    for kc in range(KC):
                        mm = nc.tensor.matmul(ps[:, 0, 2 * j:2 * j + 2], b[:, kc * P:(kc + 1) * P], condT[:, kc, :],
                                              start=kc == 0, stop=kc == KC - 1)
                    mm.then_inc(sem["block_used"], 1)
                    used[0] += 1

            def norm_phase(k):
                for kc in range(KC):
                    if kc == 0:
                        pe.wait_ge(sem["norm_x"], NT * (k + 1))
                    if kc >= 4:
                        pe.wait_ge(sem["norm_ev_act"], KC * k + kc - 3)
                        pe.wait_ge(sem["norm_ev_dve"], KC * k + kc - 3)
                    for i in range(NT):
                        mm = nc.tensor.transpose(pair640(kc % 4)[:, i * P:(i + 1) * P], xn[:, i, kc * P:(kc + 1) * P], ident)
                    mm.then_inc(sem["norm_tr"], 1)

            def proj_phase(l):
                for o in range(PROJ_B):
                    b = blk()
                    n = l * PROJ_B + o
                    if o >= 4:
                        pe.wait_ge(sem["proj_ev_act"], n - 3)
                    if 6 <= o - 4 < 18:
                        pe.wait_ge(sem["proj_ev_dve"], 13 * l + o - 9)
                    if o == 4:
                        for kc in range(KC):
                            nc.tensor.matmul(pair(o % 4)[:, 0:P], hT[:, kc, 0:P], b[:, kc * P:(kc + 1) * P],
                                             start=kc == 0, stop=kc == KC - 1)
                    if o == 5:
                        for i in range(NT):
                            for kc in range(KC):
                                mm = nc.tensor.matmul(pair640(o % 4)[:, i * P:(i + 1) * P], hT[:, kc, i * P:(i + 1) * P],
                                                      b[:, kc * P:(kc + 1) * P], start=kc == 0, stop=kc == KC - 1)
                    else:
                        for kc in range(KC):
                            mm = mm640(nc, o % 4, b[:, kc * P:(kc + 1) * P], hT[:, kc, :], kc == 0, kc == KC - 1)
                    mm.then_inc(sem["block_used"], 1)
                    used[0] += 1

            def att_phase(l):
                for c in range(5):
                    src = qT[:, c, CTX:T] if c < 4 else kT[:, CTX:T]
                    mm = nc.tensor.matmul(ps[:, c, :], C("rot"), src, start=True, stop=True)
                    mm.then_inc(sem["rope_mm"], 1)
                pe.wait_ge(sem["misc_in"], 16 * 5 * (l + 1))
                for i in range(2):
                    mm = nc.tensor.transpose(ps[:, 5, i * P:(i + 1) * P], ck[:, i, :], ident)
                mm.then_inc(sem["kc_tr"], 1)
                pe.wait_ge(sem["rope_ev"], 5 * (l + 1))
                pe.wait_ge(sem["kc_ev"], l + 1)

                def keys(u):
                    c, g, blkq = unit(u)
                    rows = slice(64 * g, 64 * g + 64)
                    own = [(kT[rows, 0:P], vtok[:, 0, rows], None)]
                    if blkq < 0:
                        return own
                    out = [(kcT[rows, i * P:(i + 1) * P], cv[:, i, rows], None) for i in range(2)]
                    for d, m in ((0, None), (-1, "m_prev"), (1, "m_next")):
                        b = blkq + d
                        if 0 <= b < 4:
                            out.append((kT[rows, CTX + b * P:CTX + (b + 1) * P], vtok[:, 1 + b, rows], m))
                    return out

                for t in range(N_UNITS + 2):
                    if t < N_UNITS:
                        c, g, blkq = unit(t)
                        rows = slice(64 * g, 64 * g + 64)
                        un = l * N_UNITS + t
                        if t >= 2:
                            pe.wait_ge(sem["att_exp"], un - 1)
                        q = qT[rows, c, (blkq + 1) * P:(blkq + 2) * P]
                        for j, (kop, _, m) in enumerate(keys(t)):
                            dst = pair(t % 2)[:, j * P:(j + 1) * P]
                            mm = nc.tensor.matmul(dst, q, kop, start=True, stop=m is None)
                            if m:
                                mm = nc.tensor.matmul(dst, ident, C(m), start=False, stop=True)
                        mm.then_inc(sem["att_s"], 1)
                    if 1 <= t <= N_UNITS:
                        u = t - 1
                        un = l * N_UNITS + u
                        pe.wait_ge(sem["att_p"], un + 1)
                        if u >= 1:
                            pe.wait_ge(sem["att_trev"], un)
                        for j in range(len(keys(u))):
                            mm = nc.tensor.transpose(pair(2)[:, j * P:(j + 1) * P], prob[:, u % 2, j * P:(j + 1) * P], ident)
                        mm.then_inc(sem["att_tr"], 1)
                    if t >= 2:
                        u = t - 2
                        c, g, blkq = unit(u)
                        rows = slice(64 * g, 64 * g + 64)
                        un = l * N_UNITS + u
                        pe.wait_ge(sem["att_trev"], un + 1)
                        if g == 0 and u >= 4:
                            pe.wait_ge(sem["att_oev"], (l * N_UNITS + u) // 2 - 1)
                        ks = keys(u)
                        for j, (_, vop, _) in enumerate(ks):
                            mm = nc.tensor.matmul(ps[rows, 6 + (u // 2) % 2, 0:P], vop, probT[:, u % 2, j * P:(j + 1) * P],
                                                  start=j == 0, stop=j == len(ks) - 1)
                        mm.then_inc(sem["att_o"], 1)

            def kk_phase(l):
                for c in range(NPAIR):
                    pe.wait_ge(sem["kk_prod"], l * NPAIR + c + 1)
                    for i in range(NT):
                        mm = nc.tensor.matmul(ps[:, 0, i * RH + 2 * c:i * RH + 2 * c + 2], sq4[:, c, i * P:(i + 1) * P], C("head_sel"),
                                              start=True, stop=True)
                mm.then_inc(sem["kk_sum"], 1)

            def spread(dst, b):
                for i in range(NT):
                    mm = nc.tensor.transpose(dst[:, i * P:(i + 1) * P], spr[:, b, i * P:(i + 1) * P], ident)
                return mm

            def rwkv_dir(l, c, d):
                g = (l * NPAIR + c) * 2 + d
                k = l * NPAIR + c
                rows = slice(64 * d, 64 * d + 64)
                mm640(nc, 0, w2[rows, 0, c * P:(c + 1) * P], zlow[rows, 0, :], True, True)
                mm640(nc, 1, w2[rows, 1, c * P:(c + 1) * P], zlow[rows, 1, :], True, True).then_inc(sem["low_mm"], 1)
                if d == 0:
                    pe.wait_ge(sem["spread_ev"], 12 * l + c + 1)
                    spread(pair640(2), 0).then_inc(sem["kk_mm"], 1)
                    for i in range(NT):
                        mm = nc.tensor.transpose(pair640(3)[:, i * P:(i + 1) * P], rkv[:, 8 + c, i * P:(i + 1) * P], ident)
                    mm.then_inc(sem["vt_tr"], 1)
                    pe.wait_ge(sem["kk_done"], k + 1)
                    pe.wait_ge(sem["vt_ev"], k + 1)
                pe.wait_ge(sem["rw_ops"], g + 1)
                for a in range(2):
                    for i in range(NT):
                        mm = nc.tensor.transpose(pair640(2 + a)[:, i * P:(i + 1) * P], bkbar[:, a, i * P:(i + 1) * P], ident)
                    mm.then_inc(sem["hat_tr"], 1)
                nc.tensor.transpose(ps[:, 0, 0:64], st_in[:, d, 2 * c:2 * c + 2, :].rearrange("v h k -> v (h k)"),
                                    ident[0:64, 0:64]).then_inc(sem["st_tr"], 1)
                pe.wait_ge(sem["hat_ev"], 2 * (g + 1))
                pe.wait_ge(sem["st_ev"], g + 1)
                pe.wait_ge(sem["ar_done"], g + 1)
                for u in range(10):
                    i, hh = u // 2, u % 2
                    h = slice(64 * hh, 64 * hh + 64)
                    if u >= 8:
                        pe.wait_ge(sem["gram_ev"], 10 * g + u - 7)
                    arr = ar[h, i, :, :].rearrange("p a t -> p (a t)")
                    nc.tensor.matmul(ps[:, u % 8, 0:256], bkbar[h, 0, i * P:(i + 1) * P], arr, start=True, stop=True)
                    nc.tensor.matmul(ps[:, u % 8, 256:512], bkbar[h, 1, i * P:(i + 1) * P], arr, start=True, stop=True).then_inc(sem["gram_mm"], 1)
                for i in range(NT):
                    pe.wait_ge(sem["gram_ev"], 10 * g + 10)
                    if i >= 4:
                        pe.wait_ge(sem["lt_ev"], 5 * g + i - 3)
                        pe.wait_ge(sem["mv_ev"], 5 * g + i - 3)
                    for hh in range(2):
                        mm = nc.tensor.transpose(ps[:, i % 4, hh * P:(hh + 1) * P], gm[:, 2 * i + hh, 0, :], ident)
                    mm.then_inc(sem["lt_tr"], 1)
                    for hh in range(2):
                        mm = nc.tensor.matmul(ps[:, 4 + i % 4, P * hh:P * hh + P], gm[:, 2 * i + hh, 2, :], vt_rw[:, i, :],
                                              start=True, stop=True)
                    mm.then_inc(sem["mv_mm"], 1)
                for j in range(1, 8):
                    for i in range(NT):
                        n = 5 * (j - 1) + i
                        if j == 1:
                            pe.wait_ge(sem["lt_ev"], 5 * g + i + 1)
                            pe.wait_ge(sem["n_ev"], 5 * g + i + 1)
                            if i == 0:
                                pe.wait_ge(sem["lt_ev"], 5 * g + 5)
                                pe.wait_ge(sem["mv_ev"], 5 * g + 5)
                        else:
                            pe.wait_ge(sem["sq_ev"], 30 * g + n - 4)
                        if j <= 6:
                            if n >= 4:
                                pe.wait_ge(sem["sq_ev"], 30 * g + n - 3)
                            for hh in range(2):
                                u = 2 * i + hh
                                nc.tensor.matmul(ps[:, n % 4, 256 * hh:256 * hh + P], nb[:, u, 1, :], nb[:, u, 0, :], start=True, stop=True)
                                mm = nc.tensor.matmul(ps[:, n % 4, 256 * hh + P:256 * hh + 256], nb[:, u, 0, :], nb[:, u, 1, :], start=True, stop=True)
                            mm.then_inc(sem["sq_mm"], 1)
                        if j >= 2:
                            m = n - 5
                            if j == 2:
                                pe.wait_ge(sem["x0_ev"], 5 * g + i + 1)
                            else:
                                pe.wait_ge(sem["inv_ev"], 30 * g + m - 4)
                            if m >= 4:
                                pe.wait_ge(sem["inv_ev"], 30 * g + m - 3)
                            for hh in range(2):
                                u = 2 * i + hh
                                mm = nc.tensor.matmul(ps[:, 4 + m % 4, hh * P:(hh + 1) * P], nb[:, u, 1, :], xq[:, u, :], start=True, stop=True)
                            mm.then_inc(sem["inv_mm"], 1)
                pe.wait_ge(sem["inv_ev"], 30 * g + 30)
                for q in range(2):
                    for i in range(NT):
                        n = (2 * g + q) * NT + i
                        if q == 0:
                            pe.wait_ge(sem["xb_ev"], 5 * g + i + 1)
                        else:
                            pe.wait_ge(sem["nw_x"], n - 4)
                        if i >= 4:
                            pe.wait_ge(sem["nw_e"], n - 3)
                            if q == 0:
                                pe.wait_ge(sem["nw_t"], 5 * g + i - 3)
                        for hh in range(2):
                            u = 2 * i + hh
                            mm = nc.tensor.matmul(ps[:, i % 4, hh * P:(hh + 1) * P], lfi[:, u, :], gm[:, u, 0, :], start=True, stop=True)
                        if q == 0:
                            for hh in range(2):
                                u = 2 * i + hh
                                mm = nc.tensor.matmul(ps[:, 4 + i % 4, hh * P:(hh + 1) * P], xq[:, u, :], identb[:, :], start=True, stop=True)
                        mm.then_inc(sem["nw_p"], 1)
                    pe.wait_ge(sem["nw_t"], 5 * g + 5)
                    for i in range(NT):
                        n = (2 * g + q) * NT + i
                        pe.wait_ge(sem["nw_e"], n + 1)
                        if i >= 4:
                            pe.wait_ge(sem["nw_x"], n - 3)
                        for hh in range(2):
                            u = 2 * i + hh
                            mm = nc.tensor.matmul(ps[:, 4 + i % 4, hh * P:(hh + 1) * P], gmb[:, u, 2, P:2 * P], gmb[:, u, 2, 0:P],
                                                  start=True, stop=True)
                        mm.then_inc(sem["nw_c"], 1)
                pe.wait_ge(sem["nw_x"], 10 * (g + 1))
                for n, i in enumerate(order(d)):
                    k5 = 5 * g + n
                    pe.wait_ge(sem["st_scaled"], k5 + 1)
                    nc.tensor.matmul(ps[:, 0, 0:P], ar[:, i, 0, :], s0s[:, i, :], start=True, stop=True).then_inc(sem["x_mm"], 1)
                    pe.wait_ge(sem["x_ev"], k5 + 1)
                    for hh in range(2):
                        mm = nc.tensor.matmul(ps[:, 1, P * hh:P * hh + P], gm[:, 2 * i + hh, 0, :], xb[:, n % 2, :], start=True, stop=True)
                    mm.then_inc(sem["u_mm"], 1)
                    pe.wait_ge(sem["u_ev"], k5 + 1)
                    if n == NT - 1:
                        break
                    nc.tensor.matmul(ps[:, 2, 0:P], bktok[:, i, 0, :], ub[:, i, :], start=True, stop=False)
                    nc.tensor.matmul(ps[:, 2, 0:P], bktok[:, i, 1, :], vt_rw[:, i, :], start=False, stop=True).then_inc(sem["s_mm"], 1)
                    pe.wait_ge(sem["s_ev"], 4 * g + n + 1)
                    if n == 0:
                        nc.tensor.transpose(ps[:, 3, 0:P], st[:, 0, :], ident).then_inc(sem["so_tr"], 1)
                for i in range(NT):
                    dst = pair640(2)[:, i * P:(i + 1) * P]
                    nc.tensor.matmul(dst, s0s[:, i, :], ar[:, i, 1, :], start=True, stop=False, skip_group_check=True)
                    for hh in range(2):
                        h = slice(64 * hh, 64 * hh + 64)
                        u = 2 * i + hh
                        nc.tensor.matmul(dst[h, :], ub[:, i, h], gm[:, u, 1, :], start=False, stop=False, skip_group_check=True)
                        mm = nc.tensor.matmul(dst[h, :], vt_rw[:, i, h], gm[:, u, 3, :], start=False, stop=True, skip_group_check=True)
                mm.then_inc(sem["y_mm"], 1)
                if d == 1:
                    for i in range(NT):
                        mm = nc.tensor.matmul(ps[:, 0, 2 * i:2 * i + 2], kds[:, i * P:(i + 1) * P], C("head_sel"), start=True, stop=True)
                    mm.then_inc(sem["bon_mm"], 1)
                next_phase()

            def gn_phase(l):
                for c in range(NPAIR):
                    mm640(nc, c, C("head_mean"), oT[:, 4 + c, :], True, True).then_inc(sem["gn_mean_mm"], 1)
                pe.wait_ge(sem["gn_cent"], NPAIR * (l + 1))
                for c in range(NPAIR):
                    pe.wait_ge(sem["gn_sq"], l * NPAIR + c + 1)
                    for i in range(NT):
                        mm = nc.tensor.matmul(ps[:, 0, i * RH + 2 * c:i * RH + 2 * c + 2], sq4[:, c, i * P:(i + 1) * P], C("head_sel"),
                                              start=True, stop=True)
                mm.then_inc(sem["gn_sum"], 1)
                for c in range(NPAIR):
                    for w in range(3):
                        n = 3 * c + w
                        if n == 0:
                            pe.wait_ge(sem["gn_pow"], l + 1)
                        if n >= 4:
                            pe.wait_ge(sem["gn_used"], 12 * l + n - 3)
                        dst = pair640((n + 1) % 4)
                        if w == 0:
                            pe.wait_ge(sem["spread_ev"], 12 * l + 4 + 2 * c + 1)
                            mm = spread(dst, 0)
                        elif w == 2:
                            mm = mm640(nc, (n + 1) % 4, w2[:, 2, c * P:(c + 1) * P], zlow[:, 2, :], True, True)
                        else:
                            pe.wait_ge(sem["spread_ev"], 12 * l + 4 + 2 * c + 2)
                            mm = spread(dst, 1)
                        mm.then_inc(sem["gn_mm"], 1)
                next_phase()

            def wo_phase(l):
                first = used[0]
                for i in range(NT):
                    if i >= 4:
                        pe.wait_ge(sem["wo_ev"], l * NT + i - 3)
                    for fc in range(WO_B):
                        n = first + fc
                        if i == 0:
                            pe.wait_ge(ring_sem[n % RING], 16 * (n // RING + 1))
                        for h in range(2):
                            mm = nc.tensor.matmul(pair(i % 4)[:, h * 512:(h + 1) * 512], oT[:, fc, i * P:(i + 1) * P],
                                                  ring[:, n % RING, h * 512:(h + 1) * 512], start=fc == 0, stop=fc == WO_B - 1)
                        if i == NT - 1:
                            mm.then_inc(sem["block_used"], 1)
                            used[0] += 1
                    if i < NT - 1:
                        mm.then_inc(sem["wo_mm"], 1)

            def rowvec(k):
                for n in range(16):
                    g, kc = n // 8, n % 8
                    pe.wait_ge(sem["rowvec_diag"], 16 * k + n + 1)
                    nc.tensor.matmul(pair(g)[:, kc * P:(kc + 1) * P], C("ones"), diag(n),
                                           start=True, stop=True).then_inc(sem["rowvec_mm"], 1)

            def dense_phase(l):
                for f in range(FT):
                    for w in range(2):
                        b = blk()
                        n = 2 * f + w
                        if n >= 4:
                            pe.wait_ge(sem["ff_g"], f - 1)
                        for kc in range(KC):
                            mm = mm640(nc, n % 4, b[:, kc * P:(kc + 1) * P], hT[:, kc, :], kc == 0, kc == KC - 1)
                        mm.then_inc(sem["block_used"], 1)
                        used[0] += 1
                for h in range(2):
                    for j in range(FT // 2):
                        b = blk()
                        for s in range(2):
                            f = 2 * j + s
                            if h == 0 and j == 0 and s == 0:
                                pe.wait_ge(sem["ff_g"], FT)
                            for i in range(NT):
                                if h == 1 and f == 0:
                                    pe.wait_ge(sem["ff_yev"], max(1, i - 2))
                                mm = nc.tensor.matmul(ps[:, (5 * h + i) % 8, :], gT[:, f, i * P:(i + 1) * P],
                                                      b[:, s * 512:(s + 1) * 512], start=f == 0, stop=f == FT - 1)
                        mm.then_inc(sem["block_used"], 1)
                        used[0] += 1

            def route_phase():
                for i in range(NT):
                    for kc in range(KC):
                        mm = nc.tensor.matmul(ps[:, 0, i * NE:(i + 1) * NE], hT[:, kc, i * P:(i + 1) * P], rout[:, kc, :],
                                              start=kc == 0, stop=kc == KC - 1)
                mm.then_inc(sem["rt_mm"], 1)
                pe.wait_ge(sem["rt_gate"], 1)
                for i in range(NT + 1):
                    dst = ps[:, 1, i * NE:(i + 1) * NE]
                    for j in range(min(i, NT - 1) + 1):
                        last = j == min(i, NT - 1)
                        w = C("before") if last and i < NT else C("ones")
                        mm = nc.tensor.matmul(dst, w, msk[:, j, :], start=j == 0, stop=last)
                mm.then_inc(sem["rt_cum"], 1)
                for i in range(NT):
                    if i >= 3:
                        pe.wait_ge(sem["htok_ev"], i - 2)
                    for kc in range(KC):
                        mm = nc.tensor.transpose(pair(1 + i % 3)[:, kc * P:(kc + 1) * P], hT[:, kc, i * P:(i + 1) * P], ident)
                    mm.then_inc(sem["htok_tr"], 1)

            def moe_pass(pre, e, n_pass, get, rel):
                k = n_pass
                pe.wait_ge(sem[pre + "sel_dve"], k + 1)
                if k >= 1:
                    pe.wait_ge(sem[pre + "comb_ev"], 10 * k)
                for s in range(2):
                    if s == 1:
                        pe.wait_ge(sem[pre + "selt_ev"], 2 * k + 1)
                    for i in range(NT):
                        mm = nc.tensor.transpose(pair640(3)[:, i * P:(i + 1) * P], selg[:, i, s * P:(s + 1) * P], ident)
                    mm.then_inc(sem[pre + "selt_tr"], 1)
                for kc in range(KC):
                    b = 4 + kc % 2
                    if kc >= 2:
                        pe.wait_ge(sem[pre + "gat_ev"], KC * k + kc - 1)
                    for i in range(NT):
                        mm = nc.tensor.matmul(ps[:, b, 0:CAP], htok[:, i, kc * P:(kc + 1) * P], sel[:, i, :], start=i == 0, stop=i == NT - 1)
                    mm.then_inc(sem[pre + "gat_mm"], 1)
                pe.wait_ge(sem[pre + "gat_ev"], KC * (k + 1))
                held = {}
                for f in range(FE + 1):
                    if f < FE:
                        if f >= 2:
                            pe.wait_ge(sem[pre + "eh_g"], FE * k + f - 1)
                        for w in range(2):
                            b = get()
                            for kc in range(KC):
                                mm = nc.tensor.matmul(ps[:, 4 + f % 2, w * CAP:(w + 1) * CAP], b[:, kc * P:(kc + 1) * P], hgT[:, kc, :],
                                                      start=kc == 0, stop=kc == KC - 1)
                            rel(mm)
                    if f >= 1:
                        g = f - 1
                        pe.wait_ge(sem[pre + "eh_g"], FE * k + g + 1)
                        b = get()
                        for s in range(2):
                            for h in range(2):
                                mm = nc.tensor.matmul(ps[:, 2 * s + h, :], geT[:, g, s * P:(s + 1) * P], b[:, h * 512:(h + 1) * 512],
                                                      start=g == 0, stop=g == FE - 1)
                        rel(mm)
                for i in range(NT):
                    pe.wait_ge(sem[pre + "ey_ev"], 4 * (k + 1))
                    for h in range(2):
                        n = 2 * i + h
                        if n >= 2:
                            pe.wait_ge(sem[pre + "comb_ev"], 10 * k + n - 1)
                        elif n == 0:
                            pe.wait_ge(sem[pre + "selt_ev"], 2 * k + 2)
                        for s in range(2):
                            mm = nc.tensor.matmul(ps[:, 6 + n % 2, :], selT[:, s, i * P:(i + 1) * P], ye[:, s, h * 512:(h + 1) * 512],
                                                  start=s == 0, stop=s == 1)
                        mm.then_inc(sem[pre + "comb_mm"], 1)

            def rel_main(mm):
                mm.then_inc(sem["block_used"], 1)
                used[0] += 1

            for l in range(DEPTH):
                mod_phase(l)
                next_phase()
                norm_phase(2 * l)
                next_phase()
                proj_phase(l)
                next_phase()
                att_phase(l)
                next_phase()
                kk_phase(l)
                next_phase()
                for c in range(NPAIR):
                    rwkv_dir(l, c, 0)
                    rwkv_dir(l, c, 1)
                gn_phase(l)
                wo_phase(l)
                next_phase()
                rowvec(2 * l)
                next_phase()
                norm_phase(2 * l + 1)
                next_phase()
                if l == 0:
                    dense_phase(l)
                else:
                    route_phase()
                    next_phase()
                    for e in range(NE):
                        moe_pass("", e, e, blk, rel_main)
                    next_phase()
                    o_used = [0]

                    def o_blk():
                        n = o_used[0]
                        pe.wait_ge(o_ring_sem[n % RING], 16 * (n // RING + 1))
                        return ring[:, n % RING, :]

                    def o_rel(mm):
                        mm.then_inc(sem["o_block_used"], 1)
                        o_used[0] += 1

                    def body():
                        for n in range(2 * NE):
                            moe_pass("o_", n % NE, n, o_blk, o_rel)
                    with_flag(pe, body)
                next_phase()
                rowvec(2 * l + 1)
                next_phase()

        @block.scalar
        def _(act):
            E = Signals("act", sem)
            phase = [0]

            def next_phase():
                phase[0] += 1
                act.drain().then_inc(sem["act_phase"], 1)
                act.wait_ge(sem["pe_phase"], phase[0])
                act.wait_ge(sem["act_phase"], phase[0])
                act.wait_ge(sem["dve_phase"], phase[0])
                act.wait_ge(sem["pool_phase"], phase[0])

            A = nc.scalar.activation

            def norm_phase(k):
                if k == 0:
                    act.wait_ge(sem["x_in"], 16)
                for i in range(NT):
                    A(xn[:, i, :], x[:, i, :], ACT.Square, accum_out=nstat[:, i:i + 1]).then_inc(*E.sig("norm_sq"))
                for kc in range(KC):
                    act.wait_ge(sem["norm_tr"], KC * k + kc + 1)
                    w, sh = k % 2, (0 if k % 2 == 0 else 24)
                    A(hT[:, kc, CTX:T], pair(kc % 4)[:, 512:1024], ACT.Identity, bias=mod[:, sh + kc, 1:2],
                            scale=gpre[:, w, kc, 1:2]).then_inc(*E.sig("norm_ev_act"))

            def proj_phase(l):
                for o in range(PROJ_B):
                    act.wait_ge(sem["block_used"], BL(l) + MOD_B + o + 1)
                    src = pair640(o % 4)
                    if o < 4:
                        A(qT[:, o, :], src, ACT.Copy, scale=HD ** -0.5).then_inc(*E.sig("proj_ev_act"))
                    elif o == 4:
                        A(kT[:, :], src, ACT.Copy).then_inc(*E.sig("act_step"))
                        A(kctok[:, :], pair(o % 4)[:, 0:P], ACT.Copy).then_inc(*E.sig("proj_ev_act"))
                    elif o == 5:
                        A(vtok[:, :, :].rearrange("p i c -> p (i c)"), src, ACT.Copy).then_inc(*E.sig("proj_ev_act"))
                    elif o < 18:
                        j = o - 6
                        pr = praw[:, j % 2, :]
                        if j < 2:
                            for z in (0, 129, 642):
                                A(pr[:, z:z + 1], C("ones")[:, 0:1], ACT.Copy, scale=0.0).then_inc(*E.sig("act_step"))
                        else:
                            act.wait_ge(sem["proj_ev_dve"], 13 * l + j - 1)
                        A(pr[:, 1:129], src[:, 0:CTX], ACT.Copy, scale=hpar[:, j:j + 1]).then_inc(*E.sig("act_step"))
                        A(pr[:, 130:642], src[:, CTX:T], ACT.Copy, scale=hpar[:, j:j + 1]).then_inc(*E.sig("proj_ev_act"))
                    elif o == 18:
                        A(zlow[:, 0, :], src, ACT.Tanh).then_inc(*E.sig("proj_ev_act"))
                    elif o == 19:
                        A(zlow[:, 1, :], src, ACT.Copy).then_inc(*E.sig("proj_ev_act"))
                    else:
                        A(zlow[:, 2, :], src, ACT.Tanh, scale=0.5).then_inc(*E.sig("proj_ev_act"))

            def att_phase(l):
                for t in range(N_UNITS + 1):
                    if t < N_UNITS:
                        c, g, blkq = unit(t)
                        un = l * N_UNITS + t
                        nk = n_keys(blkq)
                        act.wait_ge(sem["att_max"], un + 1)
                        if t >= 2:
                            act.wait_ge(sem["att_tr"], un - 1)
                        a = attst[:, t % 2, :]
                        h = l * NH + c + 4 * g
                        A(a[:, 3:4], sink[:, h:h + 1], ACT.Exp, bias=a[:, 1:2]).then_inc(*E.sig("act_step"))
                        A(prob[:, t % 2, 0:nk], pair(t % 2)[:, 0:nk], ACT.Exp, bias=a[:, 1:2], accum_out=a[:, 2:3]).then_inc(*E.sig("att_exp"))
                    if t >= 1:
                        u = t - 1
                        un = l * N_UNITS + u
                        act.wait_ge(sem["att_tr"], un + 1)
                        if u >= 2:
                            act.wait_ge(sem["att_o"], un - 1)
                        nk = n_keys(unit(u)[2])
                        A(probT[:, u % 2, 0:nk], pair(2)[:, 0:nk], ACT.Copy).then_inc(*E.sig("att_trev"))

            def spread(w, c, b):
                return A(spr[:, b, :].rearrange("p (i h k) -> p i h k", i=NT, h=2),
                         rw_s[:, w, :, 2 * c:2 * c + 2].unsqueeze(3).broadcast_to([P, NT, 2, HD]), ACT.Copy)

            def kk_phase(l):
                for c in range(NPAIR):
                    A(sq4[:, c, :], rkv[:, 4 + c, :], ACT.Square, scale=PR(l, "k_k", c)).then_inc(*E.sig("kk_prod"))

            def rwkv_dir(l, c, d):
                g = (l * NPAIR + c) * 2 + d
                k = l * NPAIR + c
                if d == 0:
                    spread(0, c, 0).then_inc(*E.sig("spread_ev"))
                act.wait_ge(sem["low_mm"], g + 1)
                A(tw[:, :], pair640(0), ACT.Tanh, bias=hpar[:, 16 + 4 * d + c:17 + 4 * d + c], scale=0.5).then_inc(*E.sig("low_w"))
                A(ta[:, :], pair640(1), ACT.Tanh, bias=hpar[:, 24 + 4 * d + c:25 + 4 * d + c], scale=0.5).then_inc(*E.sig("low_ev"))
                if d == 0:
                    act.wait_ge(sem["vt_tr"], k + 1)
                    A(vt_rw[:, :, :].rearrange("p i c -> p (i c)"), pair640(3), ACT.Copy).then_inc(*E.sig("vt_ev"))
                act.wait_ge(sem["dec_cum"], g + 1)
                if d == 0:
                    A(e_in[:, :], cumc[:, :], ACT.Exp).then_inc(*E.sig("dec_exp"))
                    A(e_inv[:, :], cumc[:, :], ACT.Exp, scale=-1.0).then_inc(*E.sig("dec_exp"))
                    act.wait_ge(sem["dec_cumx"], g + 1)
                    A(e_ex[:, :], cumx[:, :], ACT.Exp).then_inc(*E.sig("dec_exp"))
                else:
                    A(e_ex[:, :], cumc[:, :], ACT.Exp, scale=-1.0).then_inc(*E.sig("dec_exp"))
                    act.wait_ge(sem["dec_cumx"], g + 1)
                    A(e_in[:, :], cumx[:, :], ACT.Exp, scale=-1.0).then_inc(*E.sig("dec_exp"))
                    A(e_inv[:, :], cumx[:, :], ACT.Exp).then_inc(*E.sig("dec_exp"))
                A(phs[:, 0, :], nstat[:, 10:15], ACT.Exp, scale=-1.0).then_inc(*E.sig("act_step"))
                A(phs[:, 1, :], nstat[:, 10:15], ACT.Exp, scale=-2.0).then_inc(*E.sig("dec_ph"))
                for a in range(2):
                    act.wait_ge(sem["hat_tr"], 2 * g + a + 1)
                    A(bktok[:, :, a, :], pair640(2 + a).rearrange("p (i c) -> p i c", i=NT), ACT.Copy).then_inc(*E.sig("hat_ev"))
                for i in range(NT):
                    act.wait_ge(sem["gram_ev"], 10 * g + 2 * i + 2)
                    A(nb[:, 2 * i:2 * i + 2, 0, :], gm[:, 2 * i:2 * i + 2, 0, :], ACT.Copy).then_inc(*E.sig("n_ev"))
                for i in range(NT):
                    act.wait_ge(sem["mv_mm"], 5 * g + i + 1)
                    A(mv[:, i, :].rearrange("p (h v) -> p h v", h=2),
                      ps[:, 4 + i % 4, 0:384].rearrange("p (h v) -> p h v", h=2)[:, :, 0:64], ACT.Copy).then_inc(*E.sig("mv_ev"))
                    act.wait_ge(sem["lt_sub"], 5 * g + i + 1)
                    A(nb[:, 2 * i:2 * i + 2, 1, :], ps[:, i % 4, 0:256].rearrange("p (h t) -> p h t", h=2), ACT.Copy).then_inc(*E.sig("lt_ev"))
                for n in range(30):
                    i = n % 5
                    act.wait_ge(sem["sq_mm"], 30 * g + n + 1)
                    if n >= 5:
                        act.wait_ge(sem["inv_mm"], 30 * g + n - 4)
                    A(nb[:, 2 * i:2 * i + 2, :, :].rearrange("p u a t -> p (u a t)"), ps[:, n % 4, :], ACT.Copy).then_inc(*E.sig("sq_ev"))
                for i in range(NT):
                    act.wait_ge(sem["inv_ev"], 30 * g + 25 + i + 1)
                    A(xq[:, 2 * i:2 * i + 2, :], gm[:, 2 * i:2 * i + 2, 0, :], ACT.Copy).then_inc(*E.sig("xb_ev"))
                for i in range(NT):
                    act.wait_ge(sem["nw_p"], 10 * g + i + 1)
                    A(gmb[:, 2 * i:2 * i + 2, 2, P:2 * P], ps[:, 4 + i % 4, 0:256].rearrange("p (h t) -> p h t", h=2), ACT.Copy).then_inc(*E.sig("nw_t"))
                for n in range(NT):
                    act.wait_ge(sem["u_mm"], 5 * g + n + 1)
                    A(ub[:, order(d)[n], :].rearrange("p (h v) -> p h v", h=2),
                      ps[:, 1, 0:384].rearrange("p (h v) -> p h v", h=2)[:, :, 0:64], ACT.Copy).then_inc(*E.sig("u_ev"))
                act.wait_ge(sem["so_tr"], g + 1)
                for hh in range(2):
                    h = slice(64 * hh, 64 * hh + 64)
                    A(st_out[h, d, c, :], ps[h, 3, h], ACT.Copy).then_inc(*E.sig("so_ev"))
                if d == 1:
                    act.wait_ge(sem["bon_mm"], k + 1)
                    A(rw_s[:, 1, :, 2 * c:2 * c + 2], ps[:, 0, 0:10].rearrange("p (i h) -> p i h", i=NT), ACT.Copy).then_inc(*E.sig("bon_ev"))
                next_phase()

            def gn_phase(l):
                for c in range(NPAIR):
                    act.wait_ge(sem["gn_cent"], l * NPAIR + c + 1)
                    A(sq4[:, c, :], oT[:, 4 + c, :], ACT.Square).then_inc(*E.sig("gn_sq"))
                act.wait_ge(sem["gn_pow"], l + 1)
                for c in range(NPAIR):
                    for b in range(2):
                        if c >= 1:
                            act.wait_ge(sem["gn_mm"], 12 * l + 3 * (c - 1) + b + 1)
                        spread(2 - b, c, b).then_inc(*E.sig("spread_ev"))
                next_phase()

            def wo_phase(l):
                for i in range(NT):
                    if i < NT - 1:
                        act.wait_ge(sem["wo_mm"], l * (NT - 1) + i + 1)
                    else:
                        act.wait_ge(sem["block_used"], BL(l) + MOD_B + PROJ_B + WO_B)
                    A(fo[:, i, :], pair(i % 4), ACT.Copy).then_inc(*E.sig("wo_ev"))

            def post_phase(k):
                for i in range(NT):
                    A(sq_scratch(i), fo[:, i, :], ACT.Square, accum_out=nstat[:, i:i + 1]).then_inc(*E.sig("post_sq"))

            def dense_phase(l):
                for f in range(FT):
                    act.wait_ge(sem["block_used"], BL(l) + MOD_B + PROJ_B + WO_B + 2 * f + 2)
                    if f >= 2:
                        act.wait_ge(sem["ff_g"], f - 1)
                    A(ftmp[:, f % 2, :], pair640(2 * f % 4), ACT.Tanh, scale=0.5).then_inc(*E.sig("ff_th"))
                for h in range(2):
                    act.wait_ge(sem["block_used"], BL(l) + MOD_B + PROJ_B + WO_B + 2 * FT + (h + 1) * FT // 2)
                    for i in range(NT):
                        A(fo[:, i, h * 512:(h + 1) * 512], ps[:, (5 * h + i) % 8, :], ACT.Copy).then_inc(*E.sig("ff_yev"))

            def route_phase():
                act.wait_ge(sem["rt_max"], 1)
                for i in range(NT):
                    ins = A(gate[:, i, :], lg[:, i, :], ACT.Exp, bias=rstat[:, i:i + 1])
                    if i < NT - 1:
                        ins.then_inc(*E.sig("act_step"))
                    else:
                        ins.then_inc(*E.sig("rt_exp"))
                for i in range(NT):
                    act.wait_ge(sem["htok_tr"], i + 1)
                    A(htok[:, i, :], pair(1 + i % 3), ACT.Copy).then_inc(*E.sig("htok_ev"))

            def moe_pass(pre, k, used_sem, used_at):
                for s in range(2):
                    act.wait_ge(sem[pre + "selt_tr"], 2 * k + s + 1)
                    A(selT[:, s, :], pair640(3), ACT.Copy).then_inc(*E.sig(pre + "selt_ev"))
                for kc in range(KC):
                    act.wait_ge(sem[pre + "gat_mm"], KC * k + kc + 1)
                    A(hgT[:, kc, :], ps[:, 4 + kc % 2, 0:CAP], ACT.Copy).then_inc(*E.sig(pre + "gat_ev"))
                for f in range(FE):
                    act.wait_ge(sem[used_sem], used_at + up_done(f))
                    if f >= 2:
                        act.wait_ge(sem[pre + "eh_g"], FE * k + f - 1)
                    A(ftmp[:, f % 2, 0:CAP], ps[:, 4 + f % 2, 0:CAP], ACT.Tanh, scale=0.5).then_inc(*E.sig(pre + "eh_th"))
                act.wait_ge(sem[used_sem], used_at + EXP_B)
                for n in range(4):
                    A(ye[:, n // 2, (n % 2) * 512:(n % 2 + 1) * 512], ps[:, n, :], ACT.Copy).then_inc(*E.sig(pre + "ey_ev"))

            for l in range(DEPTH):
                if l == 0:
                    act.wait_ge(sem["cond_in"], 64)
                    A(tiny[:, 0:16], condT[:, :, :].rearrange("p a b -> p (a b)"), ACT.Tanh, scale=0.5).then_inc(*E.sig("act_step"))
                next_phase()
                norm_phase(2 * l)
                next_phase()
                proj_phase(l)
                next_phase()
                att_phase(l)
                next_phase()
                kk_phase(l)
                next_phase()
                for c in range(NPAIR):
                    rwkv_dir(l, c, 0)
                    rwkv_dir(l, c, 1)
                gn_phase(l)
                wo_phase(l)
                next_phase()
                post_phase(2 * l)
                next_phase()
                norm_phase(2 * l + 1)
                next_phase()
                if l == 0:
                    dense_phase(l)
                else:
                    route_phase()
                    next_phase()
                    for e in range(NE):
                        moe_pass("", e, "block_used", MOE_FIRST + e * EXP_B)
                    next_phase()

                    def body():
                        for n in range(2 * NE):
                            moe_pass("o_", n, "o_block_used", n * EXP_B)
                    with_flag(act, body)
                next_phase()
                post_phase(2 * l + 1)
                next_phase()

        @block.vector
        def _(dve):
            E = Signals("dve", sem)
            phase = [0]

            def next_phase():
                phase[0] += 1
                dve.drain().then_inc(sem["dve_phase"], 1)
                dve.wait_ge(sem["pe_phase"], phase[0])
                dve.wait_ge(sem["act_phase"], phase[0])
                dve.wait_ge(sem["dve_phase"], phase[0])
                dve.wait_ge(sem["pool_phase"], phase[0])

            V = nc.vector

            def mod_phase(l):
                if l == 0:
                    dve.wait_ge(sem["consts_in"], 16)
                    dve.wait_ge(sem["cond_in"], 64)
                    dve.wait_ge(sem["act_step"], 1)
                    cf = condT[:, :, :].rearrange("p a b -> p (a b)")
                    V.scalar_tensor_tensor(tiny[:, 16:32], tiny[:, 0:16], 1.0, cf, ALU.add, ALU.mult).then_inc(*E.sig("dve_step"))
                    dve.wait_ge(*E.own_last())
                    V.tensor_scalar(cf, tiny[:, 16:32], 0.5, None, ALU.mult).then_inc(*E.sig("silu_c"))
                    V.tensor_copy(identb[:, :], ident).then_inc(*E.sig("dve_step"))
                dve.wait_ge(sem["block_used"], BL(l) + MOD_B)
                V.tensor_tensor(mod[:, :, :], ps[:, 0, 0:96].rearrange("p (j g) -> p j g", g=2),
                                      PR(l, "b_mod").unsqueeze(2).broadcast_to([P, 48, 2]), ALU.add).then_inc(*E.sig("dve_step"))
                dve.wait_ge(*E.own_last())
                for w, (sc, gt, gpr, gpo) in enumerate([(8, 16, "g_pre_mix", "g_post_mix"), (32, 40, "g_pre_ffn", "g_post_ffn")]):
                    V.scalar_tensor_tensor(gpre[:, w, :, :], mod[:, sc:sc + 8, :], 1.0,
                                                 PR(l, gpr).unsqueeze(2).broadcast_to([P, 8, 2]), ALU.add, ALU.mult).then_inc(*E.sig("dve_step"))
                    V.tensor_tensor(gpost[:, w, :, :], mod[:, gt:gt + 8, :],
                                          PR(l, gpo).unsqueeze(2).broadcast_to([P, 8, 2]), ALU.mult).then_inc(*E.sig("dve_step"))
                V.tensor_scalar(hpar[:, 0:12], PR(l, "mu"), 0.5, None, ALU.mult).then_inc(*E.sig("dve_step"))
                V.tensor_scalar(hpar[:, 16:24], PR(l, "w0"), 0.5, None, ALU.mult).then_inc(*E.sig("dve_step"))
                V.tensor_scalar(hpar[:, 24:32], PR(l, "a0"), 0.5, None, ALU.mult).then_inc(*E.sig("dve_step"))
                V.tensor_scalar(hpar[:, 32:36], PR(l, "k_a"), 0.5, None, ALU.mult).then_inc(*E.sig("dve_step"))
                V.tensor_scalar(hpar[:, 36:40], PR(l, "k_a"), -0.5, 1.0, ALU.mult, ALU.add).then_inc(*E.sig("dve_step"))
                V.tensor_scalar(hpar[:, 40:52], PR(l, "mu"), -1.0, 1.0, ALU.mult, ALU.add).then_inc(*E.sig("mod_done"))

            def norm_phase(k):
                dve.wait_ge(sem["norm_sq"], NT * (k + 1))
                V.tensor_scalar(nstat[:, 5:10], nstat[:, 0:5], 1.0 / D, NORM_EPS, ALU.mult, ALU.add).then_inc(*E.sig("norm_ms"))
                dve.wait_ge(sem["norm_pow"], k + 1)
                for i in range(NT):
                    V.tensor_scalar(xn[:, i, :], x[:, i, :], nstat[:, 15 + i:16 + i], None, ALU.mult).then_inc(*E.sig("norm_x"))
                for kc in range(KC):
                    dve.wait_ge(sem["norm_tr"], KC * k + kc + 1)
                    w, sh = k % 2, (0 if k % 2 == 0 else 24)
                    V.tensor_scalar(hT[:, kc, 0:CTX], pair(kc % 4)[:, 384:512], gpre[:, w, kc, 0:1],
                                          mod[:, sh + kc, 0:1], ALU.mult, ALU.add).then_inc(*E.sig("norm_ev_dve"))

            def proj_phase(l):
                for o in range(PROJ_B):
                    if 6 <= o < 18 or o == 20:
                        dve.wait_ge(sem["proj_ev_act"], l * PROJ_B + o + 1)
                    if 6 <= o < 18:
                        j = o - 6
                        pr = praw[:, j % 2, :]
                        sh = pshift[:, j % 2, :]
                        V.tensor_tensor(sh[:, 0:CTX], pr[:, 0:128], pr[:, 2:130], ALU.add).then_inc(*E.sig("dve_step"))
                        V.tensor_tensor(sh[:, CTX:T], pr[:, 129:641], pr[:, 131:643], ALU.add).then_inc(*E.sig("dve_step"))
                        dve.wait_ge(*E.own_last())
                        V.scalar_tensor_tensor(rkv[:, j, :], pair640(o % 4), hpar[:, 40 + j:41 + j], sh[:, :], ALU.mult, ALU.add).then_inc(*E.sig("proj_ev_dve"))
                    elif o == 20:
                        V.tensor_scalar(zlow[:, 2, :], zlow[:, 2, :], 0.5, 0.5, ALU.mult, ALU.add).then_inc(*E.sig("proj_ev_dve"))

            def att_phase(l):
                for c in range(5):
                    dve.wait_ge(sem["rope_mm"], 5 * l + c + 1)
                    dst = qT[:, c, CTX:T] if c < 4 else kT[:, CTX:T]
                    tmp = ropetmp[:, c % 2, :]
                    V.tensor_tensor(tmp, ps[:, c, :], C("sin"), ALU.mult).then_inc(*E.sig("dve_step"))
                    V.tensor_tensor(dst, dst, C("cos"), ALU.mult).then_inc(*E.sig("dve_step"))
                    dve.wait_ge(*E.own_last())
                    V.tensor_tensor(dst, dst, tmp, ALU.add).then_inc(*E.sig("rope_ev"))
                dve.wait_ge(sem["kc_tr"], l + 1)
                V.tensor_copy(kcT[:, :], ps[:, 5, 0:PAST]).then_inc(*E.sig("kc_ev"))
                for t in range(N_UNITS + 2):
                    if t < N_UNITS:
                        c, g, blkq = unit(t)
                        un = l * N_UNITS + t
                        h = l * NH + c + 4 * g
                        a = attst[:, t % 2, :]
                        dve.wait_ge(sem["att_s"], un + 1)
                        V.tensor_reduce(a[:, 0:1], pair(t % 2)[:, 0:n_keys(blkq)], AX.X, ALU.max).then_inc(*E.sig("dve_step"))
                        dve.wait_ge(*E.own_last())
                        V.tensor_scalar(a[:, 1:2], a[:, 0:1], sink[:, h:h + 1], -1.0, ALU.max, ALU.mult).then_inc(*E.sig("att_max"))
                    if 1 <= t <= N_UNITS:
                        u = t - 1
                        un = l * N_UNITS + u
                        a = attst[:, u % 2, :]
                        dve.wait_ge(sem["att_exp"], un + 1)
                        V.tensor_tensor(a[:, 4:5], a[:, 2:3], a[:, 3:4], ALU.add).then_inc(*E.sig("dve_step"))
                        dve.wait_ge(*E.own_last())
                        V.reciprocal(a[:, 5:6], a[:, 4:5]).then_inc(*E.sig("dve_step"))
                        dve.wait_ge(*E.own_last())
                        nk = n_keys(unit(u)[2])
                        V.tensor_scalar(prob[:, u % 2, 0:nk], prob[:, u % 2, 0:nk], a[:, 5:6], None, ALU.mult).then_inc(*E.sig("att_p"))
                    if t >= 2 and t % 2 == 1:
                        u = t - 2
                        c, g, blkq = unit(u)
                        dve.wait_ge(sem["att_o"], l * N_UNITS + u + 1)
                        V.tensor_copy(oT[:, c, (blkq + 1) * P:(blkq + 2) * P], ps[:, 6 + (u // 2) % 2, 0:P]).then_inc(*E.sig("att_oev"))

            def tiles(a):
                return a.rearrange("p (i t) -> p i t", i=NT)

            def kk_phase(l):
                dve.wait_ge(sem["kk_sum"], l + 1)
                V.tensor_scalar(rw_s[:, 3, :, :].rearrange("p i h -> p (i h)"), ps[:, 0, 0:NT * RH], 1e-12, None, ALU.add).then_inc(*E.sig("kk_ss"))

            def rwkv_dir(l, c, d):
                g = (l * NPAIR + c) * 2 + d
                k = l * NPAIR + c
                kr = rkv[:, 4 + c, :]
                rr = rkv[:, c, :]
                dve.wait_ge(sem["low_w"], g + 1)
                V.tensor_scalar(lw[:, :], tw[:, :], -HALF_DECAY, -HALF_DECAY, ALU.mult, ALU.add).then_inc(*E.sig("dve_step"))
                dve.wait_ge(*E.own_last())
                V.tensor_reduce(phs[:, 0, :], tiles(lw), AX.X, ALU.add).then_inc(*E.sig("dve_step"))
                dve.wait_ge(*E.own_last())
                V.tensor_scalar(nstat[:, 10:15], phs[:, 0, :], -0.5, None, ALU.mult).then_inc(*E.sig("dve_step"))
                dve.wait_ge(*E.own_last())
                for i in range(NT):
                    sl = slice(i * P, (i + 1) * P)
                    ins = V.tensor_tensor_scan(cumc[:, sl], C("ones"), lw[:, sl], nstat[:, 10 + i:11 + i], ALU.mult, ALU.add)
                    ins.then_inc(*E.sig("dec_cum" if i == NT - 1 else "dve_step"))
                dve.wait_ge(*E.own_last())
                V.tensor_tensor(cumx[:, :], cumc[:, :], lw[:, :], ALU.subtract).then_inc(*E.sig("dec_cumx"))
                if d == 0:
                    dve.wait_ge(sem["kk_mm"], k + 1)
                    V.scalar_tensor_tensor(kk[:, :], kr, PR(l, "k_k", c), pair640(2), ALU.mult, ALU.mult).then_inc(*E.sig("kk_done"))
                dve.wait_ge(sem["low_ev"], g + 1)
                V.tensor_scalar(kdt[:, :], ta[:, :], hpar[:, 32 + c:33 + c], hpar[:, 36 + c:37 + c], ALU.mult, ALU.add).then_inc(*E.sig("dve_step"))
                V.tensor_scalar(avec[:, :], ta[:, :], 0.5, 0.5, ALU.mult, ALU.add).then_inc(*E.sig("dve_step"))
                dve.wait_ge(*E.own_last())
                V.tensor_tensor(kdt[:, :], kdt[:, :], kr, ALU.mult).then_inc(*E.sig("dve_step"))
                V.tensor_tensor(avec[:, :], avec[:, :], kk[:, :], ALU.mult).then_inc(*E.sig("dve_step"))
                dve.wait_ge(*E.own_last())
                first, second, third = 3 * g + 1, 3 * g + 2, 3 * g + 3
                dve.wait_ge(sem["dec_exp"], third)
                V.tensor_tensor(bkbar[:, 0, :], avec[:, :], e_inv[:, :], ALU.mult).then_inc(*E.sig("dve_step"))
                V.tensor_tensor(bkbar[:, 1, :], kdt[:, :], e_inv[:, :], ALU.mult).then_inc(*E.sig("rw_ops"))
                V.scalar_tensor_tensor(ar[:, :, 0, :], tiles(kk), -1.0, tiles(e_ex), ALU.mult, ALU.mult).then_inc(*E.sig("dve_step"))
                V.tensor_tensor(ar[:, :, 1, :], tiles(rr), tiles(e_in), ALU.mult).then_inc(*E.sig("ar_done"))
                V.memset(st[:, :, :].rearrange("p b v -> p (b v)"), 0.0).then_inc(*E.sig("dve_step"))
                dve.wait_ge(sem["st_tr"], g + 1)
                dve.wait_ge(*E.own_last())
                V.tensor_copy(st[0:64, 1, 0:64], ps[0:64, 0, 0:64]).then_inc(*E.sig("dve_step"))
                V.tensor_copy(st[64:128, 1, 64:128], ps[64:128, 0, 0:64]).then_inc(*E.sig("st_ev"))
                if d == 0:
                    V.tensor_copy(kds[:, :], kdt[:, :]).then_inc(*E.sig("dve_step"))
                else:
                    V.tensor_tensor(kds[:, :], kds[:, :], kdt[:, :], ALU.add).then_inc(*E.sig("dve_step"))
                    dve.wait_ge(*E.own_last())
                    V.scalar_tensor_tensor(kds[:, :], rr, PR(l, "r_k", c), kds[:, :], ALU.mult, ALU.mult).then_inc(*E.sig("bon_prod"))
                dve.wait_ge(*E.own_last())
                mask = C("mask_f" if d == 0 else "mask_b").unsqueeze(1).broadcast_to([P, 2, 256])
                dve.wait_ge(sem["dec_ph"], g + 1)
                for u in range(10):
                    dve.wait_ge(sem["gram_mm"], 10 * g + u + 1)
                    V.tensor_tensor(gm[:, u, :, :].rearrange("p (b a) t -> p b (a t)", b=2), ps[:, u % 8, :].rearrange("p (b c) -> p b c", b=2),
                                    mask, ALU.mult).then_inc(*E.sig("gram_ev"))
                idents = ident.unsqueeze(1).broadcast_to([P, 2, P])
                for i in range(NT):
                    if i == 0:
                        dve.wait_ge(*E.own_last())
                    V.tensor_tensor(xq[:, 2 * i:2 * i + 2, :], gm[:, 2 * i:2 * i + 2, 0, :], idents, ALU.add).then_inc(*E.sig("x0_ev"))
                    dve.wait_ge(sem["lt_tr"], 5 * g + i + 1)
                    V.tensor_tensor(lfi[:, 2 * i:2 * i + 2, :], ps[:, i % 4, 0:256].rearrange("p (h t) -> p h t", h=2), idents,
                                    ALU.subtract).then_inc(*E.sig("lt_sub"))
                for m in range(30):
                    i = m % 5
                    dve.wait_ge(sem["inv_mm"], 30 * g + m + 1)
                    src = ps[:, 4 + m % 4, 0:256].rearrange("p (h t) -> p h t", h=2)
                    dst = xq[:, 2 * i:2 * i + 2, :] if m < 25 else gm[:, 2 * i:2 * i + 2, 0, :]
                    V.tensor_tensor(dst, xq[:, 2 * i:2 * i + 2, :], src, ALU.add).then_inc(*E.sig("inv_ev"))
                for q in range(2):
                    for i in range(NT):
                        n = (2 * g + q) * NT + i
                        dve.wait_ge(sem["nw_p"], n + 1)
                        if q == 0:
                            dve.wait_ge(sem["mv_mm"], 5 * g + 5)
                        else:
                            dve.wait_ge(sem["nw_c"], n - 4)
                        V.tensor_tensor(gmb[:, 2 * i:2 * i + 2, 2, 0:P], ps[:, i % 4, 0:256].rearrange("p (h t) -> p h t", h=2), idents,
                                        ALU.add).then_inc(*E.sig("nw_e"))
                    for i in range(NT):
                        n = (2 * g + q) * NT + i
                        dve.wait_ge(sem["nw_c"], n + 1)
                        x_u = gm[:, 2 * i:2 * i + 2, 0, :]
                        V.tensor_tensor(x_u, x_u, ps[:, 4 + i % 4, 0:256].rearrange("p (h t) -> p h t", h=2), ALU.add).then_inc(*E.sig("nw_x"))
                for n, i in enumerate(order(d)):
                    if n == 0:
                        V.memset(s0s[:, i, :], 0.0).then_inc(*E.sig("st_scaled"))
                    else:
                        dve.wait_ge(*E.own_last())
                        V.tensor_scalar(s0s[:, i, :], st[:, 1, :], phs[:, 0, i:i + 1], None, ALU.mult).then_inc(*E.sig("st_scaled"))
                        if n < NT - 1:
                            V.tensor_scalar(stpc[:, :], st[:, 1, :], phs[:, 1, i:i + 1], None, ALU.mult).then_inc(*E.sig("dve_step"))
                    dve.wait_ge(sem["x_mm"], 5 * g + n + 1)
                    V.tensor_tensor(xb[:, n % 2, :], ps[:, 0, 0:P], mv[:, i, :], ALU.add).then_inc(*E.sig("x_ev"))
                    if n == NT - 1:
                        break
                    dve.wait_ge(sem["s_mm"], 4 * g + n + 1)
                    for hh in range(2):
                        h = slice(64 * hh, 64 * hh + 64)
                        if n == 0:
                            ins = V.tensor_scalar(st[h, 0, h], ps[h, 2, h], phs[h, 0, i:i + 1], None, ALU.mult)
                        else:
                            ins = V.scalar_tensor_tensor(st[h, 1, h], ps[h, 2, h], phs[h, 0, i:i + 1], stpc[h, h], ALU.mult, ALU.add)
                        ins.then_inc(*E.sig("s_ev" if hh == 1 else "dve_step"))
                dve.wait_ge(sem["y_mm"], g + 1)
                if d == 0:
                    V.tensor_copy(oT[:, 4 + c, :], pair640(2)).then_inc(*E.sig("y_ev"))
                else:
                    V.tensor_tensor(oT[:, 4 + c, :], oT[:, 4 + c, :], pair640(2), ALU.add).then_inc(*E.sig("y_ev"))
                next_phase()

            def gn_phase(l):
                for c in range(NPAIR):
                    y = oT[:, 4 + c, :]
                    dve.wait_ge(sem["gn_mean_mm"], l * NPAIR + c + 1)
                    V.tensor_tensor(y, y, pair640(c), ALU.subtract).then_inc(*E.sig("gn_cent"))
                dve.wait_ge(sem["gn_sum"], l + 1)
                V.tensor_scalar(rw_s[:, 3, :, :].rearrange("p i h -> p (i h)"), ps[:, 0, 0:NT * RH], 1.0 / HD, GN_EPS, ALU.mult, ALU.add).then_inc(*E.sig("gn_ms"))
                for c in range(NPAIR):
                    y = oT[:, 4 + c, :]
                    at = 12 * l + 3 * c
                    norm, bonus, gate_p = [pair640((3 * c + w + 1) % 4) for w in range(3)]
                    dve.wait_ge(sem["gn_mm"], at + 1)
                    V.scalar_tensor_tensor(y, y, PR(l, "ln_g", c), norm, ALU.mult, ALU.mult).then_inc(*E.sig("gn_used"))
                    dve.wait_ge(sem["gn_mm"], at + 2)
                    V.tensor_tensor(bon[:, c % 2, :], rkv[:, 8 + c, :], bonus, ALU.mult).then_inc(*E.sig("dve_step"))
                    dve.wait_ge(*E.own_last())
                    V.scalar_tensor_tensor(y, y, PR(l, "ln_b", c), bon[:, c % 2, :], ALU.add, ALU.add).then_inc(*E.sig("gn_used"))
                    dve.wait_ge(*E.own_last())
                    dve.wait_ge(sem["gn_mm"], at + 3)
                    V.tensor_tensor(y, y, gate_p, ALU.mult).then_inc(*E.sig("gn_used"))
                next_phase()

            def post_phase(k):
                w = k % 2
                for n in range(16):
                    g, kc = n // 8, n % 8
                    if n >= 4:
                        dve.wait_ge(sem["rowvec_mm"], 16 * k + n - 3)
                    V.tensor_scalar(diag(n), ident, gpost[:, w, kc, g:g + 1], None, ALU.mult).then_inc(*E.sig("rowvec_diag"))
                dve.wait_ge(sem["post_sq"], NT * (k + 1))
                V.tensor_scalar(nstat[:, 5:10], nstat[:, 0:5], 1.0 / D, NORM_EPS, ALU.mult, ALU.add).then_inc(*E.sig("post_ms"))
                dve.wait_ge(sem["post_pow"], k + 1)
                dve.wait_ge(sem["rowvec_mm"], 16 * (k + 1))
                for i in range(NT):
                    V.scalar_tensor_tensor(fo[:, i, :], fo[:, i, :], nstat[:, 15 + i:16 + i], pair(0 if i == 0 else 1), ALU.mult, ALU.mult).then_inc(*E.sig("post_tmp"))
                for i in range(NT):
                    if i == 0:
                        dve.wait_ge(*E.own_last())
                    V.tensor_tensor(x[:, i, :], x[:, i, :], fo[:, i, :], ALU.add).then_inc(*E.sig("post_x"))

            def dense_phase(l):
                for f in range(FT):
                    dve.wait_ge(sem["ff_th"], f + 1)
                    a, b = pair640(2 * f % 4), pair640((2 * f + 1) % 4)
                    V.scalar_tensor_tensor(ftmp[:, f % 2, :], ftmp[:, f % 2, :], 1.0, a, ALU.add, ALU.mult).then_inc(*E.sig("dve_step"))
                    dve.wait_ge(*E.own_last())
                    V.scalar_tensor_tensor(gT[:, f, :], ftmp[:, f % 2, :], 0.5, b, ALU.mult, ALU.mult).then_inc(*E.sig("ff_g"))

            def route_phase():
                dve.wait_ge(sem["rt_mm"], 1)
                V.tensor_copy(lg, ps[:, 0, 0:40].rearrange("p (i e) -> p i e", i=NT)).then_inc(*E.sig("dve_step"))
                dve.wait_ge(*E.own_last())
                for i in range(NT):
                    V.max(m8[:, i, :], lg[:, i, :]).then_inc(*E.sig("dve_step"))
                dve.wait_ge(*E.own_last())
                V.tensor_scalar(rstat[:, 0:5], m8[:, :, 0], -1.0, None, ALU.mult).then_inc(*E.sig("dve_step"))
                for i in range(NT):
                    ins = V.tensor_scalar(msk[:, i, :], lg[:, i, :], m8[:, i, 1:2], None, ALU.is_ge)
                    ins.then_inc(*E.sig("rt_max" if i == NT - 1 else "dve_step"))
                dve.wait_ge(sem["rt_exp"], 1)
                dve.wait_ge(*E.own_last())
                V.tensor_tensor(gate, gate, msk, ALU.mult).then_inc(*E.sig("dve_step"))
                dve.wait_ge(*E.own_last())
                V.tensor_reduce(rstat[:, 5:10], gate, AX.X, ALU.add).then_inc(*E.sig("dve_step"))
                dve.wait_ge(*E.own_last())
                V.reciprocal(rstat[:, 10:15], rstat[:, 5:10]).then_inc(*E.sig("dve_step"))
                dve.wait_ge(*E.own_last())
                V.tensor_tensor(gate, gate, rstat[:, 10:15].unsqueeze(2).broadcast_to([P, NT, NE]), ALU.mult).then_inc(*E.sig("rt_gate"))
                dve.wait_ge(sem["rt_cum"], 1)
                V.scalar_tensor_tensor(rk, ps[:, 1, 0:40].rearrange("p (i e) -> p i e", i=NT), 1.0, msk, ALU.add, ALU.mult).then_inc(*E.sig("dve_step"))
                V.tensor_reduce(rstat[:, 16:17], ps[:, 1, 40:48], AX.X, ALU.max).then_inc(*E.sig("dve_step"))
                dve.wait_ge(*E.own_last())
                V.tensor_scalar(rk, rk, -1.0, None, ALU.add).then_inc(*E.sig("rt_rank"))
                V.tensor_copy(flag_i[0:1, 0:1], rstat[0:1, 16:17]).then_inc(*E.sig("rt_rank"))

            def moe_pass(pre, e, k, base):
                first = base == 0 and e == 0
                if k >= 1:
                    dve.wait_ge(sem[pre + "gat_mm"], KC * k)
                    dve.wait_ge(sem[pre + "selt_tr"], 2 * k)
                if base:
                    V.tensor_scalar(rstat[:, 20:25], rk[:, :, e], -float(base), None, ALU.add).then_inc(*E.sig("dve_step"))
                else:
                    V.tensor_scalar(rstat[:, 20:25], rk[:, :, e], 0.0, None, ALU.add).then_inc(*E.sig("dve_step"))
                dve.wait_ge(*E.own_last())
                for i in range(NT):
                    V.tensor_scalar(sel[:, i, :], C("iota"), rstat[:, 20 + i:21 + i], None, ALU.is_equal).then_inc(*E.sig("dve_step"))
                for i in range(NT):
                    ins = V.tensor_scalar(selg[:, i, :], C("iota"), rstat[:, 20 + i:21 + i], gate[:, i, e:e + 1], ALU.is_equal, ALU.mult)
                    ins.then_inc(*E.sig((pre + "sel_dve") if i == NT - 1 else "dve_step"))
                for f in range(FE):
                    dve.wait_ge(sem[pre + "eh_th"], FE * k + f + 1)
                    b = ps[:, 4 + f % 2, :]
                    t = ftmp[:, f % 2, 0:CAP]
                    V.scalar_tensor_tensor(t, t, 1.0, b[:, 0:CAP], ALU.add, ALU.mult).then_inc(*E.sig("dve_step"))
                    dve.wait_ge(*E.own_last())
                    V.scalar_tensor_tensor(geT[:, f, :], t, 0.5, b[:, CAP:2 * CAP], ALU.mult, ALU.mult).then_inc(*E.sig(pre + "eh_g"))
                for n in range(10):
                    i, h = n // 2, n % 2
                    dve.wait_ge(sem[pre + "comb_mm"], 10 * k + n + 1)
                    dst = fo[:, i, h * 512:(h + 1) * 512]
                    if first:
                        V.tensor_copy(dst, ps[:, 6 + n % 2, :]).then_inc(*E.sig(pre + "comb_ev"))
                    else:
                        V.tensor_tensor(dst, dst, ps[:, 6 + n % 2, :], ALU.add).then_inc(*E.sig(pre + "comb_ev"))

            for l in range(DEPTH):
                mod_phase(l)
                next_phase()
                norm_phase(2 * l)
                next_phase()
                proj_phase(l)
                next_phase()
                att_phase(l)
                next_phase()
                kk_phase(l)
                next_phase()
                for c in range(NPAIR):
                    rwkv_dir(l, c, 0)
                    rwkv_dir(l, c, 1)
                gn_phase(l)
                next_phase()
                post_phase(2 * l)
                next_phase()
                norm_phase(2 * l + 1)
                next_phase()
                if l == 0:
                    dense_phase(l)
                else:
                    route_phase()
                    next_phase()
                    for e in range(NE):
                        moe_pass("", e, e, 0)
                    next_phase()

                    def body():
                        for n in range(2 * NE):
                            moe_pass("o_", n % NE, n, CAP * (1 + n // NE))
                    with_flag(dve, body)
                next_phase()
                post_phase(2 * l + 1)
                next_phase()

        @block.gpsimd
        def _(pool):
            E = Signals("pool", sem)
            phase = [0]

            def next_phase():
                phase[0] += 1
                pool.drain().then_inc(sem["pool_phase"], 1)
                pool.wait_ge(sem["pe_phase"], phase[0])
                pool.wait_ge(sem["act_phase"], phase[0])
                pool.wait_ge(sem["dve_phase"], phase[0])
                pool.wait_ge(sem["pool_phase"], phase[0])

            n_out = [0]

            def power(dst, src, rows, n, what):
                nc.gpsimd.tensor_tensor(dst, src, C("power", rows)[:, 0:n], ALU.pow).then_inc(sem[what], 1)

            def store(dst, src):
                pool.dma_start(dst, src).then_inc(sem["results_out"], 16)
                n_out[0] += 16

            def norm_phase(k):
                pool.wait_ge(sem["norm_ms"], k + 1)
                power(nstat[:, 15:20], nstat[:, 5:10], P, 5, "norm_pow")

            def post_phase(k):
                pool.wait_ge(sem["post_ms"], k + 1)
                power(nstat[:, 15:20], nstat[:, 5:10], P, 5, "post_pow")

            pool.wait_ge(sem["consts_in"], 16)
            for l in range(DEPTH):
                if n_out[0]:
                    pool.wait_ge(sem["results_out"], n_out[0])
                pool.dma_start(w2[:, :, :], low2[l]).then_inc(sem["misc_in"], 16)
                pool.dma_start(ck[:, :, :], cache_k[l].rearrange("(i p) c -> p i c", p=P)).then_inc(sem["misc_in"], 16)
                pool.dma_start(cv[:, :, :], cache_v[l].rearrange("(i p) c -> p i c", p=P)).then_inc(sem["misc_in"], 16)
                for d in range(2):
                    pool.dma_start(st_in[:, d, :, :], state[l, d].rearrange("h v k -> v h k")).then_inc(sem["misc_in"], 16)
                next_phase()
                norm_phase(2 * l)
                next_phase()
                next_phase()
                store(new_k[l], kctok[:, :])
                store(new_v[l], vtok[:, 0, :])
                pool.wait_ge(sem["results_out"], n_out[0])
                next_phase()
                pool.wait_ge(sem["kk_ss"], l + 1)
                power(rw_s[:, 0, :, :].rearrange("p i h -> p (i h)"), rw_s[:, 3, :, :].rearrange("p i h -> p (i h)"), P, NT * RH, "kk_pow")
                next_phase()
                for _ in range(2 * NPAIR):
                    next_phase()
                pool.wait_ge(sem["gn_ms"], l + 1)
                power(rw_s[:, 2, :, :].rearrange("p i h -> p (i h)"), rw_s[:, 3, :, :].rearrange("p i h -> p (i h)"), P, NT * RH, "gn_pow")
                next_phase()
                for d in range(2):
                    store(new_state[l, d].rearrange("(c h) v k -> (h v) c k", h=2), st_out[:, d, :, :])
                next_phase()
                post_phase(2 * l)
                next_phase()
                norm_phase(2 * l + 1)
                next_phase()
                if l == 1:
                    next_phase()
                    next_phase()
                next_phase()
                post_phase(2 * l + 1)
                next_phase()
            store(y_all.rearrange("(i p) d -> p i d", p=P), x[:, :, :])
            pool.wait_ge(sem["results_out"], n_out[0])


def kernel(**a):
    import concourse.bacc as bacc
    from concourse.bass_utils import run_bass_kernel_spmd

    a = {k: np.asarray(v) for k, v in a.items()}

    def cols(w):
        k, n = w.shape
        return w.reshape(k // P, P, n // P, P).transpose(2, 1, 0, 3).reshape(n // P, P, -1)

    def chan(v):
        return v.reshape(-1, P).T

    heads = np.arange(NH).reshape(2, 4).T.reshape(-1)
    qcols = (heads[:, None] * HD + np.arange(HD)[None, :]).reshape(-1)
    blocks, small = [], []
    for l in range(DEPTH):
        w_in = a["w_in"][l]
        blocks.append(cols(a["w_mod"][l]))
        blocks.append(cols(w_in[:, qcols]))
        blocks.append(cols(w_in[:, 512:]))
        for w in (a["rw_w1"][l], a["rw_a1"][l]):
            blocks.append(cols(np.concatenate([w[0], w[1]], 1)))
        blocks.append(cols(a["rw_g1"][l]))
        wo = a["w_o"][l]
        blocks.append(np.concatenate([wo[qcols], wo[512:]], 0).reshape(8, P, D))
        if l == 0:
            w1, w3 = cols(a["ffn_w1"][0]), cols(a["ffn_w3"][0])
            blocks.append(np.stack([w1, w3], 1).reshape(2 * FT, P, D))
            w2 = a["ffn_w2"][0].reshape(FT // 2, 2, P, 2, 512)
            blocks.append(w2.transpose(3, 0, 2, 1, 4).reshape(FT, P, D))
        else:
            for e in range(NE):
                w1, w3 = cols(a["moe_w1"][0, e]), cols(a["moe_w3"][0, e])
                w2 = a["moe_w2"][0, e].reshape(FE, P, D)
                seq = []
                for f in range(FE + 1):
                    if f < FE:
                        seq += [w1[f], w3[f]]
                    if f >= 1:
                        seq.append(w2[f - 1])
                blocks.append(np.stack(seq))
        small += [chan(v) for v in (a["b_mod"][l], a["g_pre_mix"][l], a["g_post_mix"][l], a["g_pre_ffn"][l],
                                    a["g_post_ffn"][l], a["mu_shift"][l], a["rw_w0"][l], a["rw_a0"][l], a["rw_k_k"][l],
                                    a["rw_k_a"][l], a["rw_r_k"][l], a["rw_ln_g"][l], a["rw_ln_b"][l])]
    low2 = np.stack([a["rw_w2"].reshape(DEPTH, P, 512), a["rw_a2"].reshape(DEPTH, P, 512), a["rw_g2"]], 2)
    ins = {
        "blocks": np.concatenate(blocks, 0),
        "x_all": np.concatenate([a["x_prompt"][0], a["x_sample"][0]], 0),
        "small": np.concatenate(small, 1),
        "cond": np.stack([chan(a["c_ctx"]), chan(a["c"][0])], 2),
        "sinkrows": np.broadcast_to(a["attn_sink"].reshape(1, -1), (P, DEPTH * NH)),
        "router": a["moe_router"][0].reshape(KC, P, NE).transpose(1, 0, 2),
        "low2": low2,
        "cache_k": a["cache_k"][0].reshape(DEPTH, PAST, KVH * HD),
        "cache_v": a["cache_v"][0].reshape(DEPTH, PAST, KVH * HD),
        "state": a["state_rwkv"][0],
        "consts": constants(),
    }
    nc = bacc.Bacc("TRN2", target_bir_lowering=False, num_devices=1)
    arrays, args = {}, []
    for name, v in ins.items():
        v = np.ascontiguousarray(v)
        arrays["in_" + name] = v
        args.append(nc.dram_tensor("in_" + name, v.shape, mybir.dt.from_np(v.dtype), kind="ExternalInput").ap())
    args.append(None)
    for name, shape in (("y_all", (T, D)), ("new_k", (DEPTH, CTX, KVH * HD)), ("new_v", (DEPTH, CTX, KVH * HD)),
                        ("new_state", (DEPTH, 2, RH, HD, HD))):
        args.append(nc.dram_tensor("out_" + name, shape, F32, kind="ExternalOutput").ap())
    build(nc, *args)
    r = run_bass_kernel_spmd(nc, [arrays], core_ids=[0]).results[0]
    y = r["out_y_all"]
    return (y[:CTX].reshape(1, CTX, D), y[CTX:].reshape(1, LAT, D),
            r["out_new_k"].reshape(1, DEPTH, CTX, KVH, HD), r["out_new_v"].reshape(1, DEPTH, CTX, KVH, HD),
            r["out_new_state"][None])
```

```python
from contextlib import ExitStack

import numpy as np

import concourse.bass as bass
from concourse import mybir

ALU = mybir.AluOpType
ACT = mybir.ActivationFunctionType
AX = mybir.AxisListType
F32 = mybir.dt.float32
F32R = mybir.dt.float32r
I32 = mybir.dt.int32
BF16 = mybir.dt.bfloat16

P = 128
D = 1024
KC = D // P
CTX = 128
LAT = 512
T = CTX + LAT
NT = T // P
DEPTH = 2
PAST = 256
NH, KVH, HD = 8, 2, 64
RH = 8
NPAIR = RH // 2
GRID_W = 64
WINDOW = 128
THETA = 10000.0
DFF = 2816
NE = 8
DFE = 1408
FT = DFF // P
FE = DFE // P
CAP = 256
NORM_EPS = 1e-6
GN_EPS = 64e-5
ARENA = 30208
HALF_DECAY = 0.5 * float(np.exp(-0.5))

RING = 9
MOD_B = 48
PROJ_B = 21
WO_B = 8
DENSE_B = 3 * FT
EXP_B = 3 * FE
MOD_G = 12
MOD_FIRST, MOD_MID = 4, MOD_G + 4
PROJ_AT = [4 * MOD_FIRST, 4 * MOD_MID + PROJ_B + WO_B + DENSE_B]
WO_AT = [4 * MOD_MID + PROJ_B, PROJ_AT[1] + PROJ_B + 4 * (2 * MOD_G - MOD_MID)]
FFN_AT = [WO_AT[0] + WO_B, WO_AT[1] + WO_B]
N_BLOCKS = FFN_AT[1] + NE * EXP_B
MOE_FIRST = N_BLOCKS - NE * EXP_B

PAR = {}
_n = 0
for _name, _w in [("b_mod", 48), ("g_pre_mix", 8), ("g_post_mix", 8), ("g_pre_ffn", 8), ("g_post_ffn", 8),
                  ("mu", 12), ("w0", 8), ("a0", 8), ("k_k", 4), ("k_a", 4), ("r_k", 4), ("ln_g", 4), ("ln_b", 4)]:
    PAR[_name] = (_n, _w)
    _n += _w
NPAR = _n

CON = {}
_n = 0
for _name, _w in [("ident", 128), ("rot", 128), ("mask_f", 256), ("mask_b", 256), ("cos", 512), ("sin", 512),
                  ("m_prev", 128), ("m_next", 128), ("head_ones", 128), ("head_mean", 128), ("ones", 128),
                  ("before", 128), ("iota", 256), ("head_sel", 2), ("head_exp", 128), ("power", 40)]:
    CON[_name] = (_n, _w)
    _n += _w
NCON = _n


def constants():
    c = np.zeros((P, NCON), np.float32)

    def put(name, a):
        at, w = CON[name]
        c[:a.shape[0], at:at + a.shape[1]] = a

    i = np.arange(P)
    put("ident", np.eye(P, dtype=np.float32))
    rot = np.zeros((P, P), np.float32)
    for ch in range(P):
        if ch % 32 < 16:
            rot[ch + 16, ch] = -1.0
        else:
            rot[ch - 16, ch] = 1.0
    put("rot", rot)
    s, t = i[:, None], i[None, :]
    put("mask_f", np.concatenate([s < t, s <= t], 1).astype(np.float32))
    put("mask_b", np.concatenate([s > t, s >= t], 1).astype(np.float32))
    nf = HD // 4
    inv = (np.float32(THETA) ** (-np.arange(nf, dtype=np.float32) / np.float32(nf))).astype(np.float32)
    tok = np.arange(LAT)
    ch = i % HD
    pos = np.where((ch < 32)[:, None], (tok // GRID_W)[None, :], (tok % GRID_W)[None, :]).astype(np.float32)
    ang = pos * inv[ch % nf][:, None]
    put("cos", np.cos(ang).astype(np.float32))
    put("sin", np.sin(ang).astype(np.float32))
    q, k = i[:, None], i[None, :]
    put("m_prev", np.where(k >= q, 0.0, -1e30).astype(np.float32))
    put("m_next", np.where(k <= q, 0.0, -1e30).astype(np.float32))
    same = (s // HD == t // HD).astype(np.float32)
    put("head_ones", same)
    put("head_mean", same / HD)
    put("ones", np.ones((P, P), np.float32))
    put("before", (s < t).astype(np.float32))
    put("iota", np.broadcast_to(np.arange(CAP, dtype=np.float32), (P, CAP)))
    put("head_sel", (s // HD == np.arange(2)[None, :]).astype(np.float32))
    put("head_exp", (np.arange(2)[:, None] == t // HD).astype(np.float32))
    put("power", np.full((P, NT * RH), -0.5, np.float32))
    return c


SEMS = """consts_in cond_in x_in misc_in block_used silu_c mod_row mod_tr mod_ev rowvec_diag rowvec_mm norm_sq stat_ms
stat_pow norm_x norm_tr norm_ev_act norm_ev_dve proj_ev_act proj_ev_dve rope_mm rope_ev kc_tr kc_ev att_s
att_max att_exp att_p att_tr att_trev att_o att_oev kk_prod kk_sum kk_ss kk_pow kk_mm spread_ev kk_done vt_tr
vt_ev low_mm low_w low_ev dec_cum dec_cumx dec_exp dec_ph rw_ops ar_done hat_tr hat_ev gram_mm gram_ev lt_tr
lt_ev n_ev x0_ev lt_sub mv_mm mv_ev sq_mm sq_ev inv_mm inv_ev xb_ev nw_p nw_e nw_t nw_c nw_x st_tr st_ev
st_scaled x_mm x_ev u_mm u_ev s_mm s_ev so_tr y_mm gn_mean_mm gn_cent gn_sq gn_sum gn_ms gn_pow bon_mm gn_mm
gn_used wo_mm wo_ev post_sq post_tmp post_x ff_th ff_g ff_yev rt_mm rt_max rt_exp rt_gate rt_cum rt_rank htok_tr
htok_ev sel_dve selt_tr selt_ev gat_mm gat_ev eh_th eh_g ey_ev comb_mm comb_ev x_hi x_lo w_hi w_lo gat_lo
eh_hi eh_lo ey_lo act_step dve_step pe_phase act_phase dve_phase pool_phase results_out""".split()


class Signals:

    def __init__(self, name, sem):
        self.name, self.sem, self.count, self.last = name, sem, {}, None

    def sig(self, what):
        self.count[what] = self.count.get(what, 0) + 1
        self.last = (self.sem[what], self.count[what])
        return self.sem[what], 1

    def own_last(self):
        return self.last


def aligned(at):
    return (at + 31) // 32 * 32


def build(nc, blocks, x_all, small, cond, sinkrows, router, low2, cache_k, cache_v, state, consts,
          y_all, new_k, new_v, new_state):
    ctx = ExitStack()
    with ctx:
        def sb(name, shape, dt=F32):
            return ctx.enter_context(nc.sbuf_tensor(name, shape, dt))

        con = sb("con", [P, NCON])
        par = sb("par", [P, DEPTH * NPAR])
        condT = sb("condT", [P, KC, 2])
        sink = sb("sink", [P, DEPTH * NH])
        rout = sb("rout", [P, KC, NE])
        w2 = sb("w2", [P, 3, 512])
        ring_at = aligned(nc.sbuf_base)
        ring = sb("ring", [P, RING, D])
        ring_lo = nc.alloc_sbuf_tensor_at("ring_lo", [P, RING, D], F32R, offset=ring_at)
        x = sb("x", [P, NT, D])
        mod = sb("mod", [P, DEPTH, 48, 2])
        modrow = sb("modrow", [2, 512])
        gpre = sb("gpre", [P, 2, 8, 2])
        gpost = sb("gpost", [P, 2, 8, 2])
        hpar = sb("hpar", [P, 64])
        st_in = sb("st_in", [64, 2, RH, HD])
        st_out = sb("st_out", [P, 2, NPAIR, HD])
        identb = sb("identb", [P, P], BF16)
        rw_s = sb("rw_s", [P, 4, NT, RH])
        ck = sb("ck", [P, 2, P])
        cv = sb("cv", [P, 2, P])
        tiny = sb("tiny", [P, 128])
        arena_at = aligned(nc.sbuf_base)
        arena = sb("arena", [P, ARENA])
        ps = ctx.enter_context(nc.psum_tensor("ps", [P, 8, 512], F32))
        sem = {n: ctx.enter_context(nc.semaphore(n)) for n in SEMS}
        ring_sem = [ctx.enter_context(nc.semaphore(f"block_in{i}")) for i in range(RING)]

        def C(name, rows=P):
            at, w = CON[name]
            return con[0:rows, at:at + w]

        def PR(l, name, j=None, n=1):
            at, w = PAR[name]
            at += l * NPAR
            return par[:, at:at + w] if j is None else par[:, at + j:at + j + n]

        ident = C("ident")

        cursor = [0]

        def take_r(name, n, **dims):
            cursor[0] = (cursor[0] + 7) // 8 * 8
            a = nc.alloc_sbuf_tensor_at(name, [P, n], F32R, offset=arena_at + 4 * cursor[0])[:, :]
            take(n)
            names = list(dims)
            return a.rearrange(f"p ({' '.join(names)}) -> p {' '.join(names)}", **{k: dims[k] for k in names[:-1]})

        def take(n, **dims):
            a = arena[:, cursor[0]:cursor[0] + n]
            cursor[0] += n
            assert cursor[0] <= ARENA, cursor[0]
            if not dims:
                return a
            names = list(dims)
            return a.rearrange(f"p ({' '.join(names)}) -> p {' '.join(names)}", **{k: dims[k] for k in names[:-1]})

        rkv = take(12 * T, c=12, t=T)
        zlow = take(3 * T, c=3, t=T)
        O_AT = cursor[0]
        oT = take(8 * T, c=8, t=T)
        cursor[0] = O_AT
        oT_lo = take_r("oT_lo", 8 * T, c=8, t=T)
        MIX_END = cursor[0]
        hT = take(KC * T, c=KC, t=T)
        cursor[0] = MIX_END
        hT_lo = take_r("hT_lo", KC * T, c=KC, t=T)
        cursor[0] = O_AT
        hT_hi = take_r("hT_hi", KC * T, c=KC, t=T)
        cursor[0] = MIX_END
        oT_hi = take_r("oT_hi", 8 * T, c=8, t=T)
        ATT_AT = cursor[0]
        qT = take(4 * T, c=4, t=T)
        kT = take(T)
        vtok = take(NT * P, i=NT, c=P)
        kctok = take(P)
        kcT = take(PAST)
        SCR_AT = cursor[0]
        xn = take(NT * D, i=NT, d=D)
        cursor[0] = SCR_AT
        praw = take(2 * 643, b=2, t=643)
        pshift = take(2 * T, b=2, t=T)
        w_proj = take_r("w_proj", 2 * D, b=2, d=D)
        vT = take(T)
        cursor[0] = SCR_AT
        prob = take(3 * 640, b=3, k=640)
        probT = take(2 * 640, b=2, k=640)
        ropetmp = take(2 * 512, b=2, k=512)
        cursor[0] = MIX_END
        kk = take(T)
        kds = take(T)
        vt_rw = take(NT * P, i=NT, c=P)
        ar = take(NT * 2 * P, i=NT, a=2, t=P)
        bkbar = take(2 * T, a=2, t=T)
        bktok = take(NT * 2 * P, i=NT, a=2, c=P)
        mv = take(NT * P, i=NT, v=P)
        xb = take(2 * P, b=2, v=P)
        st = take(2 * P, b=2, v=P)
        stpc = take(P)
        LG_AT = cursor[0]
        gm = take(10 * 4 * P, u=10, a=4, t=P)
        lfi = take(10 * P, u=10, t=P)
        nb = take(10 * P, u=10, t=P).bitcast(BF16).rearrange("p u (a t) -> p u a t", a=2)
        xq = take(5 * P).bitcast(BF16).rearrange("p (u t) -> p u t", u=10)
        gmb = gm.bitcast(BF16)
        over = bkbar.rearrange("p a t -> p (a t)")
        ub = over[:, 0:T].rearrange("p (i v) -> p i v", i=NT)
        s0s = over[:, T:2 * T].rearrange("p (i v) -> p i v", i=NT)
        cursor[0] = LG_AT
        tw = take(T)
        ta = take(T)
        lw = take(T)
        cumc = take(T)
        cumx = take(T)
        e_in = take(T)
        e_inv = take(T)
        e_ex = take(T)
        avec = take(T)
        kdt = take(T)
        spr = take(2 * T, b=2, t=T)
        cursor[0] = LG_AT
        sq4 = take(4 * T, c=4, t=T)
        bon = take(2 * T, c=2, t=T)
        assert cursor[0] <= LG_AT + 10 * T
        cursor[0] = 0
        w_wo = take_r("w_wo", WO_B * D, b=WO_B, d=D)
        assert cursor[0] <= O_AT
        cursor[0] = 0
        gT = take(FT * T, f=FT, t=T)
        cursor[0] = ATT_AT
        fo = take(NT * D, i=NT, d=D)
        ftmp = take(2 * T, b=2, t=T)
        w_ffn = take_r("w_ffn", 3 * D, b=3, d=D)
        cursor[0] = ATT_AT
        hT_ffn_hi = take_r("hT_ffn_hi", KC * T, c=KC, t=T)
        cursor[0] = 0
        htok = take(NT * D, i=NT, d=D)
        cursor[0] = 0
        htok_lo = take_r("htok_lo", NT * D, i=NT, d=D)
        HG_AT = cursor[0]
        hg_hi = take_r("hg_hi", KC * CAP, c=KC, s=CAP)
        hg_lo = take_r("hg_lo", KC * CAP, c=KC, s=CAP)
        cursor[0] = HG_AT
        ye_hi = take_r("ye_hi", 2 * D, s=2, d=D)
        ye_lo = take_r("ye_lo", 2 * D, s=2, d=D)
        ge_hi = take_r("ge_hi", 2 * CAP, f=2, s=CAP)
        ge_lo = take_r("ge_lo", 2 * CAP, f=2, s=CAP)
        sel = take_r("sel", NT * CAP, i=NT, s=CAP)
        selT = take_r("selT", 2 * T, s=2, t=T)
        sel_f = take(NT * CAP, i=NT, s=CAP)
        assert cursor[0] <= MIX_END, cursor[0]
        cursor[0] = MIX_END
        htok_hi = take_r("htok_hi", NT * D, i=NT, d=D)
        lg = tiny[:, 0:40].rearrange("p (i e) -> p i e", i=NT)
        rk = tiny[:, 40:80].rearrange("p (i e) -> p i e", i=NT)
        gate = tiny[:, 80:120].rearrange("p (i e) -> p i e", i=NT)
        small2 = sb("small2", [P, 256])
        flag_i = sb("flag_i", [1, 8], I32)
        m8 = small2[:, 0:40].rearrange("p (i e) -> p i e", i=NT)
        msk = small2[:, 40:80].rearrange("p (i e) -> p i e", i=NT)
        nstat = small2[:, 80:100]
        pstat = small2[:, 200:220]
        phs = small2[:, 100:110].rearrange("p (a i) -> p a i", a=2)
        attst = small2[:, 110:150].rearrange("p (b a) -> p b a", b=4)
        rstat = small2[:, 150:200]

        def pair(n):
            return ps[:, 2 * n:2 * n + 2, :].rearrange("p b c -> p (b c)")

        def pair640(n):
            return pair(n)[:, 384:1024]

        def pair_r(n):
            return pair(n)[:, 192:832]

        def mm_split(nc, dst, w_hi, w_lo, m_hi, m_lo, start, stop):
            nc.tensor.matmul(dst, w_hi, m_hi, start=start, stop=False)
            nc.tensor.matmul(dst, w_hi, m_lo, start=False, stop=False)
            return nc.tensor.matmul(dst, w_lo, m_hi, start=False, stop=stop)

        def mm640_split(nc, n, w_hi, w_lo, h_hi, h_lo, start, stop):
            for h in range(2):
                sl = slice(320 * h, 320 * h + 320)
                mm = mm_split(nc, pair_r(n)[:, sl], w_hi, w_lo, h_hi[:, sl], h_lo[:, sl], start, stop)
            return mm

        def mm640(nc, n, lhsT, rhs, start, stop, rows=P):
            nc.tensor.matmul(pair(n)[0:rows, 384:512], lhsT, rhs[:, 0:CTX], start=start, stop=stop)
            return nc.tensor.matmul(pair(n)[0:rows, 512:1024], lhsT, rhs[:, CTX:T], start=start, stop=stop)

        def MOE_SP(sp):
            sp.wait_ge(sem["rt_rank"], 2)

            def body():
                for m in range(2 * NE * EXP_B):
                    n = N_BLOCKS + m
                    sp.wait_ge(sem["block_used"], n - RING + 1)
                    sp.dma_start(ring[:, n % RING, :], blocks[MOE_FIRST + m % (NE * EXP_B)]).then_inc(ring_sem[n % RING], 16)
            with_flag(sp, body)

        def with_flag(eng, body):
            r = eng.value_load(flag_i[0:1, 0:1], min_val=0, max_val=T)
            with eng.If(r > CAP):
                body()

        def unit(u):
            return (u // 2) % 4, u % 2, u // 8 - 1

        N_UNITS = NH * NT

        def order(d):
            return [0] + (list(range(1, NT)) if d == 0 else list(range(NT - 1, 0, -1)))

        def diag(n):
            return diags[:, n % 4, :]

        diags = arena[:, ARENA - 512:ARENA].rearrange("p (n t) -> p n t", n=4)

        def up_done(f):
            return 2 * (f + 1) + max(0, f - 1)

        def mod_blocks_done(m):
            return 4 * (m + 1) + (0 if m < MOD_FIRST else PROJ_B if m < MOD_MID else 2 * PROJ_B + WO_B + DENSE_B)

        def mod_group(g, j):
            if g < (MOD_MID - MOD_FIRST) // 2:
                return MOD_FIRST + 2 * g + j
            g -= 2 * NPAIR
            return MOD_MID + 2 * g + j if 0 <= g < (2 * MOD_G - MOD_MID) // 2 else None

        def ahead(f):
            def at_w13(g, w):
                return 2 * g + w + max(0, g - 1)
            first = [at_w13(f + 1, 1)] if f + 1 < FE else []
            then = [at_w13(f + 1, 1) + 1 if f + 1 < FE else EXP_B - 1]
            if f + 2 < FE:
                then.append(at_w13(f + 2, 0))
            return first, then

        LAST_PASS = (NE - 1, 3 * NE - 1)
        X_PROJ = [0, 3 * KC]
        X_FFN = [2 * KC, 5 * KC]

        def n_keys(blkq):
            return P if blkq < 0 else PAST + P * (3 if 0 < blkq < 3 else 2)

        def sq_scratch(i):
            return arena[:, MIX_END + i * D:MIX_END + (i + 1) * D]

        block = ctx.enter_context(nc.Block())

        @block.sync
        def _(sp):
            sp.dma_start(con[:, :], consts).then_inc(sem["consts_in"], 16)
            sp.dma_start(par[:, :], small).then_inc(sem["cond_in"], 16)
            sp.dma_start(condT[:, :, :], cond).then_inc(sem["cond_in"], 16)
            sp.dma_start(sink[:, :], sinkrows).then_inc(sem["cond_in"], 16)
            sp.dma_start(rout[:, :, :], router).then_inc(sem["cond_in"], 16)
            for n in range(N_BLOCKS):
                if n >= RING:
                    sp.wait_ge(sem["block_used"], n - RING + 1)
                sp.dma_start(ring[:, n % RING, :], blocks[n]).then_inc(ring_sem[n % RING], 16)
                if n == 3:
                    sp.dma_start(x[:, :, :], x_all.rearrange("(i p) d -> p i d", p=P)).then_inc(sem["x_in"], 16)
            MOE_SP(sp)

        @block.tensor
        def _(pe):
            E = Signals("pe", sem)
            phase = [0]

            def next_phase():
                phase[0] += 1
                pe.drain().then_inc(sem["pe_phase"], 1)
                pe.wait_ge(sem["pe_phase"], phase[0])
                pe.wait_ge(sem["act_phase"], phase[0])
                pe.wait_ge(sem["dve_phase"], phase[0])
                pe.wait_ge(sem["pool_phase"], phase[0])

            used = [0]

            def blk():
                n = used[0]
                pe.wait_ge(ring_sem[n % RING], 16 * (n // RING + 1))
                return ring[:, n % RING, :]

            split = [0]

            def split_blk(high):
                n = used[0]
                split[0] += 1
                pe.wait_ge(sem["w_lo"], split[0])
                return high[:, n % high.shape[1], :], ring_lo[:, n % RING, :]

            def done(mm):
                mm.then_inc(sem["block_used"], 1)
                used[0] += 1

            def mod_block(q, bank):
                b = blk()
                for j in range(2):
                    kc = 2 * q + j
                    mm = nc.tensor.matmul(ps[0:2, bank, :], condT[:, kc, :], b[:, j * 512:(j + 1) * 512], start=kc == 0, stop=kc == KC - 1)
                mm.then_inc(sem["block_used"], 1)
                used[0] += 1

            def mod_turn(m, bank):
                pe.wait_ge(sem["mod_row"], m + 1)
                for j in range(4):
                    mm = nc.tensor.transpose(ps[:, bank, 2 * j:2 * j + 2], modrow[0:2, j * P:(j + 1) * P], ident[0:2, 0:2])
                mm.then_inc(sem["mod_tr"], 1)

            def mod_phase():
                pe.wait_ge(sem["consts_in"], 16)
                pe.wait_ge(sem["silu_c"], 1)
                for m in range(MOD_FIRST + 1):
                    if m < MOD_FIRST:
                        for q in range(4):
                            mod_block(q, m)
                    if m >= 1:
                        mod_turn(m - 1, m - 1)

            def mod_slot(g, s):
                if mod_group(g, 1) is not None and s in (0, 3, 6, 9):
                    mod_block(s // 3, 7)
                if mod_group(g, 1) is not None and s == 12:
                    mod_turn(mod_group(g, 1), 7)

            def norm_phase(k):
                for kc in range(KC):
                    if kc == 0:
                        pe.wait_ge(sem["norm_x"], NT * (k + 1))
                    if kc >= 4:
                        pe.wait_ge(sem["norm_ev_act"], KC * k + kc - 3)
                        pe.wait_ge(sem["norm_ev_dve"], KC * k + kc - 3)
                    for i in range(NT):
                        mm = nc.tensor.transpose(pair640(kc % 4)[:, i * P:(i + 1) * P], xn[:, i, kc * P:(kc + 1) * P], ident)
                    mm.then_inc(sem["norm_tr"], 1)

            def proj_phase(l):
                for o in range(PROJ_B):
                    w_h, w_l = split_blk(w_proj)
                    n = l * PROJ_B + o
                    if o >= 4:
                        pe.wait_ge(sem["proj_ev_act"], n - 3)
                    if 6 <= o - 4 < 18:
                        pe.wait_ge(sem["proj_ev_dve"], 13 * l + o - 9)
                    for kc in range(KC):
                        k = slice(kc * P, (kc + 1) * P)
                        if o == 0:
                            pe.wait_ge(sem["x_lo"], X_PROJ[l] + kc + 1)
                        mm = mm640_split(nc, o % 4, w_h[:, k], w_l[:, k], hT_hi[:, kc, :], hT_lo[:, kc, :], kc == 0, kc == KC - 1)
                    done(mm)

            def att_phase(l):
                for c in range(5):
                    src = qT[:, c, CTX:T] if c < 4 else kT[:, CTX:T]
                    mm = nc.tensor.matmul(ps[:, c, :], C("rot"), src, start=True, stop=True)
                    mm.then_inc(sem["rope_mm"], 1)
                pe.wait_ge(sem["misc_in"], 16 * 5 * (l + 1))
                for i in range(2):
                    mm = nc.tensor.transpose(ps[:, 5, i * P:(i + 1) * P], ck[:, i, :], ident)
                nc.tensor.transpose(ps[:, 5, PAST:PAST + P], kT[:, 0:CTX], ident)
                for i in range(NT):
                    mm = nc.tensor.transpose(pair640(3)[:, i * P:(i + 1) * P], vT[:, i * P:(i + 1) * P], ident)
                mm.then_inc(sem["kc_tr"], 1)
                pe.wait_ge(sem["rope_ev"], 5 * (l + 1))
                pe.wait_ge(sem["kc_ev"], l + 1)

                def keys(u):
                    c, g, blkq = unit(u)
                    rows = slice(64 * g, 64 * g + 64)
                    own = [(kT[rows, 0:P], vtok[:, 0, rows], None)]
                    if blkq < 0:
                        return own
                    out = [(kcT[rows, i * P:(i + 1) * P], cv[:, i, rows], None) for i in range(2)]
                    for d, m in ((0, None), (-1, "m_prev"), (1, "m_next")):
                        b = blkq + d
                        if 0 <= b < 4:
                            out.append((kT[rows, CTX + b * P:CTX + (b + 1) * P], vtok[:, 1 + b, rows], m))
                    return out

                for t in range(N_UNITS + 3):
                    if t < N_UNITS:
                        c, g, blkq = unit(t)
                        rows = slice(64 * g, 64 * g + 64)
                        un = l * N_UNITS + t
                        if t >= 2:
                            pe.wait_ge(sem["att_exp"], un - 1)
                        q = qT[rows, c, (blkq + 1) * P:(blkq + 2) * P]
                        for j, (kop, _, m) in enumerate(keys(t)):
                            dst = pair(t % 2)[:, j * P:(j + 1) * P]
                            mm = nc.tensor.matmul(dst, q, kop, start=True, stop=m is None)
                            if m:
                                mm = nc.tensor.matmul(dst, ident, C(m), start=False, stop=True)
                        mm.then_inc(sem["att_s"], 1)
                    if 2 <= t <= N_UNITS + 1:
                        u = t - 2
                        un = l * N_UNITS + u
                        pe.wait_ge(sem["att_p"], un + 1)
                        if u >= 1:
                            pe.wait_ge(sem["att_trev"], un)
                        for j in range(len(keys(u))):
                            mm = nc.tensor.transpose(pair(2)[:, j * P:(j + 1) * P], prob[:, u % 3, j * P:(j + 1) * P], ident)
                        mm.then_inc(sem["att_tr"], 1)
                    if t >= 3:
                        u = t - 3
                        c, g, blkq = unit(u)
                        rows = slice(64 * g, 64 * g + 64)
                        un = l * N_UNITS + u
                        pe.wait_ge(sem["att_trev"], un + 1)
                        if g == 0 and u >= 4:
                            pe.wait_ge(sem["att_oev"], (l * N_UNITS + u) // 2 - 1)
                        ks = keys(u)
                        for j, (_, vop, _) in enumerate(ks):
                            mm = nc.tensor.matmul(ps[rows, 6 + (u // 2) % 2, 0:P], vop, probT[:, u % 2, j * P:(j + 1) * P],
                                                  start=j == 0, stop=j == len(ks) - 1)
                        mm.then_inc(sem["att_o"], 1)

            def keep_clock(bank, n):
                for _ in range(n):
                    nc.tensor.matmul(ps[:, bank, :], ident, C("cos"), start=True, stop=True)

            def kk_phase(l):
                for c in range(NPAIR):
                    pe.wait_ge(sem["kk_prod"], l * NPAIR + c + 1)
                    for i in range(NT):
                        mm = nc.tensor.matmul(ps[:, 0, i * RH + 2 * c:i * RH + 2 * c + 2], sq4[:, c, i * P:(i + 1) * P], C("head_sel"),
                                              start=True, stop=True)
                mm.then_inc(sem["kk_sum"], 1)

            def spread(dst, b):
                for i in range(NT):
                    mm = nc.tensor.transpose(dst[:, i * P:(i + 1) * P], spr[:, b, i * P:(i + 1) * P], ident)
                return mm

            def rwkv_dir(l, c, d):
                g = (l * NPAIR + c) * 2 + d
                k = l * NPAIR + c
                rows = slice(64 * d, 64 * d + 64)
                mm640(nc, 0, w2[rows, 0, c * P:(c + 1) * P], zlow[rows, 0, :], True, True)
                mm640(nc, 1, w2[rows, 1, c * P:(c + 1) * P], zlow[rows, 1, :], True, True).then_inc(sem["low_mm"], 1)
                nc.tensor.transpose(ps[:, 4, 0:64], st_in[:, d, 2 * c:2 * c + 2, :].rearrange("v h k -> v (h k)"),
                                    ident[0:64, 0:64]).then_inc(sem["st_tr"], 1)
                if d == 0:
                    pe.wait_ge(sem["spread_ev"], 12 * l + c + 1)
                    spread(pair640(2), 0).then_inc(sem["kk_mm"], 1)
                    for i in range(NT):
                        mm = nc.tensor.transpose(pair640(3)[:, i * P:(i + 1) * P], rkv[:, 8 + c, i * P:(i + 1) * P], ident)
                    mm.then_inc(sem["vt_tr"], 1)
                    pe.wait_ge(sem["kk_done"], k + 1)
                    pe.wait_ge(sem["vt_ev"], k + 1)
                mod_early = mod_group(g, 0) is not None
                if mod_early:
                    pe.wait_ge(sem["low_ev"], g + 1)
                    for q in range(4):
                        mod_block(q, 2)
                else:
                    keep_clock(7, 5 if d == 0 else 7)
                pe.wait_ge(sem["rw_ops"], g + 1)
                for a in range(2):
                    for i in range(NT):
                        mm = nc.tensor.transpose(pair640(2 + a)[:, i * P:(i + 1) * P], bkbar[:, a, i * P:(i + 1) * P], ident)
                    mm.then_inc(sem["hat_tr"], 1)
                if mod_early:
                    mod_turn(mod_group(g, 0), 2)
                    pe.wait_ge(sem["mod_ev"], mod_group(g, 0) + 1)
                pe.wait_ge(sem["st_ev"], g + 1)
                pe.wait_ge(sem["ar_done"], g + 1)
                for u in range(10):
                    i, hh = u // 2, u % 2
                    h = slice(64 * hh, 64 * hh + 64)
                    if u == 4:
                        pe.wait_ge(sem["hat_ev"], 2 * (g + 1))
                    if u >= 8:
                        pe.wait_ge(sem["gram_ev"], 10 * g + u - 7)
                    arr = ar[h, i, :, :].rearrange("p a t -> p (a t)")
                    nc.tensor.matmul(ps[:, u % 8, 0:256], bkbar[h, 0, i * P:(i + 1) * P], arr, start=True, stop=True)
                    nc.tensor.matmul(ps[:, u % 8, 256:512], bkbar[h, 1, i * P:(i + 1) * P], arr, start=True, stop=True).then_inc(sem["gram_mm"], 1)
                for i in range(NT):
                    pe.wait_ge(sem["gram_ev"], 10 * g + 10)
                    if i >= 4:
                        pe.wait_ge(sem["lt_ev"], 5 * g + i - 3)
                        pe.wait_ge(sem["mv_ev"], 5 * g + i - 3)
                    for hh in range(2):
                        mm = nc.tensor.transpose(ps[:, i % 4, hh * P:(hh + 1) * P], gm[:, 2 * i + hh, 0, :], ident)
                    mm.then_inc(sem["lt_tr"], 1)
                    for hh in range(2):
                        mm = nc.tensor.matmul(ps[:, 4 + i % 4, P * hh:P * hh + P], gm[:, 2 * i + hh, 2, :], vt_rw[:, i, :],
                                              start=True, stop=True)
                    mm.then_inc(sem["mv_mm"], 1)
                for j in range(1, 8):
                    for i in range(NT):
                        n = 5 * (j - 1) + i
                        if j == 1:
                            pe.wait_ge(sem["lt_ev"], 5 * g + i + 1)
                            pe.wait_ge(sem["n_ev"], 5 * g + i + 1)
                            if i == 0:
                                pe.wait_ge(sem["lt_ev"], 5 * g + 5)
                                pe.wait_ge(sem["mv_ev"], 5 * g + 5)
                        else:
                            pe.wait_ge(sem["sq_ev"], 30 * g + n - 4)
                        if j <= 6:
                            if n >= 4:
                                pe.wait_ge(sem["sq_ev"], 30 * g + n - 3)
                            for hh in range(2):
                                u = 2 * i + hh
                                if j < 6:
                                    nc.tensor.matmul(ps[:, n % 4, 256 * hh:256 * hh + P], nb[:, u, 1, :], nb[:, u, 0, :], start=True, stop=True)
                                mm = nc.tensor.matmul(ps[:, n % 4, 256 * hh + P:256 * hh + 256], nb[:, u, 0, :], nb[:, u, 1, :], start=True, stop=True)
                            mm.then_inc(sem["sq_mm"], 1)
                        if j >= 2:
                            m = n - 5
                            if j == 2:
                                pe.wait_ge(sem["x0_ev"], 5 * g + i + 1)
                            else:
                                pe.wait_ge(sem["inv_ev"], 30 * g + m - 4)
                            if m >= 4:
                                pe.wait_ge(sem["inv_ev"], 30 * g + m - 3)
                            for hh in range(2):
                                u = 2 * i + hh
                                mm = nc.tensor.matmul(ps[:, 4 + m % 4, hh * P:(hh + 1) * P], nb[:, u, 1, :], xq[:, u, :], start=True, stop=True)
                            mm.then_inc(sem["inv_mm"], 1)
                pe.wait_ge(sem["inv_ev"], 30 * g + 30)
                for q in range(2):
                    for i in range(NT):
                        n = (2 * g + q) * NT + i
                        if q == 0:
                            pe.wait_ge(sem["xb_ev"], 5 * g + i + 1)
                        else:
                            pe.wait_ge(sem["nw_x"], n - 4)
                        if i >= 4:
                            pe.wait_ge(sem["nw_e"], n - 3)
                            if q == 0:
                                pe.wait_ge(sem["nw_t"], 5 * g + i - 3)
                        for hh in range(2):
                            u = 2 * i + hh
                            mm = nc.tensor.matmul(ps[:, i % 4, hh * P:(hh + 1) * P], lfi[:, u, :], gm[:, u, 0, :], start=True, stop=True)
                        if q == 0:
                            for hh in range(2):
                                u = 2 * i + hh
                                mm = nc.tensor.matmul(ps[:, 4 + i % 4, hh * P:(hh + 1) * P], xq[:, u, :], identb[:, :], start=True, stop=True)
                        mm.then_inc(sem["nw_p"], 1)
                    pe.wait_ge(sem["nw_t"], 5 * g + 5)
                    for i in range(NT):
                        n = (2 * g + q) * NT + i
                        pe.wait_ge(sem["nw_e"], n + 1)
                        if i >= 4:
                            pe.wait_ge(sem["nw_x"], n - 3)
                        for hh in range(2):
                            u = 2 * i + hh
                            mm = nc.tensor.matmul(ps[:, 4 + i % 4, hh * P:(hh + 1) * P], gmb[:, u, 2, P:2 * P], gmb[:, u, 2, 0:P],
                                                  start=True, stop=True)
                        mm.then_inc(sem["nw_c"], 1)
                pe.wait_ge(sem["nw_x"], 10 * (g + 1))
                def tile_out(i):
                    dst = pair640(2)[:, i * P:(i + 1) * P]
                    nc.tensor.matmul(dst, s0s[:, i, :], ar[:, i, 1, :], start=True, stop=False, skip_group_check=True)
                    for hh in range(2):
                        h = slice(64 * hh, 64 * hh + 64)
                        u = 2 * i + hh
                        nc.tensor.matmul(dst[h, :], ub[:, i, h], gm[:, u, 1, :], start=False, stop=False, skip_group_check=True)
                        mm = nc.tensor.matmul(dst[h, :], vt_rw[:, i, h], gm[:, u, 3, :], start=False, stop=True, skip_group_check=True)
                    return mm

                for n, i in enumerate(order(d)):
                    k5 = 5 * g + n
                    pe.wait_ge(sem["st_scaled"], k5 + 1)
                    nc.tensor.matmul(ps[:, 0, 0:P], ar[:, i, 0, :], s0s[:, i, :], start=True, stop=True).then_inc(sem["x_mm"], 1)
                    mod_slot(g, 3 * n)
                    pe.wait_ge(sem["x_ev"], k5 + 1)
                    for hh in range(2):
                        mm = nc.tensor.matmul(ps[:, 1, P * hh:P * hh + P], gm[:, 2 * i + hh, 0, :], xb[:, n % 2, :], start=True, stop=True)
                    mm.then_inc(sem["u_mm"], 1)
                    pe.wait_ge(sem["u_ev"], k5 + 1)
                    if n == NT - 1:
                        break
                    nc.tensor.matmul(ps[:, 2, 0:P], bktok[:, i, 0, :], ub[:, i, :], start=True, stop=False)
                    nc.tensor.matmul(ps[:, 2, 0:P], bktok[:, i, 1, :], vt_rw[:, i, :], start=False, stop=True).then_inc(sem["s_mm"], 1)
                    tile_out(i)
                    pe.wait_ge(sem["s_ev"], 4 * g + n + 1)
                    if n == 0:
                        nc.tensor.transpose(ps[:, 3, 0:P], st[:, 0, :], ident).then_inc(sem["so_tr"], 1)
                mm = tile_out(order(d)[-1])
                mm.then_inc(sem["y_mm"], 1)
                if d == 1:
                    for i in range(NT):
                        mm = nc.tensor.matmul(ps[:, 0, 2 * i:2 * i + 2], kds[:, i * P:(i + 1) * P], C("head_sel"), start=True, stop=True)
                    mm.then_inc(sem["bon_mm"], 1)
                next_phase()

            def gn_phase(l):
                for c in range(NPAIR):
                    mm640(nc, c, C("head_mean"), oT[:, 4 + c, :], True, True).then_inc(sem["gn_mean_mm"], 1)
                pe.wait_ge(sem["gn_cent"], NPAIR * (l + 1))
                for c in range(NPAIR):
                    pe.wait_ge(sem["gn_sq"], l * NPAIR + c + 1)
                    for i in range(NT):
                        mm = nc.tensor.matmul(ps[:, 0, i * RH + 2 * c:i * RH + 2 * c + 2], sq4[:, c, i * P:(i + 1) * P], C("head_sel"),
                                              start=True, stop=True)
                mm.then_inc(sem["gn_sum"], 1)
                for c in range(NPAIR):
                    for w in range(3):
                        n = 3 * c + w
                        if n == 0:
                            pe.wait_ge(sem["gn_pow"], l + 1)
                        if n >= 4:
                            pe.wait_ge(sem["gn_used"], 12 * l + n - 3)
                        dst = pair640((n + 1) % 4)
                        if w == 0:
                            pe.wait_ge(sem["spread_ev"], 12 * l + 4 + 2 * c + 1)
                            mm = spread(dst, 0)
                        elif w == 2:
                            mm = mm640(nc, (n + 1) % 4, w2[:, 2, c * P:(c + 1) * P], zlow[:, 2, :], True, True)
                        else:
                            pe.wait_ge(sem["spread_ev"], 12 * l + 4 + 2 * c + 2)
                            mm = spread(dst, 1)
                        mm.then_inc(sem["gn_mm"], 1)
                next_phase()

            def wo_phase(l):
                first = used[0]
                for i in range(NT):
                    if i >= 4:
                        pe.wait_ge(sem["wo_ev"], l * NT + i - 3)
                    for fc in range(WO_B):
                        n = first + fc
                        if i == 0:
                            pe.wait_ge(sem["w_lo"], split[0] + fc + 1)
                        tok = slice(i * P, (i + 1) * P)
                        for h in range(2):
                            half = slice(h * 512, (h + 1) * 512)
                            mm = mm_split(nc, pair(i % 4)[:, half], oT_hi[:, fc, tok], oT_lo[:, fc, tok], w_wo[:, fc, half],
                                          ring_lo[:, n % RING, half], fc == 0, fc == WO_B - 1)
                        if i == NT - 1:
                            done(mm)
                    if i < NT - 1:
                        mm.then_inc(sem["wo_mm"], 1)
                split[0] += WO_B

            def rowvec(k):
                for n in range(16):
                    g, kc = n // 8, n % 8
                    pe.wait_ge(sem["rowvec_diag"], 16 * k + n + 1)
                    nc.tensor.matmul(pair(g)[:, kc * P:(kc + 1) * P], C("ones"), diag(n),
                                           start=True, stop=True).then_inc(sem["rowvec_mm"], 1)

            def dense_phase(l):
                for f in range(FT):
                    for w in range(2):
                        w_h, w_l = split_blk(w_ffn)
                        n = 2 * f + w
                        if n >= 4:
                            pe.wait_ge(sem["ff_g"], f - 1)
                        for kc in range(KC):
                            k = slice(kc * P, (kc + 1) * P)
                            if n == 0:
                                pe.wait_ge(sem["x_lo"], X_FFN[l] + kc + 1)
                            mm = mm640_split(nc, n % 4, w_h[:, k], w_l[:, k], hT_ffn_hi[:, kc, :], hT_lo[:, kc, :], kc == 0, kc == KC - 1)
                        done(mm)
                for h in range(2):
                    for j in range(FT // 2):
                        b = blk()
                        for s in range(2):
                            f = 2 * j + s
                            if h == 0 and j == 0 and s == 0:
                                pe.wait_ge(sem["ff_g"], FT)
                            for i in range(NT):
                                if h == 1 and f == 0:
                                    pe.wait_ge(sem["ff_yev"], max(1, i - 2))
                                mm = nc.tensor.matmul(ps[:, (5 * h + i) % 8, :], gT[:, f, i * P:(i + 1) * P],
                                                      b[:, s * 512:(s + 1) * 512], start=f == 0, stop=f == FT - 1)
                        mm.then_inc(sem["block_used"], 1)
                        used[0] += 1

            def route_phase():
                for i in range(NT):
                    for kc in range(KC):
                        mm = nc.tensor.matmul(ps[:, 0, i * NE:(i + 1) * NE], hT[:, kc, i * P:(i + 1) * P], rout[:, kc, :],
                                              start=kc == 0, stop=kc == KC - 1)
                mm.then_inc(sem["rt_mm"], 1)
                for i in range(NT):
                    if i >= 3:
                        pe.wait_ge(sem["htok_ev"], i - 2)
                    for kc in range(KC):
                        mm = nc.tensor.transpose(pair(1 + i % 3)[:, kc * P:(kc + 1) * P], hT[:, kc, i * P:(i + 1) * P], ident)
                    mm.then_inc(sem["htok_tr"], 1)
                pe.wait_ge(sem["rt_gate"], 1)
                for i in range(NT + 1):
                    dst = ps[:, 1, i * NE:(i + 1) * NE]
                    for j in range(min(i, NT - 1) + 1):
                        last = j == min(i, NT - 1)
                        w = C("before") if last and i < NT else C("ones")
                        mm = nc.tensor.matmul(dst, w, msk[:, j, :], start=j == 0, stop=last)
                mm.then_inc(sem["rt_cum"], 1)

            def moe_pass(k):
                pe.wait_ge(sem["sel_dve"], k + 1)
                if k == 0:
                    pe.wait_ge(sem["x_lo"], X_FFN[1] + NT)
                for kc in range(KC):
                    b = 4 + kc % 2
                    if kc >= 2:
                        pe.wait_ge(sem["gat_lo"], KC * k + kc - 1)
                    for i in range(NT):
                        ch = slice(kc * P, (kc + 1) * P)
                        nc.tensor.matmul(ps[:, b, 0:CAP], htok_hi[:, i, ch], sel[:, i, :], start=i == 0, stop=False)
                        mm = nc.tensor.matmul(ps[:, b, 0:CAP], htok_lo[:, i, ch], sel[:, i, :], start=False, stop=i == NT - 1)
                    mm.then_inc(sem["gat_mm"], 1)
                if k >= 1:
                    pe.wait_ge(sem["comb_ev"], 10 * k)
                for s in range(2):
                    if s == 1:
                        pe.wait_ge(sem["selt_ev"], 2 * k + 1)
                    for i in range(NT):
                        mm = nc.tensor.transpose(pair640(3)[:, i * P:(i + 1) * P], sel_f[:, i, s * P:(s + 1) * P], ident)
                    mm.then_inc(sem["selt_tr"], 1)
                pe.wait_ge(sem["gat_lo"], KC * (k + 1))
                for f in range(FE + 1):
                    if f < FE:
                        if f >= 2:
                            pe.wait_ge(sem["eh_lo"], FE * k + f - 1)
                        for w in range(2):
                            w_h, w_l = split_blk(w_ffn)
                            for kc in range(KC):
                                c = slice(kc * P, (kc + 1) * P)
                                mm = mm_split(nc, ps[:, 4 + f % 2, w * CAP:(w + 1) * CAP], w_h[:, c], w_l[:, c], hg_hi[:, kc, :],
                                              hg_lo[:, kc, :], kc == 0, kc == KC - 1)
                            done(mm)
                    if f >= 1:
                        g = f - 1
                        pe.wait_ge(sem["eh_lo"], FE * k + g + 1)
                        w_h, w_l = split_blk(w_ffn)
                        for s in range(2):
                            slots = slice(s * P, (s + 1) * P)
                            for h in range(2):
                                half = slice(h * 512, (h + 1) * 512)
                                mm = mm_split(nc, ps[:, 2 * s + h, :], ge_hi[:, g % 2, slots], ge_lo[:, g % 2, slots], w_h[:, half],
                                              w_l[:, half], g == 0, g == FE - 1)
                        done(mm)
                for i in range(NT):
                    pe.wait_ge(sem["ey_lo"], 4 * (k + 1))
                    for h in range(2):
                        n = 2 * i + h
                        if n >= 2:
                            pe.wait_ge(sem["comb_ev"], 10 * k + n - 1)
                        elif n == 0:
                            pe.wait_ge(sem["selt_ev"], 2 * k + 2)
                        for s in range(2):
                            half = slice(h * 512, (h + 1) * 512)
                            w = selT[:, s, i * P:(i + 1) * P]
                            nc.tensor.matmul(ps[:, 6 + n % 2, :], w, ye_hi[:, s, half], start=s == 0, stop=False)
                            mm = nc.tensor.matmul(ps[:, 6 + n % 2, :], w, ye_lo[:, s, half], start=False, stop=s == 1)
                        mm.then_inc(sem["comb_mm"], 1)

            for l in range(DEPTH):
                if l == 0:
                    mod_phase()
                    next_phase()
                norm_phase(2 * l)
                next_phase()
                proj_phase(l)
                next_phase()
                att_phase(l)
                next_phase()
                kk_phase(l)
                next_phase()
                for c in range(NPAIR):
                    rwkv_dir(l, c, 0)
                    rwkv_dir(l, c, 1)
                gn_phase(l)
                wo_phase(l)
                next_phase()
                rowvec(2 * l)
                norm_phase(2 * l + 1)
                next_phase()
                if l == 0:
                    dense_phase(l)
                else:
                    route_phase()
                    next_phase()
                    for e in range(NE):
                        moe_pass(e)
                    next_phase()

                    def body():
                        for n in range(2 * NE):
                            moe_pass(NE + n)
                    with_flag(pe, body)
                next_phase()
                rowvec(2 * l + 1)

        @block.scalar
        def _(act):
            E = Signals("act", sem)
            phase = [0]

            def next_phase():
                phase[0] += 1
                act.drain().then_inc(sem["act_phase"], 1)
                act.wait_ge(sem["pe_phase"], phase[0])
                act.wait_ge(sem["act_phase"], phase[0])
                act.wait_ge(sem["dve_phase"], phase[0])
                act.wait_ge(sem["pool_phase"], phase[0])

            A = nc.scalar.activation

            def w_hi(high, n):
                slots = high.shape[1]
                act.wait_ge(ring_sem[n % RING], 16 * (n // RING + 1))
                act.wait_ge(sem["block_used"], n - slots + 1)
                A(high[:, n % slots, :], ring[:, n % RING, :], ACT.Copy).then_inc(*E.sig("w_hi"))

            def mod_row(m, bank):
                act.wait_ge(sem["block_used"], mod_blocks_done(m))
                if m >= 1:
                    act.wait_ge(sem["mod_tr"], m)
                A(modrow[0:2, :], ps[0:2, bank, :], ACT.Copy).then_inc(*E.sig("mod_row"))

            def norm_phase(k):
                if k == 0:
                    act.wait_ge(sem["x_in"], 16)
                for i in range(NT):
                    if k >= 1:
                        act.wait_ge(sem["post_x"], NT * (k - 1) + i + 1)
                    act.wait_ge(*E.own_last())
                    A(sq_scratch(i), x[:, i, :], ACT.Square, accum_out=nstat[:, i:i + 1]).then_inc(*E.sig("norm_sq"))
                for kc in range(KC):
                    act.wait_ge(sem["norm_tr"], KC * k + kc + 1)
                    w, sh = k % 2, (0 if k % 2 == 0 else 24)
                    A(hT[:, kc, CTX:T], pair(kc % 4)[:, 512:1024], ACT.Identity, bias=mod[:, k // 2, sh + kc, 1:2],
                            scale=gpre[:, w, kc, 1:2]).then_inc(*E.sig("norm_ev_act"))

            def proj_phase(l):
                first = PROJ_AT[l]
                w_hi(w_proj, first)
                for kc in range(KC):
                    A(hT_hi[:, kc, :], hT[:, kc, :], ACT.Copy).then_inc(*E.sig("x_hi"))
                w_hi(w_proj, first + 1)
                for o in range(PROJ_B):
                    act.wait_ge(sem["block_used"], first + o + 1)
                    if o + 2 < PROJ_B:
                        w_hi(w_proj, first + o + 2)
                    src = pair_r(o % 4)
                    if o < 4:
                        A(qT[:, o, :], src, ACT.Copy, scale=HD ** -0.5).then_inc(*E.sig("proj_ev_act"))
                    elif o == 4:
                        A(kT[:, :], src, ACT.Copy).then_inc(*E.sig("proj_ev_act"))
                    elif o == 5:
                        A(vT[:, :], src, ACT.Copy).then_inc(*E.sig("proj_ev_act"))
                    elif o < 18:
                        j = o - 6
                        pr = praw[:, j % 2, :]
                        if j < 2:
                            for z in (0, 129, 642):
                                A(pr[:, z:z + 1], C("ones")[:, 0:1], ACT.Copy, scale=0.0).then_inc(*E.sig("act_step"))
                        else:
                            act.wait_ge(sem["proj_ev_dve"], 13 * l + j - 1)
                        A(pr[:, 1:129], src[:, 0:CTX], ACT.Copy, scale=hpar[:, j:j + 1]).then_inc(*E.sig("act_step"))
                        A(pr[:, 130:642], src[:, CTX:T], ACT.Copy, scale=hpar[:, j:j + 1]).then_inc(*E.sig("proj_ev_act"))
                    elif o == 18:
                        A(zlow[:, 0, :], src, ACT.Tanh).then_inc(*E.sig("proj_ev_act"))
                    elif o == 19:
                        A(zlow[:, 1, :], src, ACT.Copy).then_inc(*E.sig("proj_ev_act"))
                    else:
                        A(zlow[:, 2, :], src, ACT.Tanh, scale=0.5).then_inc(*E.sig("proj_ev_act"))

            def att_phase(l):
                for t in range(N_UNITS + 2):
                    if t < N_UNITS:
                        c, g, blkq = unit(t)
                        un = l * N_UNITS + t
                        nk = n_keys(blkq)
                        act.wait_ge(sem["att_max"], un + 1)
                        if t >= 3:
                            act.wait_ge(sem["att_tr"], un - 2)
                        a = attst[:, t % 4, :]
                        h = l * NH + c + 4 * g
                        A(a[:, 3:4], sink[:, h:h + 1], ACT.Exp, bias=a[:, 1:2]).then_inc(*E.sig("act_step"))
                        A(prob[:, t % 3, 0:nk], pair(t % 2)[:, 0:nk], ACT.Exp, bias=a[:, 1:2], accum_out=a[:, 2:3]).then_inc(*E.sig("att_exp"))
                    if t >= 2:
                        u = t - 2
                        un = l * N_UNITS + u
                        act.wait_ge(sem["att_tr"], un + 1)
                        if u >= 2:
                            act.wait_ge(sem["att_o"], un - 1)
                        nk = n_keys(unit(u)[2])
                        A(probT[:, u % 2, 0:nk], pair(2)[:, 0:nk], ACT.Copy).then_inc(*E.sig("att_trev"))

            def spread(w, c, b):
                return A(spr[:, b, :].rearrange("p (i h k) -> p i h k", i=NT, h=2),
                         rw_s[:, w, :, 2 * c:2 * c + 2].unsqueeze(3).broadcast_to([P, NT, 2, HD]), ACT.Copy)

            def kk_phase(l):
                for c in range(NPAIR):
                    A(sq4[:, c, :], rkv[:, 4 + c, :], ACT.Square, scale=PR(l, "k_k", c)).then_inc(*E.sig("kk_prod"))

            def rwkv_dir(l, c, d):
                g = (l * NPAIR + c) * 2 + d
                k = l * NPAIR + c
                if d == 0:
                    spread(0, c, 0).then_inc(*E.sig("spread_ev"))
                act.wait_ge(sem["low_mm"], g + 1)
                A(tw[:, :], pair640(0), ACT.Tanh, bias=hpar[:, 16 + 4 * d + c:17 + 4 * d + c], scale=0.5).then_inc(*E.sig("low_w"))
                A(ta[:, :], pair640(1), ACT.Tanh, bias=hpar[:, 24 + 4 * d + c:25 + 4 * d + c], scale=0.5).then_inc(*E.sig("low_ev"))
                if d == 0:
                    act.wait_ge(sem["vt_tr"], k + 1)
                    A(vt_rw[:, :, :].rearrange("p i c -> p (i c)"), pair640(3), ACT.Copy).then_inc(*E.sig("vt_ev"))
                act.wait_ge(sem["dec_cum"], g + 1)
                if d == 0:
                    A(e_in[:, :], cumc[:, :], ACT.Exp).then_inc(*E.sig("dec_exp"))
                    A(e_inv[:, :], cumc[:, :], ACT.Exp, scale=-1.0).then_inc(*E.sig("dec_exp"))
                    act.wait_ge(sem["dec_cumx"], g + 1)
                    A(e_ex[:, :], cumx[:, :], ACT.Exp).then_inc(*E.sig("dec_exp"))
                else:
                    A(e_ex[:, :], cumc[:, :], ACT.Exp, scale=-1.0).then_inc(*E.sig("dec_exp"))
                    act.wait_ge(sem["dec_cumx"], g + 1)
                    A(e_in[:, :], cumx[:, :], ACT.Exp, scale=-1.0).then_inc(*E.sig("dec_exp"))
                    A(e_inv[:, :], cumx[:, :], ACT.Exp).then_inc(*E.sig("dec_exp"))
                A(phs[:, 0, :], nstat[:, 10:15], ACT.Exp, scale=-1.0).then_inc(*E.sig("act_step"))
                A(phs[:, 1, :], nstat[:, 10:15], ACT.Exp, scale=-2.0).then_inc(*E.sig("dec_ph"))
                if mod_group(g, 0) is not None:
                    mod_row(mod_group(g, 0), 2)
                for a in range(2):
                    act.wait_ge(sem["hat_tr"], 2 * g + a + 1)
                    A(bktok[:, :, a, :], pair640(2 + a).rearrange("p (i c) -> p i c", i=NT), ACT.Copy).then_inc(*E.sig("hat_ev"))
                for i in range(NT):
                    act.wait_ge(sem["gram_ev"], 10 * g + 2 * i + 2)
                    A(nb[:, 2 * i:2 * i + 2, 0, :], gm[:, 2 * i:2 * i + 2, 0, :], ACT.Copy).then_inc(*E.sig("n_ev"))
                for i in range(NT):
                    act.wait_ge(sem["mv_mm"], 5 * g + i + 1)
                    A(mv[:, i, :].rearrange("p (h v) -> p h v", h=2),
                      ps[:, 4 + i % 4, 0:384].rearrange("p (h v) -> p h v", h=2)[:, :, 0:64], ACT.Copy).then_inc(*E.sig("mv_ev"))
                    act.wait_ge(sem["lt_sub"], 5 * g + i + 1)
                    A(nb[:, 2 * i:2 * i + 2, 1, :], ps[:, i % 4, 0:256].rearrange("p (h t) -> p h t", h=2), ACT.Copy).then_inc(*E.sig("lt_ev"))
                for n in range(30):
                    i = n % 5
                    act.wait_ge(sem["sq_mm"], 30 * g + n + 1)
                    if n >= 5:
                        act.wait_ge(sem["inv_mm"], 30 * g + n - 4)
                    if n < 25:
                        A(nb[:, 2 * i:2 * i + 2, :, :].rearrange("p u a t -> p (u a t)"), ps[:, n % 4, :], ACT.Copy).then_inc(*E.sig("sq_ev"))
                    else:
                        A(nb[:, 2 * i:2 * i + 2, 1, :], ps[:, n % 4, :].rearrange("p (u a t) -> p u a t", u=2, a=2)[:, :, 1, :],
                          ACT.Copy).then_inc(*E.sig("sq_ev"))
                for i in range(NT):
                    act.wait_ge(sem["inv_ev"], 30 * g + 25 + i + 1)
                    A(xq[:, 2 * i:2 * i + 2, :], gm[:, 2 * i:2 * i + 2, 0, :], ACT.Copy).then_inc(*E.sig("xb_ev"))
                for i in range(NT):
                    act.wait_ge(sem["nw_p"], 10 * g + i + 1)
                    A(gmb[:, 2 * i:2 * i + 2, 2, P:2 * P], ps[:, 4 + i % 4, 0:256].rearrange("p (h t) -> p h t", h=2), ACT.Copy).then_inc(*E.sig("nw_t"))
                for n in range(NT):
                    act.wait_ge(sem["u_mm"], 5 * g + n + 1)
                    A(ub[:, order(d)[n], :].rearrange("p (h v) -> p h v", h=2),
                      ps[:, 1, 0:384].rearrange("p (h v) -> p h v", h=2)[:, :, 0:64], ACT.Copy).then_inc(*E.sig("u_ev"))
                    if mod_group(g, 1) is not None and n == 3:
                        mod_row(mod_group(g, 1), 7)
                act.wait_ge(sem["so_tr"], g + 1)
                for hh in range(2):
                    h = slice(64 * hh, 64 * hh + 64)
                    A(st_out[h, d, c, :], ps[h, 3, h], ACT.Copy).then_inc(*E.sig("act_step"))
                if d == 1:
                    act.wait_ge(sem["bon_mm"], k + 1)
                    A(rw_s[:, 1, :, 2 * c:2 * c + 2], ps[:, 0, 0:10].rearrange("p (i h) -> p i h", i=NT), ACT.Copy).then_inc(*E.sig("act_step"))
                next_phase()

            def gn_phase(l):
                for c in range(NPAIR):
                    act.wait_ge(sem["gn_cent"], l * NPAIR + c + 1)
                    A(sq4[:, c, :], oT[:, 4 + c, :], ACT.Square).then_inc(*E.sig("gn_sq"))
                act.wait_ge(sem["gn_pow"], l + 1)
                for c in range(NPAIR):
                    for b in range(2):
                        if c >= 1:
                            act.wait_ge(sem["gn_mm"], 12 * l + 3 * (c - 1) + b + 1)
                        spread(2 - b, c, b).then_inc(*E.sig("spread_ev"))
                next_phase()

            def wo_phase(l):
                for fc in range(WO_B):
                    A(oT_hi[:, fc, :], oT[:, fc, :], ACT.Copy).then_inc(*E.sig("x_hi"))
                    n = WO_AT[l] + fc
                    act.wait_ge(ring_sem[n % RING], 16 * (n // RING + 1))
                    A(w_wo[:, fc, :], ring[:, n % RING, :], ACT.Copy).then_inc(*E.sig("w_hi"))
                for i in range(NT):
                    if i < NT - 1:
                        act.wait_ge(sem["wo_mm"], l * (NT - 1) + i + 1)
                    else:
                        act.wait_ge(sem["block_used"], WO_AT[l] + WO_B)
                    A(fo[:, i, :], pair(i % 4), ACT.Copy).then_inc(*E.sig("wo_ev"))

            def post_phase(k):
                for i in range(NT):
                    A(sq_scratch(i), fo[:, i, :], ACT.Square, accum_out=pstat[:, i:i + 1]).then_inc(*E.sig("post_sq"))

            def dense_phase(l):
                first = FFN_AT[l]
                w_hi(w_ffn, first)
                for kc in range(KC):
                    A(hT_ffn_hi[:, kc, :], hT[:, kc, :], ACT.Copy).then_inc(*E.sig("x_hi"))
                for n in (1, 2):
                    w_hi(w_ffn, first + n)
                for f in range(FT):
                    act.wait_ge(sem["block_used"], first + 2 * f + 2)
                    if f >= 2:
                        act.wait_ge(sem["ff_g"], f - 1)
                    A(ftmp[:, f % 2, :], pair_r(2 * f % 4), ACT.Tanh, scale=0.5).then_inc(*E.sig("ff_th"))
                    for n in (2 * f + 3, 2 * f + 4):
                        if n < 2 * FT:
                            w_hi(w_ffn, first + n)
                for h in range(2):
                    act.wait_ge(sem["block_used"], FFN_AT[l] + 2 * FT + (h + 1) * FT // 2)
                    for i in range(NT):
                        A(fo[:, i, h * 512:(h + 1) * 512], ps[:, (5 * h + i) % 8, :], ACT.Copy).then_inc(*E.sig("ff_yev"))

            def route_phase():
                for i in range(NT):
                    if i == 3:
                        act.wait_ge(sem["rt_max"], 1)
                        for j in range(NT):
                            A(gate[:, j, :], lg[:, j, :], ACT.Exp, bias=rstat[:, j:j + 1]).then_inc(*E.sig("rt_exp"))
                    act.wait_ge(sem["htok_tr"], i + 1)
                    A(htok[:, i, :], pair(1 + i % 3), ACT.Copy).then_inc(*E.sig("htok_ev"))
                for n in range(3):
                    w_hi(w_ffn, FFN_AT[1] + n)

            def moe_start():
                for i in range(NT):
                    A(htok_hi[:, i, :], htok[:, i, :], ACT.Copy).then_inc(*E.sig("x_hi"))

            def moe_pass(k):
                first = FFN_AT[1] + k * EXP_B
                for kc in range(KC):
                    act.wait_ge(sem["gat_mm"], KC * k + kc + 1)
                    A(hg_hi[:, kc, :], ps[:, 4 + kc % 2, 0:CAP], ACT.Copy).then_inc(*E.sig("gat_ev"))
                for s in range(2):
                    act.wait_ge(sem["selt_tr"], 2 * k + s + 1)
                    A(selT[:, s, :], pair640(3), ACT.Copy).then_inc(*E.sig("selt_ev"))
                for f in range(FE):
                    act.wait_ge(sem["block_used"], first + up_done(f))
                    if f >= 2:
                        act.wait_ge(sem["eh_lo"], FE * k + f - 1)
                    A(ftmp[:, f % 2, 0:CAP], ps[:, 4 + f % 2, 0:CAP], ACT.Tanh, scale=0.5).then_inc(*E.sig("eh_th"))
                    for n in ahead(f)[0]:
                        w_hi(w_ffn, first + n)
                    act.wait_ge(sem["eh_g"], FE * k + f + 1)
                    A(ge_hi[:, f % 2, :], ftmp[:, f % 2, CAP:2 * CAP], ACT.Copy).then_inc(*E.sig("eh_hi"))
                    for n in ahead(f)[1]:
                        w_hi(w_ffn, first + n)
                if k not in LAST_PASS:
                    w_hi(w_ffn, first + EXP_B)
                    w_hi(w_ffn, first + EXP_B + 1)
                act.wait_ge(sem["block_used"], first + EXP_B)
                for n in range(4):
                    A(ye_hi[:, n // 2, (n % 2) * 512:(n % 2 + 1) * 512], ps[:, n, :], ACT.Copy).then_inc(*E.sig("ey_ev"))
                if k not in LAST_PASS:
                    w_hi(w_ffn, first + EXP_B + 2)

            for l in range(DEPTH):
                if l == 0:
                    act.wait_ge(sem["cond_in"], 64)
                    A(tiny[:, 0:16], condT[:, :, :].rearrange("p a b -> p (a b)"), ACT.Tanh, scale=0.5).then_inc(*E.sig("act_step"))
                    for m in range(MOD_FIRST):
                        mod_row(m, m)
                    next_phase()
                norm_phase(2 * l)
                next_phase()
                proj_phase(l)
                next_phase()
                att_phase(l)
                next_phase()
                kk_phase(l)
                next_phase()
                for c in range(NPAIR):
                    rwkv_dir(l, c, 0)
                    rwkv_dir(l, c, 1)
                gn_phase(l)
                wo_phase(l)
                next_phase()
                post_phase(2 * l)
                norm_phase(2 * l + 1)
                next_phase()
                if l == 0:
                    dense_phase(l)
                else:
                    route_phase()
                    next_phase()
                    moe_start()
                    for e in range(NE):
                        moe_pass(e)
                    next_phase()

                    def body():
                        for n in range(3):
                            w_hi(w_ffn, N_BLOCKS + n)
                        for n in range(2 * NE):
                            moe_pass(NE + n)
                    with_flag(act, body)
                next_phase()
                post_phase(2 * l + 1)

        @block.vector
        def _(dve):
            E = Signals("dve", sem)
            phase = [0]

            def next_phase():
                phase[0] += 1
                dve.drain().then_inc(sem["dve_phase"], 1)
                dve.wait_ge(sem["pe_phase"], phase[0])
                dve.wait_ge(sem["act_phase"], phase[0])
                dve.wait_ge(sem["dve_phase"], phase[0])
                dve.wait_ge(sem["pool_phase"], phase[0])

            V = nc.vector

            split = [0]
            x_split = [0]

            def w_lo(high, n):
                split[0] += 1
                dve.wait_ge(sem["w_hi"], split[0])
                dve.wait_ge(ring_sem[n % RING], 16 * (n // RING + 1))
                V.tensor_tensor(ring_lo[:, n % RING, :], ring[:, n % RING, :], high[:, n % high.shape[1], :], ALU.subtract).then_inc(*E.sig("w_lo"))

            def x_lo(low, x_f, high):
                x_split[0] += 1
                dve.wait_ge(sem["x_hi"], x_split[0])
                V.tensor_tensor(low, x_f, high, ALU.subtract).then_inc(*E.sig("x_lo"))

            def mod_bias(m, bank):
                l, n = divmod(m, MOD_G)
                dve.wait_ge(sem["mod_tr"], m + 1)
                V.tensor_tensor(mod[:, l, 4 * n:4 * n + 4, :], ps[:, bank, 0:8].rearrange("p (j g) -> p j g", g=2),
                                PR(l, "b_mod", 4 * n, 4).unsqueeze(2).broadcast_to([P, 4, 2]), ALU.add).then_inc(*E.sig("mod_ev"))

            def pre_scale(l, w):
                sc, gpr = [(8, "g_pre_mix"), (32, "g_pre_ffn")][w]
                V.scalar_tensor_tensor(gpre[:, w, :, :], mod[:, l, sc:sc + 8, :], 1.0,
                                       PR(l, gpr).unsqueeze(2).broadcast_to([P, 8, 2]), ALU.add, ALU.mult).then_inc(*E.sig("dve_step"))

            def post_scale(l, w):
                gt, gpo = [(16, "g_post_mix"), (40, "g_post_ffn")][w]
                V.tensor_tensor(gpost[:, w, :, :], mod[:, l, gt:gt + 8, :],
                                PR(l, gpo).unsqueeze(2).broadcast_to([P, 8, 2]), ALU.mult).then_inc(*E.sig("dve_step"))

            def mod_phase(l):
                if l == 0:
                    dve.wait_ge(sem["consts_in"], 16)
                    dve.wait_ge(sem["cond_in"], 64)
                    dve.wait_ge(sem["act_step"], 1)
                    cf = condT[:, :, :].rearrange("p a b -> p (a b)")
                    V.scalar_tensor_tensor(tiny[:, 16:32], tiny[:, 0:16], 1.0, cf, ALU.add, ALU.mult).then_inc(*E.sig("dve_step"))
                    dve.wait_ge(*E.own_last())
                    V.tensor_scalar(cf, tiny[:, 16:32], 0.5, None, ALU.mult).then_inc(*E.sig("silu_c"))
                    V.tensor_copy(identb[:, :], ident).then_inc(*E.sig("dve_step"))
                    for m in range(MOD_FIRST):
                        mod_bias(m, m)
                    dve.wait_ge(*E.own_last())
                pre_scale(l, 0)
                V.tensor_scalar(hpar[:, 0:12], PR(l, "mu"), 0.5, None, ALU.mult).then_inc(*E.sig("dve_step"))
                V.tensor_scalar(hpar[:, 16:24], PR(l, "w0"), 0.5, None, ALU.mult).then_inc(*E.sig("dve_step"))
                V.tensor_scalar(hpar[:, 24:32], PR(l, "a0"), 0.5, None, ALU.mult).then_inc(*E.sig("dve_step"))
                V.tensor_scalar(hpar[:, 32:36], PR(l, "k_a"), 0.5, None, ALU.mult).then_inc(*E.sig("dve_step"))
                V.tensor_scalar(hpar[:, 36:40], PR(l, "k_a"), -0.5, 1.0, ALU.mult, ALU.add).then_inc(*E.sig("dve_step"))
                V.tensor_scalar(hpar[:, 40:52], PR(l, "mu"), -1.0, 1.0, ALU.mult, ALU.add).then_inc(*E.sig("dve_step"))

            def norm_phase(k):
                dve.wait_ge(sem["norm_sq"], NT * (k + 1))
                V.tensor_scalar(nstat[:, 5:10], nstat[:, 0:5], 1.0 / D, NORM_EPS, ALU.mult, ALU.add).then_inc(*E.sig("stat_ms"))
                dve.wait_ge(sem["stat_pow"], 2 * k + 1)
                dve.wait_ge(*E.own_last())
                for i in range(NT):
                    V.tensor_scalar(xn[:, i, :], x[:, i, :], nstat[:, 15 + i:16 + i], None, ALU.mult).then_inc(*E.sig("norm_x"))
                for kc in range(KC):
                    dve.wait_ge(sem["norm_tr"], KC * k + kc + 1)
                    w, sh = k % 2, (0 if k % 2 == 0 else 24)
                    V.tensor_scalar(hT[:, kc, 0:CTX], pair(kc % 4)[:, 384:512], gpre[:, w, kc, 0:1],
                                          mod[:, k // 2, sh + kc, 0:1], ALU.mult, ALU.add).then_inc(*E.sig("norm_ev_dve"))

            def proj_phase(l):
                first = PROJ_AT[l]
                w_lo(w_proj, first)
                for kc in range(KC):
                    x_lo(hT_lo[:, kc, :], hT[:, kc, :], hT_hi[:, kc, :])
                w_lo(w_proj, first + 1)
                for o in range(PROJ_B):
                    if o + 2 < PROJ_B:
                        w_lo(w_proj, first + o + 2)
                    if 6 <= o < 18 or o == 20:
                        dve.wait_ge(sem["proj_ev_act"], l * PROJ_B + o + 1)
                    if 6 <= o < 18:
                        j = o - 6
                        pr = praw[:, j % 2, :]
                        sh = pshift[:, j % 2, :]
                        V.tensor_tensor(sh[:, 0:CTX], pr[:, 0:128], pr[:, 2:130], ALU.add).then_inc(*E.sig("dve_step"))
                        V.tensor_tensor(sh[:, CTX:T], pr[:, 129:641], pr[:, 131:643], ALU.add).then_inc(*E.sig("dve_step"))
                        dve.wait_ge(*E.own_last())
                        V.scalar_tensor_tensor(rkv[:, j, :], pair_r(o % 4), hpar[:, 40 + j:41 + j], sh[:, :], ALU.mult, ALU.add).then_inc(*E.sig("proj_ev_dve"))
                    elif o == 20:
                        V.tensor_scalar(zlow[:, 2, :], zlow[:, 2, :], 0.5, 0.5, ALU.mult, ALU.add).then_inc(*E.sig("proj_ev_dve"))

            def att_phase(l):
                for c in range(5):
                    dve.wait_ge(sem["rope_mm"], 5 * l + c + 1)
                    dst = qT[:, c, CTX:T] if c < 4 else kT[:, CTX:T]
                    tmp = ropetmp[:, c % 2, :]
                    V.tensor_tensor(tmp, ps[:, c, :], C("sin"), ALU.mult).then_inc(*E.sig("dve_step"))
                    V.tensor_tensor(dst, dst, C("cos"), ALU.mult).then_inc(*E.sig("dve_step"))
                    dve.wait_ge(*E.own_last())
                    V.tensor_tensor(dst, dst, tmp, ALU.add).then_inc(*E.sig("rope_ev"))
                dve.wait_ge(sem["kc_tr"], l + 1)
                V.tensor_copy(vtok[:, :, :].rearrange("p i c -> p (i c)"), pair640(3)).then_inc(*E.sig("dve_step"))
                V.tensor_copy(kctok[:, :], ps[:, 5, PAST:PAST + P]).then_inc(*E.sig("dve_step"))
                V.tensor_copy(kcT[:, :], ps[:, 5, 0:PAST]).then_inc(*E.sig("kc_ev"))
                for t in range(N_UNITS + 3):
                    if t < N_UNITS:
                        c, g, blkq = unit(t)
                        un = l * N_UNITS + t
                        h = l * NH + c + 4 * g
                        a = attst[:, t % 4, :]
                        dve.wait_ge(sem["att_s"], un + 1)
                        V.tensor_reduce(a[:, 0:1], pair(t % 2)[:, 0:n_keys(blkq)], AX.X, ALU.max).then_inc(*E.sig("dve_step"))
                        dve.wait_ge(*E.own_last())
                        V.tensor_scalar(a[:, 1:2], a[:, 0:1], sink[:, h:h + 1], -1.0, ALU.max, ALU.mult).then_inc(*E.sig("att_max"))
                    if 1 <= t <= N_UNITS:
                        u = t - 1
                        un = l * N_UNITS + u
                        a = attst[:, u % 4, :]
                        dve.wait_ge(sem["att_exp"], un + 1)
                        V.tensor_tensor(a[:, 4:5], a[:, 2:3], a[:, 3:4], ALU.add).then_inc(*E.sig("dve_step"))
                        dve.wait_ge(*E.own_last())
                        V.reciprocal(a[:, 5:6], a[:, 4:5]).then_inc(*E.sig("dve_step"))
                        dve.wait_ge(*E.own_last())
                        nk = n_keys(unit(u)[2])
                        V.tensor_scalar(prob[:, u % 3, 0:nk], prob[:, u % 3, 0:nk], a[:, 5:6], None, ALU.mult).then_inc(*E.sig("att_p"))
                    if t >= 4 and t % 2 == 0:
                        u = t - 3
                        c, g, blkq = unit(u)
                        dve.wait_ge(sem["att_o"], l * N_UNITS + u + 1)
                        V.tensor_copy(oT[:, c, (blkq + 1) * P:(blkq + 2) * P], ps[:, 6 + (u // 2) % 2, 0:P]).then_inc(*E.sig("att_oev"))

            def tiles(a):
                return a.rearrange("p (i t) -> p i t", i=NT)

            def kk_phase(l):
                dve.wait_ge(sem["kk_sum"], l + 1)
                V.tensor_scalar(rw_s[:, 3, :, :].rearrange("p i h -> p (i h)"), ps[:, 0, 0:NT * RH], 1e-12, None, ALU.add).then_inc(*E.sig("kk_ss"))

            def rwkv_dir(l, c, d):
                g = (l * NPAIR + c) * 2 + d
                k = l * NPAIR + c
                kr = rkv[:, 4 + c, :]
                rr = rkv[:, c, :]
                V.memset(st[:, :, :].rearrange("p b v -> p (b v)"), 0.0).then_inc(*E.sig("dve_step"))
                dve.wait_ge(sem["low_w"], g + 1)
                V.tensor_scalar(lw[:, :], tw[:, :], -HALF_DECAY, -HALF_DECAY, ALU.mult, ALU.add).then_inc(*E.sig("dve_step"))
                dve.wait_ge(*E.own_last())
                V.tensor_reduce(phs[:, 0, :], tiles(lw), AX.X, ALU.add).then_inc(*E.sig("dve_step"))
                dve.wait_ge(*E.own_last())
                V.tensor_scalar(nstat[:, 10:15], phs[:, 0, :], -0.5, None, ALU.mult).then_inc(*E.sig("dve_step"))
                dve.wait_ge(*E.own_last())
                for i in range(NT):
                    sl = slice(i * P, (i + 1) * P)
                    ins = V.tensor_tensor_scan(cumc[:, sl], C("ones"), lw[:, sl], nstat[:, 10 + i:11 + i], ALU.mult, ALU.add)
                    ins.then_inc(*E.sig("dec_cum" if i == NT - 1 else "dve_step"))
                dve.wait_ge(*E.own_last())
                V.tensor_tensor(cumx[:, :], cumc[:, :], lw[:, :], ALU.subtract).then_inc(*E.sig("dec_cumx"))
                if d == 0:
                    dve.wait_ge(sem["kk_mm"], k + 1)
                    V.scalar_tensor_tensor(kk[:, :], kr, PR(l, "k_k", c), pair640(2), ALU.mult, ALU.mult).then_inc(*E.sig("kk_done"))
                dve.wait_ge(sem["st_tr"], g + 1)
                dve.wait_ge(*E.own_last())
                V.tensor_copy(st[0:64, 1, 0:64], ps[0:64, 4, 0:64]).then_inc(*E.sig("dve_step"))
                V.tensor_copy(st[64:128, 1, 64:128], ps[64:128, 4, 0:64]).then_inc(*E.sig("st_ev"))
                dve.wait_ge(sem["low_ev"], g + 1)
                V.tensor_scalar(kdt[:, :], ta[:, :], hpar[:, 32 + c:33 + c], hpar[:, 36 + c:37 + c], ALU.mult, ALU.add).then_inc(*E.sig("dve_step"))
                dve.wait_ge(*E.own_last())
                V.tensor_tensor(kdt[:, :], kdt[:, :], kr, ALU.mult).then_inc(*E.sig("dve_step"))
                V.scalar_tensor_tensor(avec[:, :], ta[:, :], 1.0, kk[:, :], ALU.add, ALU.mult).then_inc(*E.sig("dve_step"))
                dve.wait_ge(*E.own_last())
                first, second, third = 3 * g + 1, 3 * g + 2, 3 * g + 3
                dve.wait_ge(sem["dec_exp"], third)
                V.scalar_tensor_tensor(bkbar[:, 0, :], avec[:, :], 0.5, e_inv[:, :], ALU.mult, ALU.mult).then_inc(*E.sig("dve_step"))
                V.tensor_tensor(bkbar[:, 1, :], kdt[:, :], e_inv[:, :], ALU.mult).then_inc(*E.sig("rw_ops"))
                V.scalar_tensor_tensor(ar[:, :, 0, :], tiles(kk), -1.0, tiles(e_ex), ALU.mult, ALU.mult).then_inc(*E.sig("dve_step"))
                V.tensor_tensor(ar[:, :, 1, :], tiles(rr), tiles(e_in), ALU.mult).then_inc(*E.sig("ar_done"))
                if mod_group(g, 0) is not None:
                    mod_bias(mod_group(g, 0), 2)
                mask = C("mask_f" if d == 0 else "mask_b").unsqueeze(1).broadcast_to([P, 2, 256])
                dve.wait_ge(sem["dec_ph"], g + 1)
                for u in range(10):
                    dve.wait_ge(sem["gram_mm"], 10 * g + u + 1)
                    V.tensor_tensor(gm[:, u, :, :].rearrange("p (b a) t -> p b (a t)", b=2), ps[:, u % 8, :].rearrange("p (b c) -> p b c", b=2),
                                    mask, ALU.mult).then_inc(*E.sig("gram_ev"))
                    if u == 2 and d == 0:
                        V.tensor_copy(kds[:, :], kdt[:, :]).then_inc(*E.sig("dve_step"))
                    elif u == 2:
                        V.tensor_tensor(kds[:, :], kds[:, :], kdt[:, :], ALU.add).then_inc(*E.sig("dve_step"))
                    elif u == 6 and d == 1:
                        dve.wait_ge(*E.own_last())
                        V.scalar_tensor_tensor(kds[:, :], rr, PR(l, "r_k", c), kds[:, :], ALU.mult, ALU.mult).then_inc(*E.sig("dve_step"))
                idents = ident.unsqueeze(1).broadcast_to([P, 2, P])
                for i in range(NT):
                    if i == 0:
                        dve.wait_ge(*E.own_last())
                    V.tensor_tensor(xq[:, 2 * i:2 * i + 2, :], gm[:, 2 * i:2 * i + 2, 0, :], idents, ALU.add).then_inc(*E.sig("x0_ev"))
                    dve.wait_ge(sem["lt_tr"], 5 * g + i + 1)
                    V.tensor_tensor(lfi[:, 2 * i:2 * i + 2, :], ps[:, i % 4, 0:256].rearrange("p (h t) -> p h t", h=2), idents,
                                    ALU.subtract).then_inc(*E.sig("lt_sub"))
                for m in range(30):
                    i = m % 5
                    dve.wait_ge(sem["inv_mm"], 30 * g + m + 1)
                    src = ps[:, 4 + m % 4, 0:256].rearrange("p (h t) -> p h t", h=2)
                    dst = xq[:, 2 * i:2 * i + 2, :] if m < 25 else gm[:, 2 * i:2 * i + 2, 0, :]
                    V.tensor_tensor(dst, xq[:, 2 * i:2 * i + 2, :], src, ALU.add).then_inc(*E.sig("inv_ev"))
                for q in range(2):
                    for i in range(NT):
                        n = (2 * g + q) * NT + i
                        dve.wait_ge(sem["nw_p"], n + 1)
                        if q == 0:
                            dve.wait_ge(sem["mv_mm"], 5 * g + 5)
                        else:
                            dve.wait_ge(sem["nw_c"], n - 4)
                        V.tensor_tensor(gmb[:, 2 * i:2 * i + 2, 2, 0:P], ps[:, i % 4, 0:256].rearrange("p (h t) -> p h t", h=2), idents,
                                        ALU.add).then_inc(*E.sig("nw_e"))
                    for i in range(NT):
                        n = (2 * g + q) * NT + i
                        dve.wait_ge(sem["nw_c"], n + 1)
                        x_u = gm[:, 2 * i:2 * i + 2, 0, :]
                        V.tensor_tensor(x_u, x_u, ps[:, 4 + i % 4, 0:256].rearrange("p (h t) -> p h t", h=2), ALU.add).then_inc(*E.sig("nw_x"))
                for n, i in enumerate(order(d)):
                    if n == 0:
                        V.memset(s0s[:, i, :], 0.0).then_inc(*E.sig("st_scaled"))
                    else:
                        dve.wait_ge(*E.own_last())
                        V.tensor_scalar(s0s[:, i, :], st[:, 1, :], phs[:, 0, i:i + 1], None, ALU.mult).then_inc(*E.sig("st_scaled"))
                        if n < NT - 1:
                            V.tensor_scalar(stpc[:, :], st[:, 1, :], phs[:, 1, i:i + 1], None, ALU.mult).then_inc(*E.sig("dve_step"))
                    dve.wait_ge(sem["x_mm"], 5 * g + n + 1)
                    V.tensor_tensor(xb[:, n % 2, :], ps[:, 0, 0:P], mv[:, i, :], ALU.add).then_inc(*E.sig("x_ev"))
                    if mod_group(g, 1) is not None and n == NT - 1:
                        mod_bias(mod_group(g, 1), 7)
                        dve.wait_ge(sem["x_ev"], 5 * g + n + 1)
                    if n == NT - 1:
                        break
                    dve.wait_ge(sem["s_mm"], 4 * g + n + 1)
                    for hh in range(2):
                        h = slice(64 * hh, 64 * hh + 64)
                        if n == 0:
                            ins = V.tensor_scalar(st[h, 0, h], ps[h, 2, h], phs[h, 0, i:i + 1], None, ALU.mult)
                        else:
                            ins = V.scalar_tensor_tensor(st[h, 1, h], ps[h, 2, h], phs[h, 0, i:i + 1], stpc[h, h], ALU.mult, ALU.add)
                        ins.then_inc(*E.sig("s_ev" if hh == 1 else "dve_step"))
                dve.wait_ge(sem["y_mm"], g + 1)
                if d == 0:
                    V.tensor_copy(oT[:, 4 + c, :], pair640(2)).then_inc(*E.sig("dve_step"))
                else:
                    V.tensor_tensor(oT[:, 4 + c, :], oT[:, 4 + c, :], pair640(2), ALU.add).then_inc(*E.sig("dve_step"))
                next_phase()

            def gn_phase(l):
                post_scale(l, 0)
                pre_scale(l, 1)
                post_scale(l, 1)
                for c in range(NPAIR):
                    y = oT[:, 4 + c, :]
                    dve.wait_ge(sem["gn_mean_mm"], l * NPAIR + c + 1)
                    V.tensor_tensor(y, y, pair640(c), ALU.subtract).then_inc(*E.sig("gn_cent"))
                dve.wait_ge(sem["gn_sum"], l + 1)
                V.tensor_scalar(rw_s[:, 3, :, :].rearrange("p i h -> p (i h)"), ps[:, 0, 0:NT * RH], 1.0 / HD, GN_EPS, ALU.mult, ALU.add).then_inc(*E.sig("gn_ms"))
                for c in range(NPAIR):
                    y = oT[:, 4 + c, :]
                    at = 12 * l + 3 * c
                    norm, bonus, gate_p = [pair640((3 * c + w + 1) % 4) for w in range(3)]
                    dve.wait_ge(sem["gn_mm"], at + 1)
                    V.scalar_tensor_tensor(y, y, PR(l, "ln_g", c), norm, ALU.mult, ALU.mult).then_inc(*E.sig("gn_used"))
                    dve.wait_ge(sem["gn_mm"], at + 2)
                    V.tensor_tensor(bon[:, c % 2, :], rkv[:, 8 + c, :], bonus, ALU.mult).then_inc(*E.sig("dve_step"))
                    dve.wait_ge(*E.own_last())
                    V.scalar_tensor_tensor(y, y, PR(l, "ln_b", c), bon[:, c % 2, :], ALU.add, ALU.add).then_inc(*E.sig("gn_used"))
                    dve.wait_ge(*E.own_last())
                    dve.wait_ge(sem["gn_mm"], at + 3)
                    V.tensor_tensor(y, y, gate_p, ALU.mult).then_inc(*E.sig("gn_used"))
                next_phase()

            def post_phase(k):
                w = k % 2
                for n in range(16):
                    g, kc = n // 8, n % 8
                    if n >= 4:
                        dve.wait_ge(sem["rowvec_mm"], 16 * k + n - 3)
                    V.tensor_scalar(diag(n), ident, gpost[:, w, kc, g:g + 1], None, ALU.mult).then_inc(*E.sig("rowvec_diag"))
                dve.wait_ge(sem["post_sq"], NT * (k + 1))
                V.tensor_scalar(pstat[:, 5:10], pstat[:, 0:5], 1.0 / D, NORM_EPS, ALU.mult, ALU.add).then_inc(*E.sig("stat_ms"))
                dve.wait_ge(sem["stat_pow"], 2 * k + 2)
                dve.wait_ge(sem["rowvec_mm"], 16 * (k + 1))
                for n in range(NT + 1):
                    if n < NT:
                        V.scalar_tensor_tensor(fo[:, n, :], fo[:, n, :], pstat[:, 15 + n:16 + n], pair(0 if n == 0 else 1), ALU.mult, ALU.mult).then_inc(*E.sig("post_tmp"))
                    if n >= 1:
                        dve.wait_ge(sem["post_tmp"], NT * k + n)
                        V.tensor_tensor(x[:, n - 1, :], x[:, n - 1, :], fo[:, n - 1, :], ALU.add).then_inc(*E.sig("post_x"))

            def wo_phase(l):
                for fc in range(WO_B):
                    x_lo(oT_lo[:, fc, :], oT[:, fc, :], oT_hi[:, fc, :])
                    n = WO_AT[l] + fc
                    split[0] += 1
                    dve.wait_ge(sem["w_hi"], split[0])
                    dve.wait_ge(ring_sem[n % RING], 16 * (n // RING + 1))
                    V.tensor_tensor(ring_lo[:, n % RING, :], ring[:, n % RING, :], w_wo[:, fc, :], ALU.subtract).then_inc(*E.sig("w_lo"))

            def dense_phase(l):
                first = FFN_AT[l]
                w_lo(w_ffn, first)
                for kc in range(KC):
                    x_lo(hT_lo[:, kc, :], hT[:, kc, :], hT_ffn_hi[:, kc, :])
                for n in (1, 2):
                    w_lo(w_ffn, first + n)
                for f in range(FT):
                    dve.wait_ge(sem["ff_th"], f + 1)
                    a, b = pair_r(2 * f % 4), pair_r((2 * f + 1) % 4)
                    V.scalar_tensor_tensor(ftmp[:, f % 2, :], ftmp[:, f % 2, :], 1.0, a, ALU.add, ALU.mult).then_inc(*E.sig("dve_step"))
                    dve.wait_ge(*E.own_last())
                    V.scalar_tensor_tensor(gT[:, f, :], ftmp[:, f % 2, :], 0.5, b, ALU.mult, ALU.mult).then_inc(*E.sig("ff_g"))
                    for n in (2 * f + 3, 2 * f + 4):
                        if n < 2 * FT:
                            w_lo(w_ffn, first + n)

            def route_phase():
                dve.wait_ge(sem["rt_mm"], 1)
                V.tensor_copy(lg, ps[:, 0, 0:40].rearrange("p (i e) -> p i e", i=NT)).then_inc(*E.sig("dve_step"))
                dve.wait_ge(*E.own_last())
                for i in range(NT):
                    V.max(m8[:, i, :], lg[:, i, :]).then_inc(*E.sig("dve_step"))
                dve.wait_ge(*E.own_last())
                V.tensor_scalar(rstat[:, 0:5], m8[:, :, 0], -1.0, None, ALU.mult).then_inc(*E.sig("dve_step"))
                for i in range(NT):
                    ins = V.tensor_scalar(msk[:, i, :], lg[:, i, :], m8[:, i, 1:2], None, ALU.is_ge)
                    ins.then_inc(*E.sig("rt_max" if i == NT - 1 else "dve_step"))
                dve.wait_ge(sem["rt_exp"], NT)
                dve.wait_ge(*E.own_last())
                V.tensor_tensor(gate, gate, msk, ALU.mult).then_inc(*E.sig("dve_step"))
                dve.wait_ge(*E.own_last())
                V.tensor_reduce(rstat[:, 5:10], gate, AX.X, ALU.add).then_inc(*E.sig("dve_step"))
                dve.wait_ge(*E.own_last())
                V.reciprocal(rstat[:, 10:15], rstat[:, 5:10]).then_inc(*E.sig("dve_step"))
                dve.wait_ge(*E.own_last())
                V.tensor_tensor(gate, gate, rstat[:, 10:15].unsqueeze(2).broadcast_to([P, NT, NE]), ALU.mult).then_inc(*E.sig("rt_gate"))
                dve.wait_ge(sem["rt_cum"], 1)
                V.scalar_tensor_tensor(rk, ps[:, 1, 0:40].rearrange("p (i e) -> p i e", i=NT), 1.0, msk, ALU.add, ALU.mult).then_inc(*E.sig("dve_step"))
                V.tensor_reduce(rstat[:, 16:17], ps[:, 1, 40:48], AX.X, ALU.max).then_inc(*E.sig("dve_step"))
                dve.wait_ge(*E.own_last())
                V.tensor_scalar(rk, rk, -1.0, None, ALU.add).then_inc(*E.sig("rt_rank"))
                V.tensor_copy(flag_i[0:1, 0:1], rstat[0:1, 16:17]).then_inc(*E.sig("rt_rank"))

            def moe_start():
                for i in range(NT):
                    x_lo(htok_lo[:, i, :], htok[:, i, :], htok_hi[:, i, :])

            def select(k, e, base):
                if k >= 1:
                    dve.wait_ge(sem["gat_mm"], KC * k)
                    dve.wait_ge(sem["selt_tr"], 2 * k)
                V.tensor_scalar(rstat[:, 20:25], rk[:, :, e], -float(base), None, ALU.add).then_inc(*E.sig("dve_step"))
                dve.wait_ge(*E.own_last())
                for i in range(NT):
                    V.tensor_scalar(sel[:, i, :], C("iota"), rstat[:, 20 + i:21 + i], None, ALU.is_equal).then_inc(*E.sig("dve_step"))
                for i in range(NT):
                    ins = V.tensor_scalar(sel_f[:, i, :], C("iota"), rstat[:, 20 + i:21 + i], None, ALU.is_equal)
                    ins.then_inc(*E.sig("sel_dve" if i == NT - 1 else "dve_step"))

            def moe_pass(k):
                e = k % NE
                first = FFN_AT[1] + k * EXP_B
                for kc in range(KC):
                    dve.wait_ge(sem["gat_ev"], KC * k + kc + 1)
                    V.tensor_tensor(hg_lo[:, kc, :], ps[:, 4 + kc % 2, 0:CAP], hg_hi[:, kc, :], ALU.subtract).then_inc(*E.sig("gat_lo"))
                for f in range(FE):
                    dve.wait_ge(sem["eh_th"], FE * k + f + 1)
                    b = ps[:, 4 + f % 2, :]
                    t, g = ftmp[:, f % 2, 0:CAP], ftmp[:, f % 2, CAP:2 * CAP]
                    V.scalar_tensor_tensor(t, t, 1.0, b[:, 0:CAP], ALU.add, ALU.mult).then_inc(*E.sig("dve_step"))
                    dve.wait_ge(*E.own_last())
                    V.scalar_tensor_tensor(g, t, 0.5, b[:, CAP:2 * CAP], ALU.mult, ALU.mult).then_inc(*E.sig("eh_g"))
                    for n in ahead(f)[0]:
                        w_lo(w_ffn, first + n)
                    dve.wait_ge(sem["eh_hi"], FE * k + f + 1)
                    dve.wait_ge(sem["eh_g"], FE * k + f + 1)
                    V.tensor_tensor(ge_lo[:, f % 2, :], g, ge_hi[:, f % 2, :], ALU.subtract).then_inc(*E.sig("eh_lo"))
                    for n in ahead(f)[1]:
                        w_lo(w_ffn, first + n)
                    if f == FE // 2 and k not in LAST_PASS:
                        select(k + 1, (k + 1) % NE, CAP * ((k + 1) // NE))
                if k not in LAST_PASS:
                    w_lo(w_ffn, first + EXP_B)
                    w_lo(w_ffn, first + EXP_B + 1)
                for n in range(4):
                    dve.wait_ge(sem["ey_ev"], 4 * k + n + 1)
                    half = slice((n % 2) * 512, (n % 2 + 1) * 512)
                    V.tensor_tensor(ye_lo[:, n // 2, half], ps[:, n, :], ye_hi[:, n // 2, half], ALU.subtract).then_inc(*E.sig("ey_lo"))
                for n in range(10):
                    i, h = n // 2, n % 2
                    dve.wait_ge(sem["comb_mm"], 10 * k + n + 1)
                    dst = fo[:, i, h * 512:(h + 1) * 512]
                    if k == 0:
                        V.tensor_scalar(dst, ps[:, 6 + n % 2, :], gate[:, i, e:e + 1], None, ALU.mult).then_inc(*E.sig("comb_ev"))
                    else:
                        V.scalar_tensor_tensor(dst, ps[:, 6 + n % 2, :], gate[:, i, e:e + 1], dst, ALU.mult, ALU.add).then_inc(*E.sig("comb_ev"))
                if k not in LAST_PASS:
                    w_lo(w_ffn, first + EXP_B + 2)

            for l in range(DEPTH):
                mod_phase(l)
                if l == 0:
                    next_phase()
                norm_phase(2 * l)
                next_phase()
                proj_phase(l)
                next_phase()
                att_phase(l)
                next_phase()
                kk_phase(l)
                next_phase()
                for c in range(NPAIR):
                    rwkv_dir(l, c, 0)
                    rwkv_dir(l, c, 1)
                gn_phase(l)
                wo_phase(l)
                next_phase()
                post_phase(2 * l)
                norm_phase(2 * l + 1)
                next_phase()
                if l == 0:
                    dense_phase(l)
                else:
                    route_phase()
                    dve.wait_ge(*E.own_last())
                    select(0, 0, 0)
                    for n in range(3):
                        w_lo(w_ffn, FFN_AT[1] + n)
                    next_phase()
                    moe_start()
                    for e in range(NE):
                        moe_pass(e)
                    next_phase()

                    def body():
                        for n in range(3):
                            w_lo(w_ffn, N_BLOCKS + n)
                        select(NE, 0, CAP)
                        for n in range(2 * NE):
                            moe_pass(NE + n)
                    with_flag(dve, body)
                next_phase()
                post_phase(2 * l + 1)

        @block.gpsimd
        def _(pool):
            E = Signals("pool", sem)
            phase = [0]

            def next_phase():
                phase[0] += 1
                pool.drain().then_inc(sem["pool_phase"], 1)
                pool.wait_ge(sem["pe_phase"], phase[0])
                pool.wait_ge(sem["act_phase"], phase[0])
                pool.wait_ge(sem["dve_phase"], phase[0])
                pool.wait_ge(sem["pool_phase"], phase[0])

            n_out = [0]

            def power(dst, src, rows, n, what):
                nc.gpsimd.tensor_tensor(dst, src, C("power", rows)[:, 0:n], ALU.pow).then_inc(sem[what], 1)

            def store(dst, src):
                pool.dma_start(dst, src).then_inc(sem["results_out"], 16)
                n_out[0] += 16

            def norm_phase(k):
                pool.wait_ge(sem["stat_ms"], 2 * k + 1)
                power(nstat[:, 15:20], nstat[:, 5:10], P, 5, "stat_pow")

            def post_phase(k):
                pool.wait_ge(sem["stat_ms"], 2 * k + 2)
                power(pstat[:, 15:20], pstat[:, 5:10], P, 5, "stat_pow")

            pool.wait_ge(sem["consts_in"], 16)
            for l in range(DEPTH):
                if l == 0:
                    next_phase()
                norm_phase(2 * l)
                if n_out[0]:
                    pool.wait_ge(sem["results_out"], n_out[0])
                pool.dma_start(w2[:, :, :], low2[l]).then_inc(sem["misc_in"], 16)
                pool.dma_start(ck[:, :, :], cache_k[l].rearrange("(i p) c -> p i c", p=P)).then_inc(sem["misc_in"], 16)
                pool.dma_start(cv[:, :, :], cache_v[l].rearrange("(i p) c -> p i c", p=P)).then_inc(sem["misc_in"], 16)
                for d in range(2):
                    pool.dma_start(st_in[:, d, :, :], state[l, d].rearrange("h v k -> v h k")).then_inc(sem["misc_in"], 16)
                next_phase()
                next_phase()
                pool.wait_ge(sem["kc_ev"], l + 1)
                store(new_k[l], kctok[:, :])
                store(new_v[l], vtok[:, 0, :])
                pool.wait_ge(sem["results_out"], n_out[0])
                next_phase()
                pool.wait_ge(sem["kk_ss"], l + 1)
                power(rw_s[:, 0, :, :].rearrange("p i h -> p (i h)"), rw_s[:, 3, :, :].rearrange("p i h -> p (i h)"), P, NT * RH, "kk_pow")
                next_phase()
                for _ in range(2 * NPAIR):
                    next_phase()
                pool.wait_ge(sem["gn_ms"], l + 1)
                power(rw_s[:, 2, :, :].rearrange("p i h -> p (i h)"), rw_s[:, 3, :, :].rearrange("p i h -> p (i h)"), P, NT * RH, "gn_pow")
                next_phase()
                for d in range(2):
                    store(new_state[l, d].rearrange("(c h) v k -> (h v) c k", h=2), st_out[:, d, :, :])
                next_phase()
                post_phase(2 * l)
                norm_phase(2 * l + 1)
                next_phase()
                if l == 1:
                    next_phase()
                    next_phase()
                next_phase()
                post_phase(2 * l + 1)
            for i in range(NT):
                pool.wait_ge(sem["post_x"], NT * (2 * DEPTH - 1) + i + 1)
                store(y_all[i * P:(i + 1) * P, :], x[:, i, :])
            pool.wait_ge(sem["results_out"], n_out[0])


def kernel(**a):
    import concourse.bacc as bacc
    from concourse.bass_utils import run_bass_kernel_spmd

    a = {k: np.asarray(v) for k, v in a.items()}

    def cols(w):
        k, n = w.shape
        return w.reshape(k // P, P, n // P, P).transpose(2, 1, 0, 3).reshape(n // P, P, -1)

    def chan(v):
        return v.reshape(-1, P).T

    def modulation(l):
        return a["w_mod"][l].reshape(4, 2, P, MOD_G, 512).transpose(3, 0, 2, 1, 4).reshape(MOD_B, P, D)

    heads = np.arange(NH).reshape(2, 4).T.reshape(-1)
    qcols = (heads[:, None] * HD + np.arange(HD)[None, :]).reshape(-1)
    w_mod = np.concatenate([modulation(0), modulation(1)], 0)
    blocks, small = [], []
    for l in range(DEPTH):
        w_in = a["w_in"][l]
        if l == 0:
            blocks.append(w_mod[:4 * MOD_FIRST])
        blocks.append(cols(w_in[:, qcols]))
        blocks.append(cols(w_in[:, 512:]))
        for w in (a["rw_w1"][l], a["rw_a1"][l]):
            blocks.append(cols(np.concatenate([w[0], w[1]], 1)))
        blocks.append(cols(a["rw_g1"][l]))
        blocks.append(w_mod[4 * MOD_FIRST:4 * MOD_MID] if l == 0 else w_mod[4 * MOD_MID:])
        wo = a["w_o"][l]
        blocks.append(np.concatenate([wo[qcols], wo[512:]], 0).reshape(8, P, D))
        if l == 0:
            w1, w3 = cols(a["ffn_w1"][0]), cols(a["ffn_w3"][0])
            blocks.append(np.stack([w1, w3], 1).reshape(2 * FT, P, D))
            w2 = a["ffn_w2"][0].reshape(FT // 2, 2, P, 2, 512)
            blocks.append(w2.transpose(3, 0, 2, 1, 4).reshape(FT, P, D))
        else:
            for e in range(NE):
                w1, w3 = cols(a["moe_w1"][0, e]), cols(a["moe_w3"][0, e])
                w2 = a["moe_w2"][0, e].reshape(FE, P, D)
                seq = []
                for f in range(FE + 1):
                    if f < FE:
                        seq += [w1[f], w3[f]]
                    if f >= 1:
                        seq.append(w2[f - 1])
                blocks.append(np.stack(seq))
        small += [chan(v) for v in (a["b_mod"][l], a["g_pre_mix"][l], a["g_post_mix"][l], a["g_pre_ffn"][l],
                                    a["g_post_ffn"][l], a["mu_shift"][l], a["rw_w0"][l], a["rw_a0"][l], a["rw_k_k"][l],
                                    a["rw_k_a"][l], a["rw_r_k"][l], a["rw_ln_g"][l], a["rw_ln_b"][l])]
    low2 = np.stack([a["rw_w2"].reshape(DEPTH, P, 512), a["rw_a2"].reshape(DEPTH, P, 512), a["rw_g2"]], 2)
    ins = {
        "blocks": np.concatenate(blocks, 0),
        "x_all": np.concatenate([a["x_prompt"][0], a["x_sample"][0]], 0),
        "small": np.concatenate(small, 1),
        "cond": np.stack([chan(a["c_ctx"]), chan(a["c"][0])], 2),
        "sinkrows": np.broadcast_to(a["attn_sink"].reshape(1, -1), (P, DEPTH * NH)),
        "router": a["moe_router"][0].reshape(KC, P, NE).transpose(1, 0, 2),
        "low2": low2,
        "cache_k": a["cache_k"][0].reshape(DEPTH, PAST, KVH * HD),
        "cache_v": a["cache_v"][0].reshape(DEPTH, PAST, KVH * HD),
        "state": a["state_rwkv"][0],
        "consts": constants(),
    }
    nc = bacc.Bacc("TRN2", target_bir_lowering=False, num_devices=1)
    arrays, args = {}, []
    for name, v in ins.items():
        v = np.ascontiguousarray(v)
        arrays["in_" + name] = v
        args.append(nc.dram_tensor("in_" + name, v.shape, mybir.dt.from_np(v.dtype), kind="ExternalInput").ap())
    for name, shape in (("y_all", (T, D)), ("new_k", (DEPTH, CTX, KVH * HD)), ("new_v", (DEPTH, CTX, KVH * HD)),
                        ("new_state", (DEPTH, 2, RH, HD, HD))):
        args.append(nc.dram_tensor("out_" + name, shape, F32, kind="ExternalOutput").ap())
    build(nc, *args)
    r = run_bass_kernel_spmd(nc, [arrays], core_ids=[0]).results[0]
    y = r["out_y_all"]
    return (y[:CTX].reshape(1, CTX, D), y[CTX:].reshape(1, LAT, D),
            r["out_new_k"].reshape(1, DEPTH, CTX, KVH, HD), r["out_new_v"].reshape(1, DEPTH, CTX, KVH, HD),
            r["out_new_state"][None])
```
